# Optimizing a Trainium2 kernel written in Bass

```python
import math
import jax
import jax.numpy as jnp
from jax import lax
import numpy as np

D_MODEL = 1024
BATCH = 1
SEQ = 128
DEPTH = 2
DEC_BATCH = 1
DEC_SEQ = 1024
PAST_LEN = 128

GRID_W = 64
N_EVEN = (DEPTH + 1) // 2
N_ODD = DEPTH // 2
ATT_WIDTH = D_MODEL // 2
POOL_WIDTH = D_MODEL - ATT_WIDTH
ATT_HEADS = 4
ATT_DH = ATT_WIDTH // (2 * ATT_HEADS)
ATT_DV = 2 * ATT_DH
Q_BLOCK = 128
ROPE_BASE = 10000.0
POOL_WINDOWS = (2, 4, 8, 16)
POOL_GROUP = POOL_WIDTH // len(POOL_WINDOWS)
GLA_HEADS = 4
GLA_DK_TOTAL = D_MODEL // 2
GLA_DV_TOTAL = D_MODEL
GLA_DK = GLA_DK_TOTAL // GLA_HEADS
GLA_DV = GLA_DV_TOTAL // GLA_HEADS
GATE_RANK = 16
GATE_TEMP = 16.0
CHUNK = 64
ODD_IN = 2 * GLA_DK_TOTAL + 2 * GLA_DV_TOTAL + 2 * GATE_RANK
FFN_HIDDEN = ((8 * D_MODEL + 3 * 256 - 1) // (3 * 256)) * 256
EPS = 1e-6

kernel_name = "hybrid_diffattn_pool_gla_prefix_dit_step"

F32 = jnp.float32

def rmsnorm(x, g):
    xf = x.astype(F32)
    y = xf * lax.rsqrt(jnp.mean(xf * xf, axis=-1, keepdims=True) + EPS)
    return (y * g.astype(F32)).astype(x.dtype)

def adaln(cvec, w, b):
    mod = jax.nn.silu(cvec) @ w + b
    return jnp.split(mod, 6, axis=-1)

def modulate(h, shift, scale):
    return h * (1 + scale) + shift

def axial_rope(x, rows, cols):
    half = ATT_DH // 2
    inv = 1.0 / (ROPE_BASE ** (jnp.arange(0, half, 2, dtype=F32) / half))

    def rot(xh, pos):
        ang = pos[:, None] * inv[None, :]
        ang = jnp.concatenate([ang, ang], axis=-1)
        cos = jnp.cos(ang)[None, :, None, None, :].astype(x.dtype)
        sin = jnp.sin(ang)[None, :, None, None, :].astype(x.dtype)
        x1, x2 = jnp.split(xh, 2, axis=-1)
        return xh * cos + jnp.concatenate([-x2, x1], axis=-1) * sin

    return jnp.concatenate([rot(x[..., :half], rows), rot(x[..., half:], cols)], axis=-1)

def diff_lambda(lam_p, layer):
    lp = lam_p.astype(F32)
    lam_init = 0.8 - 0.6 * math.exp(-0.3 * layer)
    lam = jnp.exp(jnp.sum(lp[0] * lp[1])) - jnp.exp(jnp.sum(lp[2] * lp[3])) + lam_init
    return lam, lam_init

def diff_attention(q, k, v, lam):
    B, Tq = q.shape[0], q.shape[1]
    nb = Tq // Q_BLOCK
    qb = q.reshape(B, nb, Q_BLOCK, ATT_HEADS, 2, ATT_DH).transpose(1, 0, 2, 3, 4, 5)
    scale = ATT_DH ** -0.5

    def one_block(qblk):
        s = jnp.einsum('bqhad,bkhad->bhaqk', qblk, k).astype(F32) * scale
        p = jax.nn.softmax(s, axis=-1)
        a = p[:, :, 0] - lam * p[:, :, 1]
        return jnp.einsum('bhqk,bkhv->bqhv', a.astype(v.dtype), v)

    o = lax.map(one_block, qb)
    return o.transpose(1, 0, 2, 3, 4).reshape(B, Tq, ATT_HEADS, ATT_DV)

def multiscale_pool(u, w_pool, pool_scale):
    B, T, C = u.shape
    cs = jnp.concatenate([jnp.zeros((B, 1, C), F32), jnp.cumsum(u.astype(F32), axis=1)], axis=1)
    t = jnp.arange(T)
    outs = []
    for g, w in enumerate(POOL_WINDOWS):
        lo = jnp.clip(t - w // 2, 0, T)
        hi = jnp.clip(t - w // 2 + w, 0, T)
        csg = cs[..., g * POOL_GROUP:(g + 1) * POOL_GROUP]
        cnt = (hi - lo).astype(F32)[None, :, None]
        ug = u[..., g * POOL_GROUP:(g + 1) * POOL_GROUP].astype(F32)
        y = (csg[:, hi] - csg[:, lo]) / cnt - ug
        outs.append(jnp.einsum('btc,cd->btd', y.astype(u.dtype), w_pool[g]))
    return jnp.concatenate(outs, axis=-1) * pool_scale

def even_project(h, w_in):
    B, T, _ = h.shape
    q, k, v, u = jnp.split(h @ w_in, [ATT_WIDTH, 2 * ATT_WIDTH, 3 * ATT_WIDTH], axis=-1)
    q = q.reshape(B, T, ATT_HEADS, 2, ATT_DH)
    k = k.reshape(B, T, ATT_HEADS, 2, ATT_DH)
    v = v.reshape(B, T, ATT_HEADS, ATT_DV)
    return q, k, v, u

def even_output(o, u, lam_init, subln_g, w_pool, pool_scale, w_out):
    B, T = o.shape[0], o.shape[1]
    o = rmsnorm(o, subln_g.reshape(ATT_HEADS, ATT_DV)) * (1.0 - lam_init)
    p = multiscale_pool(u, w_pool, pool_scale)
    return jnp.concatenate([o.reshape(B, T, ATT_WIDTH).astype(p.dtype), p], axis=-1) @ w_out

def gla_chunked(q, k, v, g, s0):
    B, T = q.shape[0], q.shape[1]
    N = T // CHUNK

    def r(a):
        return a.reshape(B, N, CHUNK, GLA_HEADS, a.shape[-1])

    q, k, v, g = r(q), r(k), r(v), r(g)
    b = jnp.cumsum(g, axis=2)
    b_last = b[:, :, -1]
    q_t = q * jnp.exp(b)
    k_t = k * jnp.exp(-b)
    k_end = k * jnp.exp(b_last[:, :, None] - b)
    mask = jnp.tril(jnp.ones((CHUNK, CHUNK), dtype=bool))
    A = jnp.where(mask, jnp.einsum('bnihd,bnjhd->bnhij', q_t, k_t), 0.0)
    o_intra = jnp.einsum('bnhij,bnjhv->bnihv', A, v)
    kv_chunk = jnp.einsum('bnjhd,bnjhv->bnhdv', k_end, v)

    def step(S, xs):
        qc, decay, kv = xs
        o = jnp.einsum('bihd,bhdv->bihv', qc, S)
        return S * decay[..., None] + kv, o

    S, o_inter = lax.scan(step, s0, (q_t.transpose(1, 0, 2, 3, 4),
                                     jnp.exp(b_last).transpose(1, 0, 2, 3),
                                     kv_chunk.transpose(1, 0, 2, 3, 4)))
    o = o_intra + o_inter.transpose(1, 0, 2, 3, 4)
    return o.reshape(B, T, GLA_HEADS, GLA_DV), S

def gla_project(h, w_in, w_gate_up, b_gate):
    B, T, _ = h.shape
    q, k, v, r, gd = jnp.split(h @ w_in, [GLA_DK_TOTAL, 2 * GLA_DK_TOTAL,
                                         2 * GLA_DK_TOTAL + GLA_DV_TOTAL,
                                         2 * GLA_DK_TOTAL + 2 * GLA_DV_TOTAL], axis=-1)
    q = q.reshape(B, T, GLA_HEADS, GLA_DK).astype(F32) * (GLA_DK ** -0.5)
    k = k.reshape(B, T, GLA_HEADS, GLA_DK).astype(F32)
    v = v.reshape(B, T, GLA_HEADS, GLA_DV).astype(F32)
    gates = []
    for d in range(2):
        logit = gd[..., d * GATE_RANK:(d + 1) * GATE_RANK] @ w_gate_up[d] + b_gate[d]
        gates.append((jax.nn.log_sigmoid(logit.astype(F32)) / GATE_TEMP).reshape(B, T, GLA_HEADS, GLA_DK))
    return q, k, v, r, gates

def gla_bidir(q, k, v, gates, s_f0, s_b0):
    o_f, s_f = gla_chunked(q, k, v, gates[0], s_f0)
    fl = lambda a: jnp.flip(a, axis=1)
    o_b, s_b = gla_chunked(fl(q), fl(k), fl(v), fl(gates[1]), s_b0)
    return o_f + fl(o_b), jnp.stack([s_f, s_b], axis=1)

def gla_output(o, r, norm_g, w_out):
    B, T = o.shape[0], o.shape[1]
    o = rmsnorm(o, norm_g.reshape(GLA_HEADS, GLA_DV)).reshape(B, T, GLA_DV_TOTAL).astype(r.dtype)
    return (o * jax.nn.silu(r)) @ w_out

def swiglu(h, w_in, w_out):
    a, b = jnp.split(h @ w_in, 2, axis=-1)
    return (jax.nn.silu(a) * b) @ w_out

def setup_inputs(seed: int = 0) -> dict:
    key = jax.random.key(seed)
    ks = jax.random.split(key, 32)

    def nrm(k, shape, scale):
        return jax.random.normal(k, shape, F32) * scale

    D = D_MODEL
    return {
        "x_prompt": nrm(ks[0], (BATCH, SEQ, D), 1.0),
        "x_sample": nrm(ks[1], (DEC_BATCH, DEC_SEQ, D), 1.0),
        "c": nrm(ks[2], (DEC_BATCH, D), 1.0),
        "cache_attn_k": nrm(ks[3], (DEC_BATCH, N_EVEN, PAST_LEN, ATT_HEADS, 2, ATT_DH), 1.0),
        "cache_attn_v": nrm(ks[4], (DEC_BATCH, N_EVEN, PAST_LEN, ATT_HEADS, ATT_DV), 1.0),
        "state_gla": nrm(ks[5], (DEC_BATCH, N_ODD, 2, GLA_HEADS, GLA_DK, GLA_DV), 0.5),
        "c_ctx": nrm(ks[6], (D,), 1.0),
        "norm1_g": 1.0 + nrm(ks[7], (DEPTH, D), 0.05),
        "norm2_g": 1.0 + nrm(ks[8], (DEPTH, D), 0.05),
        "w_mod": nrm(ks[9], (DEPTH, D, 6 * D), 0.5 * D ** -0.5),
        "b_mod": nrm(ks[10], (DEPTH, 6 * D), 0.02),
        "w_in_even": nrm(ks[11], (N_EVEN, D, 3 * ATT_WIDTH + POOL_WIDTH), D ** -0.5),
        "lam_params": nrm(ks[12], (N_EVEN, 4, ATT_DH), 0.1),
        "subln_g": 1.0 + nrm(ks[13], (N_EVEN, ATT_WIDTH), 0.05),
        "w_pool": nrm(ks[14], (N_EVEN, len(POOL_WINDOWS), POOL_GROUP, POOL_GROUP), POOL_GROUP ** -0.5),
        "pool_scale": 1.0 + nrm(ks[15], (N_EVEN, POOL_WIDTH), 0.1),
        "w_out_even": nrm(ks[16], (N_EVEN, D, D), D ** -0.5),
        "w_in_odd": nrm(ks[17], (N_ODD, D, ODD_IN), D ** -0.5),
        "w_gate_up": nrm(ks[18], (N_ODD, 2, GATE_RANK, GLA_DK_TOTAL), GATE_RANK ** -0.5),
        "b_gate": nrm(ks[19], (N_ODD, 2, GLA_DK_TOTAL), 0.1),
        "gla_norm_g": 1.0 + nrm(ks[20], (N_ODD, GLA_DV_TOTAL), 0.05),
        "w_out_odd": nrm(ks[21], (N_ODD, GLA_DV_TOTAL, D), GLA_DV_TOTAL ** -0.5),
        "w_ffn_in": nrm(ks[22], (DEPTH, D, 2 * FFN_HIDDEN), D ** -0.5),
        "w_ffn_out": nrm(ks[23], (DEPTH, FFN_HIDDEN, D), FFN_HIDDEN ** -0.5),
        "final_g": 1.0 + nrm(ks[24], (D,), 0.05),
    }

def reference(x_prompt, x_sample, c, cache_attn_k, cache_attn_v, state_gla, c_ctx,
              norm1_g, norm2_g, w_mod, b_mod, w_in_even, lam_params, subln_g, w_pool,
              pool_scale, w_out_even, w_in_odd, w_gate_up, b_gate, gla_norm_g, w_out_odd,
              w_ffn_in, w_ffn_out, final_g):
    xp, xs = x_prompt, x_sample
    Bp = xp.shape[0]
    n_lat = xs.shape[1]
    n_rows = n_lat // GRID_W
    rows = jnp.repeat(jnp.arange(n_rows, dtype=F32), GRID_W)
    cols = jnp.tile(jnp.arange(GRID_W, dtype=F32), n_rows)
    ks_new, vs_new, ss_new = [], [], []
    for l in range(DEPTH):
        m_ctx = adaln(c_ctx, w_mod[l], b_mod[l])
        m_lat = [m[:, None, :] for m in adaln(c, w_mod[l], b_mod[l])]
        hp = modulate(rmsnorm(xp, norm1_g[l]), m_ctx[0], m_ctx[1])
        hs = modulate(rmsnorm(xs, norm1_g[l]), m_lat[0], m_lat[1])
        i = l // 2
        if l % 2 == 0:
            lam, lam_init = diff_lambda(lam_params[i], l)
            q, k, v, u = even_project(hp, w_in_even[i])
            o = diff_attention(q, k, v, lam)
            out_p = even_output(o, u, lam_init, subln_g[i], w_pool[i], pool_scale[i], w_out_even[i])
            ks_new.append(k)
            vs_new.append(v)
            q, k, v, u = even_project(hs, w_in_even[i])
            q = axial_rope(q, rows, cols)
            k = axial_rope(k, rows, cols)
            k_all = jnp.concatenate([k, cache_attn_k[:, i].astype(k.dtype)], axis=1)
            v_all = jnp.concatenate([v, cache_attn_v[:, i].astype(v.dtype)], axis=1)
            o = diff_attention(q, k_all, v_all, lam)
            out_s = even_output(o, u, lam_init, subln_g[i], w_pool[i], pool_scale[i], w_out_even[i])
        else:
            q, k, v, r, gates = gla_project(hp, w_in_odd[i], w_gate_up[i], b_gate[i])
            z0 = jnp.zeros((Bp, GLA_HEADS, GLA_DK, GLA_DV), F32)
            o, s_ctx = gla_bidir(q, k, v, gates, z0, z0)
            out_p = gla_output(o, r, gla_norm_g[i], w_out_odd[i])
            ss_new.append(s_ctx)
            q, k, v, r, gates = gla_project(hs, w_in_odd[i], w_gate_up[i], b_gate[i])
            st = state_gla[:, i].astype(F32)
            o, _ = gla_bidir(q, k, v, gates, st[:, 0], st[:, 1])
            out_s = gla_output(o, r, gla_norm_g[i], w_out_odd[i])
        xp = xp + m_ctx[2] * out_p
        xs = xs + m_lat[2] * out_s
        hp = modulate(rmsnorm(xp, norm2_g[l]), m_ctx[3], m_ctx[4])
        hs = modulate(rmsnorm(xs, norm2_g[l]), m_lat[3], m_lat[4])
        xp = xp + m_ctx[5] * swiglu(hp, w_ffn_in[l], w_ffn_out[l])
        xs = xs + m_lat[5] * swiglu(hs, w_ffn_in[l], w_ffn_out[l])
    y_prompt = rmsnorm(xp, final_g)
    y_sample = rmsnorm(xs, final_g)
    new_attn_k = jnp.stack(ks_new, axis=1)
    new_attn_v = jnp.stack(vs_new, axis=1)
    new_gla_state = jnp.stack(ss_new, axis=1)
    return (y_prompt, y_sample, new_attn_k, new_attn_v, new_gla_state)


_drawn_inputs = setup_inputs


def setup_inputs(seed=0):
    import zlib

    import numpy as np

    out = dict(_drawn_inputs(seed))
    spreads = {}
    factors = {'cache_attn_k': 5.096,
     'cache_attn_v': 4.338,
     'state_gla': 8.0,
     'lam_params': 3.79,
     'subln_g': 3.496,
     'pool_scale': 2.696,
     'gla_norm_g': 5.919,
     'norm2_g': 2.883}
    for name, (base, spread) in spreads.items():
        noise = np.random.default_rng([zlib.crc32(name.encode()), seed]).standard_normal(out[name].shape)
        drawn = base * np.exp(spread * noise) if base else spread * noise
        out[name] = jnp.asarray(drawn.astype(out[name].dtype))
    for name, factor in factors.items():
        out[name] = (out[name] * factor).astype(out[name].dtype)
    return out
```

```python
from contextlib import ExitStack

import concourse.bass as bass
from concourse import mybir

F32 = mybir.dt.float32
F32R = mybir.dt.float32r
ALU = mybir.AluOpType
ACT = mybir.ActivationFunctionType
AX_X = mybir.AxisListType.X

P = 128
D = 1024
KT = D // P
CTX = 128
LAT = 1024
T = CTX + LAT
NC = 3
CW = T // NC
EPS = 1e-6
HEADS = 4
HIDDEN = 2816
FFN_PAIRS = HIDDEN // (2 * P)
LAM_INIT = 0.2
DH = 64
WINDOWS = (2, 4, 8, 16)
GCH = 64
NCHUNK = T // GCH
NT = T // P
GATE_TEMP = 16.0
DK_SCALE = float(P) ** -0.5
SHIFT1, SCALE1, GATE1, SHIFT2, SCALE2, GATE2 = range(6)
PAD = 8
PADW = PAD + CTX + 2 * PAD + LAT + PAD
EVEN_TILES = 16
ODD_TILES = 24


def wait(eng, sem, i, per, n):
    if isinstance(i, int):
        if i * per + n > 0:
            eng.wait_ge(sem, i * per + n)
    else:
        eng.wait_ge(sem, i * per + n)


def peeled(eng, body, n):
    body(0)
    if n > 1:
        with eng.Fori(1, n) as i:
            body(i)


def build(nc, inp, out):
    base = (nc.sbuf_base + 63) // 64 * 64

    def at(name, shape, dtype, offset):
        return nc.alloc_sbuf_tensor_at(name, shape, dtype, offset=base + offset)

    XB = 4 * KT * T
    C0 = 6656
    HH0, HL0, X0, W0 = C0, C0 + XB, C0 + 2 * XB, C0 + 3 * XB
    END = nc.sbuf_usable_end - base
    GD0 = END // 32 * 32 - 4 * T

    ctx = ExitStack()

    pos = [0]

    def const(name, shape, dtype=F32):
        t = at(name, shape, dtype, pos[0])
        n = 4
        for s in shape[1:]:
            n *= s
        pos[0] += (n + 31) // 32 * 32
        assert pos[0] <= C0, pos[0]
        return t

    ident = const("ident", [P, P])
    ones = const("ones", [P, P])
    rot_t = const("rot_t", [P, P])
    mask_gla = const("mask_gla", [P, 2, P])
    cond = const("cond", [P, KT, 2])
    silu_c = const("silu_c", [P, KT, 2])
    bmod = const("bmod", [P, 2, 6 * KT])
    mod = const("mod", [P, 2, 6 * KT, 2])
    gnorm = const("gnorm", [P, 5, KT])
    amod = const("amod", [P, 4, KT, 2])
    eps = const("eps", [P, 1])
    lamp = const("lamp", [P, 4, DH])
    lamw = const("lamw", [P, 8])
    neglam = const("neglam", [P, 1])
    subg = const("subg", [P, HEADS])
    pscale = const("pscale", [P, HEADS])
    edge = const("edge", [P, len(WINDOWS), 2, PAD])
    bgate = const("bgate", [P, 2, HEADS])
    nbgate = const("nbgate", [P, 2, HEADS])
    vnorm = const("vnorm", [P, 2 * HEADS])

    hh = at("hh", [P, KT, T], F32R, HH0)
    hl = at("hl", [P, KT, T], F32R, HL0)
    x = at("x", [P, KT, T], F32, X0)

    xs_dram = nc.dram_tensor("x_spill", [P, KT, T], F32, kind="Internal").ap()
    gla_dram = nc.dram_tensor("gla_spill", [ODD_TILES, P, T], F32, kind="Internal").ap()

    nstage = [0]
    semaphores = []

    def stage():
        s = ExitStack()
        nstage[0] += 1
        k = nstage[0]
        psum = s.enter_context(nc.psum_tensor(f"ps{k}", [P, 8, 512], F32))

        def sem(name):
            semaphores.append(nc.alloc_semaphore(f"s{k}_{name}"))
            return semaphores[-1]
        return s, sem, psum, k

    def recycle():
        nc.clear_and_free_semaphores(semaphores)
        semaphores.clear()
        nc.all_engine_barrier()

    cs = [slice(c * CW, (c + 1) * CW) for c in range(NC)]
    pieces = [[(slice(0, CTX), 0), (slice(CTX, CW), 1)]] + [[(cs[c], 1)] for c in range(1, NC)]

    def modulation():
        s, sem, ps, k = stage()
        SL = 4
        NM = 2 * 6 * KT
        with s:
            wm = at("wm", [P, SL, KT, P], F32, W0)
            consts_in = sem("consts_in")
            w_in = [sem(f"w_in{j}") for j in range(SL)]
            w_used = sem("w_used")
            silu_done = sem("silu_done")
            mod_done = sem("mod_done")
            dve_step = sem("dve_step")
            lam_exp = sem("lam_exp")
            small = [(ident, "c_ident"), (rot_t, "c_rot"), (mask_gla, "c_mask"), (cond, "cond"), (bmod, "b_mod"),
                     (gnorm, "gnorm"), (lamp, "lam"), (subg, "subln"), (pscale, "pscale"), (edge, "c_edge"),
                     (bgate, "bgate"), (vnorm, "gla_norm")]
            block = s.enter_context(nc.Block())

            @block.scalar
            def _(act):
                for t, name in small:
                    act.dma_start(t[:], inp[name]).then_inc(consts_in, 16)
                act.wait_ge(consts_in, 16 * len(small))
                act.activation(silu_c[:], cond[:], ACT.Silu).then_inc(silu_done, 1)
                act.wait_ge(dve_step, 2)
                act.activation(lamw[:, 2:4], lamw[:, 0:2], ACT.Exp).then_inc(lam_exp, 1)

            @block.sync
            def _(sp):
                def body(i):
                    for j in range(SL):
                        wait(sp, w_used, i, SL, j + 1 - SL)
                        m = i * SL + j
                        src = inp["w_mod"][m] if isinstance(m, int) else inp["w_mod"][bass.ds(m, 1)].rearrange("o p n -> p (o n)")
                        sp.dma_start(wm[:, j].rearrange("p k n -> p (k n)"), src).then_inc(w_in[j], 16)
                peeled(sp, body, NM // SL)

            @block.tensor
            def _(pe):
                pe.wait_ge(silu_done, 1)

                def body(i):
                    for j in range(SL):
                        wait(pe, w_in[j], i, 16, 16)
                        for kk in range(KT):
                            mm = pe.matmul(ps[:, 0, bass.ds((i * SL + j) * 2, 2)], wm[:, j, kk, :], silu_c[:, kk, :],
                                           start=(kk == 0), stop=(kk == KT - 1))
                        mm.then_inc(w_used, 1)
                peeled(pe, body, NM // SL)

            @block.gpsimd
            def _(pool):
                pool.memset(ones[:], 1.0)
                pool.memset(eps[:], EPS)

            @block.vector
            def _(dve):
                dve.wait_ge(consts_in, 16 * len(small))
                dve.tensor_tensor(lamp[:, 0:3:2], lamp[:, 0:3:2], lamp[:, 1:4:2], ALU.mult).then_inc(dve_step, 1)
                dve.wait_ge(dve_step, 1)
                dve.tensor_reduce(lamw[:, 0:2], lamp[:, 0:3:2], AX_X, ALU.add).then_inc(dve_step, 1)
                dve.wait_ge(lam_exp, 1)
                dve.tensor_tensor(lamw[:, 4:5], lamw[:, 3:4], lamw[:, 2:3], ALU.subtract).then_inc(dve_step, 1)
                dve.wait_ge(dve_step, 3)
                dve.tensor_scalar(neglam[:], lamw[:, 4:5], -LAM_INIT, None, ALU.add)
                dve.tensor_scalar(subg[:], subg[:], 1.0 - LAM_INIT, None, ALU.mult)
                dve.wait_ge(w_used, NM)
                dve.tensor_tensor(mod[:].rearrange("p l m v -> p (l m) v"),
                                  ps[:, 0, 0:2 * NM].rearrange("p (m v) -> p m v", v=2),
                                  bmod[:].rearrange("p l m -> p (l m)").unsqueeze(2).broadcast_to([P, NM, 2]),
                                  ALU.add).then_inc(mod_done, 1)
                dve.wait_ge(mod_done, 1)
                for l in range(2):
                    for w, kind in enumerate((SCALE1, SCALE2)):
                        dve.scalar_tensor_tensor(
                            out=amod[:, 2 * l + w], in0=mod[:, l, kind * KT:(kind + 1) * KT, :], scalar=1.0,
                            in1=gnorm[:, 2 * l + w].unsqueeze(2).broadcast_to([P, KT, 2]),
                            op0=ALU.add, op1=ALU.mult)

    def norm(n, layer=None, shift=None, load=None, spill=False, final=None):
        s, sem, ps, k = stage()
        with s:
            sq = [at(f"sq{k}_{j}", [P, KT, CW], F32, W0 + j * 4 * KT * CW) for j in range(2)]
            xn = [at(f"xn{k}_{j}", [P, KT, CW], F32, W0 + (2 + j) * 4 * KT * CW) for j in range(2)]
            ssq = at(f"ssq{k}", [P, NC, CW], F32, W0 + 16 * KT * CW)
            std = at(f"std{k}", [P, NC, CW], F32, W0 + 16 * KT * CW + 4 * T)
            rstd = at(f"rstd{k}", [P, NC, CW], F32, W0 + 16 * KT * CW + 8 * T)
            x_in = [sem(f"x_in{c}") for c in range(NC)]
            y_out = [sem(f"y_out{j}") for j in range(2)]
            squared, summed, averaged, rooted = sem("squared"), sem("summed"), sem("averaged"), sem("rooted")
            inverted, scaled, modulated, high, low, stored = (sem("inverted"), sem("scaled"), sem("modulated"),
                                                              sem("high"), sem("low"), sem("stored"))
            block = s.enter_context(nc.Block())

            @block.sync
            def _(sp):
                sent = 0
                if load is not None:
                    for c in range(NC):
                        sp.dma_start(x[:, :, cs[c]], load[:, :, cs[c]]).then_inc(x_in[c], 16)
                if spill:
                    if load is not None:
                        for c in range(NC):
                            sp.wait_ge(x_in[c], 16)
                    sp.dma_start(xs_dram, x[:]).then_inc(stored, 16)
                    sent += 16
                if final is not None:
                    for c in range(NC):
                        sp.wait_ge(modulated, c + 1)
                        sp.dma_start(final[:, :, cs[c]], xn[c % 2][:]).then_inc(y_out[c % 2], 16)
                    sp.wait_ge(y_out[0], 32)
                    sp.wait_ge(y_out[1], 16)
                if sent:
                    sp.wait_ge(stored, sent)

            @block.scalar
            def _(act):
                def square(c):
                    if load is not None:
                        act.wait_ge(x_in[c], 16)
                    if c >= 2:
                        act.wait_ge(summed, c - 1)
                    act.activation(sq[c % 2][:], x[:, :, cs[c]], ACT.Square).then_inc(squared, 1)

                def root(c):
                    act.wait_ge(averaged, c + 1)
                    act.activation(std[:, c], ps[:, c, 0:CW], ACT.Sqrt, bias=eps[:], scale=1.0 / D).then_inc(rooted, 1)

                square(0)
                square(1)
                root(0)
                for c in range(NC):
                    if c + 1 < NC:
                        root(c + 1)
                    if c == 0:
                        square(2)
                    act.wait_ge(scaled, c + 1)
                    for ft in range(KT):
                        for cols, v in pieces[c]:
                            loc = slice(cols.start - c * CW, cols.stop - c * CW)
                            xi = xn[c % 2][:, ft, loc]
                            if final is not None:
                                last = act.activation(xi, xi, ACT.Identity, scale=gnorm[:, n, ft:ft + 1])
                            else:
                                last = act.activation(xi, xi, ACT.Identity, scale=amod[:, n, ft, v:v + 1],
                                                      bias=mod[:, layer, shift * KT + ft, v:v + 1])
                    last.then_inc(modulated, 1)
                    if final is None:
                        act.wait_ge(modulated, c + 1)
                        act.activation(hh[:, :, cs[c]], xn[c % 2][:], ACT.Copy).then_inc(high, 1)

            @block.vector
            def _(dve):
                def total(c):
                    dve.wait_ge(squared, c + 1)
                    dve.tensor_reduce(ssq[:, c], sq[c % 2][:].rearrange("p f t -> p t f"), AX_X, ALU.add).then_inc(summed, 1)
                total(0)
                for c in range(NC):
                    dve.wait_ge(rooted, c + 1)
                    dve.reciprocal(rstd[:, c], std[:, c]).then_inc(inverted, 1)
                    if c + 1 < NC:
                        total(c + 1)
                    dve.wait_ge(inverted, c + 1)
                    if c >= 2:
                        if final is None:
                            dve.wait_ge(low, c - 1)
                        else:
                            dve.wait_ge(y_out[c % 2], 16)
                    dve.tensor_tensor(xn[c % 2][:], x[:, :, cs[c]], rstd[:, c].unsqueeze(1).broadcast_to([P, KT, CW]),
                                      ALU.mult).then_inc(scaled, 1)

            @block.tensor
            def _(pe):
                for c in range(NC):
                    pe.wait_ge(summed, c + 1)
                    pe.matmul(ps[:, c, 0:CW], ones[:], ssq[:, c], start=True, stop=True).then_inc(averaged, 1)

            @block.gpsimd
            def _(pool):
                if final is None:
                    for c in range(NC):
                        pool.wait_ge(high, c + 1)
                        pool.tensor_tensor(hl[:, :, cs[c]], xn[c % 2][:], hh[:, :, cs[c]].bitcast(F32),
                                           ALU.subtract).then_inc(low, 1)

    def product(pe, acc, w_hi, w_lo, in_hi, in_lo, first, last):
        pe.matmul(acc, w_hi, in_hi, start=first, stop=False)
        pe.matmul(acc, w_hi, in_lo, start=False, stop=False)
        return pe.matmul(acc, w_lo, in_hi, start=False, stop=last)

    def projection(w_dram, n_tiles, w_off, result=None, spill=None, residual=None, extra=None):
        s, sem, ps, k = stage()
        with s:
            WB = 4 * D
            raw = [at(f"raw{k}_{j}", [P, D], F32, w_off + j * WB) for j in range(2)]
            whi = [at(f"whi{k}_{j}", [P, KT, P], F32R, w_off + (2 + j) * WB) for j in range(2)]
            wlo = [at(f"wlo{k}_{j}", [P, KT, P], F32R, w_off + (4 + j) * WB) for j in range(2)]
            turn = [at(f"turn{k}_{j}", [P, T], F32, w_off + 6 * WB + j * 4 * T) for j in range(2)] if spill is not None else None
            w_in = [sem(f"w_in{j}") for j in range(2)]
            w_high, w_low = sem("w_high"), sem("w_low")
            multiplied, taken = sem("multiplied"), sem("taken")
            x_in, tile_out = sem("x_in"), [sem(f"tile_out{j}") for j in range(2)]
            extra_w, extra_hi, extra_lo, extra_mm, extra_out = (sem("extra_w"), sem("extra_hi"), sem("extra_lo"),
                                                                sem("extra_mm"), sem("extra_out"))
            pairs = n_tiles // 2
            if extra is not None:
                ex_dram, ex_n, ex_dst = extra
                ex_raw = at(f"exraw{k}", [P, KT * ex_n], F32, w_off + 6 * WB + 8 * T)
                ex_hi = at(f"exhi{k}", [P, KT, ex_n], F32R, w_off + 6 * WB + 8 * T + 4 * KT * ex_n)
                ex_lo = at(f"exlo{k}", [P, KT, ex_n], F32R, w_off + 6 * WB + 8 * T + 8 * KT * ex_n)
            block = s.enter_context(nc.Block())

            @block.sync
            def _(sp):
                if extra is not None:
                    sp.dma_start(ex_raw[:], ex_dram).then_inc(extra_w, 16)

                def body(i):
                    for j in range(2):
                        wait(sp, w_low, i, 2, j - 1)
                        m = i * 2 + j
                        sp.dma_start(raw[j][:], w_dram[bass.ds(m, 1)].rearrange("o p n -> p (o n)")).then_inc(w_in[j], 16)
                    if residual is not None and isinstance(i, int):
                        for c in range(NC):
                            sp.dma_start(x[:, :, cs[c]], residual[0][:, :, cs[c]]).then_inc(x_in, 16)
                    if spill is not None and not isinstance(i, int):
                        store(i - 1)

                def store(i):
                    for j in range(2):
                        wait(sp, taken, i, 2 * NC, NC * (j + 1))
                        sp.dma_start(spill[bass.ds(i * 2 + j, 1)].rearrange("o p n -> p (o n)"), turn[j][:]).then_inc(tile_out[j], 16)
                peeled(sp, body, pairs)
                if spill is not None:
                    store(pairs - 1)
                    for j in range(2):
                        sp.wait_ge(tile_out[j], 16 * pairs)

            @block.scalar
            def _(act):
                if extra is not None:
                    act.wait_ge(extra_w, 16)
                    act.activation(ex_hi[:].rearrange("p k n -> p (k n)"), ex_raw[:], ACT.Copy).then_inc(extra_hi, 1)

                def body(i):
                    for j in range(2):
                        wait(act, w_in[j], i, 16, 16)
                        wait(act, multiplied, i, 2 * NC, NC * (j + 1) - 2 * NC)
                        act.activation(whi[j][:].rearrange("p k n -> p (k n)"), raw[j][:], ACT.Copy).then_inc(w_high, 1)
                peeled(act, body, pairs)

            @block.gpsimd
            def _(pool):
                if extra is not None:
                    pool.wait_ge(extra_hi, 1)
                    pool.tensor_tensor(ex_lo[:].rearrange("p k n -> p (k n)"), ex_raw[:],
                                       ex_hi[:].rearrange("p k n -> p (k n)").bitcast(F32), ALU.subtract).then_inc(extra_lo, 1)

                def body(i):
                    for j in range(2):
                        wait(pool, w_high, i, 2, j + 1)
                        pool.tensor_tensor(wlo[j][:].rearrange("p k n -> p (k n)"), raw[j][:],
                                           whi[j][:].rearrange("p k n -> p (k n)").bitcast(F32), ALU.subtract).then_inc(w_low, 1)
                peeled(pool, body, pairs)

            @block.tensor
            def _(pe):
                if extra is not None:
                    pe.wait_ge(extra_lo, 1)
                    for c in range(NC):
                        if c >= 2:
                            pe.wait_ge(extra_out, c - 1)
                        for kk in range(KT):
                            mm = product(pe, ps[0:ex_n, 6 + c % 2, 0:CW], ex_hi[:, kk, :], ex_lo[:, kk, :],
                                         hh[:, kk, cs[c]], hl[:, kk, cs[c]], kk == 0, kk == KT - 1)
                        mm.then_inc(extra_mm, 1)

                def body(i):
                    for j in range(2):
                        wait(pe, w_low, i, 2, j + 1)
                        for c in range(NC):
                            bank = ps[:, NC * j + c]
                            wait(pe, taken, i, 2 * NC, NC * j + c + 1 - 2 * NC)
                            for kk in range(KT):
                                mm = product(pe, bank[:, 0:CW], whi[j][:, kk, :], wlo[j][:, kk, :],
                                             hh[:, kk, cs[c]], hl[:, kk, cs[c]], kk == 0, kk == KT - 1)
                            mm.then_inc(multiplied, 1)
                peeled(pe, body, pairs)

            @block.vector
            def _(dve):
                if extra is not None:
                    for c in range(NC):
                        dve.wait_ge(extra_mm, c + 1)
                        dve.tensor_copy(ex_dst[:, cs[c]], ps[0:ex_n, 6 + c % 2, 0:CW]).then_inc(extra_out, 1)
                if residual is not None:
                    dve.wait_ge(x_in, 16 * NC)

                def body(i):
                    for j in range(2):
                        m = i * 2 + j
                        for c in range(NC):
                            acc = ps[:, NC * j + c]
                            wait(dve, multiplied, i, 2 * NC, NC * j + c + 1)
                            if residual is not None:
                                _, layer, kind = residual
                                for cols, v in pieces[c]:
                                    loc = slice(cols.start - c * CW, cols.stop - c * CW)
                                    xo = x[:, bass.ds(m, 1), cols].rearrange("p o t -> p (o t)")
                                    last = dve.scalar_tensor_tensor(
                                        out=xo, in0=acc[:, loc], scalar=mod[:, layer, bass.ds(m + kind * KT, 1), v],
                                        in1=xo, op0=ALU.mult, op1=ALU.add)
                            elif spill is not None:
                                if c == 0:
                                    wait(dve, tile_out[j], i, 16, 0)
                                last = dve.tensor_copy(turn[j][:, cs[c]], acc[:, 0:CW])
                            else:
                                last = dve.tensor_copy(result[:, bass.ds(m, 1), cs[c]].rearrange("p o t -> p (o t)"), acc[:, 0:CW])
                            last.then_inc(taken, 1)
                peeled(dve, body, pairs)

    def ffn(layer):
        s, sem, ps, k = stage()
        with s:
            o = W0
            raw_in = at(f"raw_in{k}", [P, 2, 2 * D], F32, o)
            raw_out = at(f"raw_out{k}", [P, 2 * D], F32, o + 16 * D)
            wi_hi = at(f"wi_hi{k}", [P, 2, 2, KT, P], F32R, o + 24 * D)
            wi_lo = at(f"wi_lo{k}", [P, 2, 2, KT, P], F32R, o + 40 * D)
            wo_hi = at(f"wo_hi{k}", [P, 2, KT, P], F32R, o + 56 * D)
            wo_lo = at(f"wo_lo{k}", [P, 2, KT, P], F32R, o + 64 * D)
            o += 72 * D
            hid_hi = at(f"hid_hi{k}", [P, NC, 2, CW], F32R, o)
            hid_lo = at(f"hid_lo{k}", [P, NC, 2, CW], F32R, o + 8 * T)
            hid = at(f"hid{k}", [P, 2, CW], F32, o + 16 * T)
            assert o + 16 * T + 8 * CW <= END
            win_in = [sem("win_in0"), sem("win_in1")]
            wout_in = sem("wout_in")
            win_high, win_low, wout_high, wout_low = sem("win_high"), sem("win_low"), sem("wout_high"), sem("wout_low")
            ab_done, silu_done, hid_done, hid_high, hid_low = (sem("ab_done"), sem("silu_done"), sem("hid_done"),
                                                               sem("hid_high"), sem("hid_low"))
            out_acc, added = sem("out_acc"), sem("added")
            N = FFN_PAIRS
            w_in, w_out = inp["w_ffn_in"][layer], inp["w_ffn_out"][layer]
            block = s.enter_context(nc.Block())

            @block.sync
            def _(sp):
                def body(i):
                    for t in range(2):
                        wait(sp, win_low, i, 2, t - 1)
                        sp.dma_start(raw_in[:, t], w_in[bass.ds(i * 2 + t, 1)].rearrange("o p n -> p (o n)")).then_inc(win_in[t], 16)
                    wait(sp, wout_low, i, 1, 0)
                    sp.dma_start(raw_out[:], w_out[bass.ds(i, 1)].rearrange("o p n -> p (o n)")).then_inc(wout_in, 16)
                peeled(sp, body, N)

            @block.scalar
            def _(act):
                def cast_in(i, t):
                    wait(act, win_in[t], i, 16, 16)
                    wait(act, ab_done, i, 6, -(1 - t))
                    act.activation(wi_hi[:, t].rearrange("p a k n -> p (a k n)"), raw_in[:, t], ACT.Copy).then_inc(win_high, 1)

                def body(i, last=False):
                    cast_in(i, 1)
                    for c in range(NC):
                        for t in range(2):
                            wait(act, ab_done, i, 6, 2 * c + t + 1)
                            wait(act, hid_low, i, 3, c)
                            act.activation(hid[:, t], ps[:, 2 * t, 0:CW], ACT.Silu).then_inc(silu_done, 1)
                            if c == NC - 1 and t == 0 and not last:
                                cast_in(i + 1, 0)
                        wait(act, hid_done, i, 6, 2 * c + 2)
                        wait(act, out_acc, i, 3 * KT, KT * (c + 1 - NC))
                        act.activation(hid_hi[:, c], hid[:], ACT.Copy).then_inc(hid_high, 1)
                        if c == 0:
                            wait(act, wout_in, i, 16, 16)
                            wait(act, out_acc, i, 3 * KT, 0)
                            act.activation(wo_hi[:].rearrange("p t k n -> p (t k n)"), raw_out[:], ACT.Copy).then_inc(wout_high, 1)
                cast_in(0, 0)
                body(0)
                with act.Fori(1, N - 1) as i:
                    body(i)
                body(N - 1, last=True)

            @block.gpsimd
            def _(pool):
                def split_in(i, t):
                    wait(pool, win_high, i, 2, t + 1)
                    pool.tensor_tensor(wi_lo[:, t].rearrange("p a k n -> p (a k n)"), raw_in[:, t],
                                       wi_hi[:, t].rearrange("p a k n -> p (a k n)").bitcast(F32), ALU.subtract).then_inc(win_low, 1)

                def body(i):
                    for t in range(2):
                        split_in(i, t)
                    wait(pool, wout_high, i, 1, 1)
                    pool.tensor_tensor(wo_lo[:].rearrange("p t k n -> p (t k n)"), raw_out[:],
                                       wo_hi[:].rearrange("p t k n -> p (t k n)").bitcast(F32), ALU.subtract).then_inc(wout_low, 1)
                peeled(pool, body, N)

            @block.tensor
            def _(pe):
                def contract(i, c):
                    wait(pe, hid_low, i, 3, c + 1)
                    wait(pe, wout_low, i, 1, 1)
                    for ft in range(KT):
                        acc = ps[:, 4 + ft % 4, 0:CW]
                        wait(pe, added, i, 3 * KT, KT * c + ft - 3)
                        for t in range(2):
                            mm = product(pe, acc, wo_hi[:, t, ft], wo_lo[:, t, ft], hid_hi[:, c, t], hid_lo[:, c, t],
                                         t == 0, t == 1)
                        mm.then_inc(out_acc, 1)

                def body(i, first=False):
                    for c in range(NC):
                        for t in range(2):
                            if c == 0:
                                wait(pe, win_low, i, 2, t + 1)
                            wait(pe, hid_done, i, 6, 2 * c + t + 1 - 2)
                            for ab in range(2):
                                for kk in range(KT):
                                    mm = product(pe, ps[:, 2 * t + ab, 0:CW], wi_hi[:, t, ab, kk], wi_lo[:, t, ab, kk],
                                                 hh[:, kk, cs[c]], hl[:, kk, cs[c]], kk == 0, kk == KT - 1)
                            mm.then_inc(ab_done, 1)
                        if c == 0 and first:
                            continue
                        contract(i - 1 if c == 0 else i, (c - 1) % NC)
                body(0, first=True)
                with pe.Fori(1, N) as i:
                    body(i)
                contract(N - 1, NC - 1)

            @block.vector
            def _(dve):
                def add(i, c):
                    for ft in range(KT):
                        wait(dve, out_acc, i, 3 * KT, KT * c + ft + 1)
                        for cols, v in pieces[c]:
                            loc = slice(cols.start - c * CW, cols.stop - c * CW)
                            last = dve.scalar_tensor_tensor(
                                out=x[:, ft, cols], in0=ps[:, 4 + ft % 4, loc],
                                scalar=mod[:, layer, GATE2 * KT + ft, v:v + 1], in1=x[:, ft, cols],
                                op0=ALU.mult, op1=ALU.add)
                        last.then_inc(added, 1)

                def body(i, first=False):
                    for c in range(NC):
                        for t in range(2):
                            wait(dve, silu_done, i, 6, 2 * c + t + 1)
                            dve.tensor_tensor(hid[:, t], ps[:, 2 * t + 1, 0:CW], hid[:, t], ALU.mult).then_inc(hid_done, 1)
                        wait(dve, hid_high, i, 3, c + 1)
                        dve.tensor_tensor(hid_lo[:, c], hid[:], hid_hi[:, c].bitcast(F32), ALU.subtract).then_inc(hid_low, 1)
                        if c == 0 and first:
                            continue
                        add(i - 1 if c == 0 else i, (c - 1) % NC)
                body(0, first=True)
                with dve.Fori(1, N) as i:
                    body(i)
                add(N - 1, NC - 1)

    def attention(qkvu, w_off):
        s, sem, ps, k = stage()
        KALL = T + CTX
        QB = P
        UN = T // QB
        GROUP = 4
        with s:
            o = HH0
            at_buf = [at(f"at{k}_{g}", [P, NT, GROUP * QB], F32, o + g * 4 * NT * GROUP * QB) for g in range(2)]
            o += 8 * NT * GROUP * QB
            prob = [[at(f"prob{k}_{r}{a}", [P, T], F32, o + (2 * r + a) * 4 * T) for a in range(2)] for r in range(2)]
            o += 16 * T
            at_ctx = at(f"at_ctx{k}", [P, QB], F32, o)
            o += 4 * QB
            v_tok = at(f"v_tok{k}", [P, NT + 1, P], F32, o)
            o += 4 * (NT + 1) * P
            v_head = at(f"v_head{k}", [P, T], F32, o)
            o += 4 * T
            rot_cos = at(f"rot_cos{k}", [P, LAT], F32, o)
            rot_sin = at(f"rot_sin{k}", [P, LAT], F32, o + 4 * LAT)
            o += 8 * LAT
            assert o <= X0
            o = w_off
            cos = at(f"cos{k}", [P, LAT], F32, o)
            sin = at(f"sin{k}", [P, LAT], F32, o + 4 * LAT)
            o += 8 * LAT
            q_f = at(f"q_f{k}", [P, T], F32, o)
            k_f = at(f"k_f{k}", [P, KALL], F32, o + 4 * T)
            o += 4 * (T + KALL)
            q_hi = at(f"q_hi{k}", [P, T], F32R, o)
            q_lo = at(f"q_lo{k}", [P, T], F32R, o + 4 * T)
            o += 8 * T
            k_hi = at(f"k_hi{k}", [P, KALL], F32R, o)
            k_lo = at(f"k_lo{k}", [P, KALL], F32R, o + 4 * KALL)
            o += 8 * KALL
            ck = at(f"ck{k}", [P, HEADS, CTX], F32, o)
            cv = at(f"cv{k}", [P, HEADS, P], F32, o + 4 * HEADS * CTX)
            o += 8 * HEADS * P
            win = [at(f"win{k}_{j}", [P, PADW], F32, o + j * 4 * PADW) for j in range(3)]
            o += 12 * PADW
            nmax = at(f"nmax{k}", [P, 2, 2], F32, o)
            esum = at(f"esum{k}", [P, 2, 2], F32, o + 32)
            rinv = at(f"rinv{k}", [P, 2, 2], F32, o + 64)
            w1 = at(f"w1{k}", [P, 2], F32, o + 96)
            assert o + 128 <= END, (o, END)

            loaded, stored = sem("loaded"), sem("stored")
            rotated, v_turned = sem("rotated"), sem("v_turned")
            v_copied, v_out = sem("v_copied"), sem("v_out")
            rope_part, roped = sem("rope_part"), sem("roped")
            qk_high, qk_low = sem("qk_high"), sem("qk_low")
            scored, maxed, exped = sem("scored"), sem("maxed"), sem("exped")
            weighed, combined = sem("weighed"), sem("combined")
            turned, at_out = sem("turned"), sem("at_out")
            pv_done, o_out = sem("pv_done"), sem("o_out")
            pool_step = sem("pool_step")
            H2 = 2 * UN
            ROUNDS = 1 + 3 * (UN - 1)
            tile = lambda n, cols: qkvu[:, bass.ds(n, 1), cols].rearrange("p o t -> p (o t)")
            lat = slice(CTX, T)
            block = s.enter_context(nc.Block())

            @block.sync
            def _(sp):
                for dst, src in ((cos, inp["c_cos"]), (sin, inp["c_sin"]), (ck, inp["cache_k"]), (cv, inp["cache_v"])):
                    sp.dma_start(dst[:], src).then_inc(loaded, 16)
                sp.dma_start(out["new_k"].rearrange("h p t -> p h t"), qkvu[:, HEADS:2 * HEADS, 0:CTX]).then_inc(stored, 16)
                sp.dma_start(out["new_v"].rearrange("h p t -> p h t"), qkvu[:, 2 * HEADS:3 * HEADS, 0:CTX]).then_inc(stored, 16)
                sp.wait_ge(stored, 32)

            @block.scalar
            def _(act):
                act.wait_ge(loaded, 64)

                def exps(i, u, a):
                    r = u % 2
                    if a == 0:
                        wait(act, combined, i, UN, -u if u < 2 else u - 1)
                    wait(act, maxed, i, H2, 2 * u + a + 1)
                    if u == 0:
                        act.activation(prob[r][a][:, 0:CTX], ps[:, 3 * a, 0:CTX], ACT.Exp, bias=nmax[:, r, a:a + 1],
                                       accum_out=esum[:, r, a:a + 1]).then_inc(exped, 1)
                    else:
                        act.activation(prob[r][a][:].rearrange("p (b n) -> p b n", b=3), ps[:, 3 * a:3 * a + 3, 0:CW],
                                       ACT.Exp, bias=nmax[:, r, a:a + 1], accum_out=esum[:, r, a:a + 1]).then_inc(exped, 1)

                def out_of_psum(i, u, r):
                    if u == 0:
                        if r == 0:
                            wait(act, turned, i, ROUNDS, 1)
                            wait(act, pv_done, i, 3, -2)
                            act.activation(at_ctx[:], ps[:, 6, 0:QB], ACT.Copy).then_inc(at_out, 1)
                        return
                    g, j = (u - 1) // GROUP, (u - 1) % GROUP
                    wait(act, turned, i, ROUNDS, 1 + 3 * (u - 1) + r + 1)
                    if j == 0 and r == 0:
                        wait(act, pv_done, i, 3, g + 2 - 3)
                    act.activation(at_buf[g][:, 3 * r:3 * r + 3, j * QB:(j + 1) * QB],
                                   ps[:, 6, 0:3 * QB].rearrange("p (b n) -> p b n", b=3), ACT.Copy).then_inc(at_out, 1)

                def body(i):
                    wait(act, v_turned, i, 1, 0)
                    act.activation(v_head[:], tile(i + 2 * HEADS, slice(0, T)), ACT.Copy).then_inc(v_copied, 1)
                    wait(act, pv_done, i, 3, 0)
                    act.activation(v_tok[:, NT], cv[:, bass.ds(i, 1)].rearrange("p o t -> p (o t)"), ACT.Copy).then_inc(v_out, 1)
                    wait(act, v_turned, i, 1, 1)
                    for r in range(3):
                        act.activation(v_tok[:, 3 * r:3 * r + 3].rearrange("p b n -> p (b n)"), ps[:, 4 + r, 0:3 * P],
                                       ACT.Copy).then_inc(v_out, 1)
                    wait(act, scored, i, H2, 0)
                    wait(act, roped, i, 2, 1)
                    act.activation(q_hi[:], q_f[:], ACT.Copy).then_inc(qk_high, 1)
                    wait(act, roped, i, 2, 2)
                    act.activation(k_hi[:], k_f[:], ACT.Copy).then_inc(qk_high, 1)
                    for u in range(UN):
                        exps(i, u, 0)
                        if u >= 1:
                            out_of_psum(i, u - 1, 0)
                            out_of_psum(i, u - 1, 1)
                        exps(i, u, 1)
                        if u >= 1:
                            out_of_psum(i, u - 1, 2)
                    for r in range(3):
                        out_of_psum(i, UN - 1, r)
                peeled(act, body, HEADS)

            @block.vector
            def _(dve):
                dve.wait_ge(loaded, 64)

                def rope(i, n, dst, src, scale):
                    wait(dve, rotated, i, 2, n + 1)
                    wait(dve, roped, i, 2, n)
                    dve.scalar_tensor_tensor(out=rot_cos[:], in0=src(lat), scalar=scale, in1=cos[:],
                                             op0=ALU.mult, op1=ALU.mult).then_inc(rope_part, 1)
                    dve.scalar_tensor_tensor(out=rot_sin[:].rearrange("p (b n) -> p b n", b=2), in0=ps[:, 2 * n:2 * n + 2],
                                             scalar=scale, in1=sin[:].rearrange("p (b n) -> p b n", b=2),
                                             op0=ALU.mult, op1=ALU.mult).then_inc(rope_part, 1)
                    wait(dve, qk_low, i, 2, n + 1 - 2)
                    dve.tensor_scalar(dst[:, 0:CTX], src(slice(0, CTX)), scale, None, ALU.mult)
                    if n == 1:
                        dve.tensor_copy(dst[:, T:KALL], ck[:, bass.ds(i, 1)].rearrange("p o t -> p (o t)"))
                    wait(dve, rope_part, i, 4, 2 * n + 2)
                    dve.tensor_tensor(dst[:, CTX:T], rot_cos[:], rot_sin[:], ALU.add).then_inc(roped, 1)

                def minus_max(i, u, a):
                    r = u % 2
                    wait(dve, scored, i, H2, 2 * u + a + 1)
                    if a == 0:
                        wait(dve, exped, i, H2, 2 * (u - 1))
                    src = ps[:, 3 * a, 0:CTX] if u == 0 else ps[:, 3 * a:3 * a + 3, 0:CW]
                    dve.tensor_reduce(nmax[:, r, a:a + 1], src, AX_X if u == 0 else mybir.AxisListType.XY, ALU.max,
                                      negate=True).then_inc(maxed, 1)

                def combine(i, u):
                    r = u % 2
                    n = CTX if u == 0 else T
                    wait(dve, exped, i, H2, 2 * u + 2)
                    dve.reciprocal(rinv[:, r], esum[:, r]).then_inc(weighed, 1)
                    wait(dve, weighed, i, 3 * UN, 3 * u + 1)
                    dve.tensor_scalar(w1[:, r:r + 1], rinv[:, r, 1:2], neglam[:, 0:1], None, ALU.mult).then_inc(weighed, 1)
                    wait(dve, weighed, i, 3 * UN, 3 * u + 2)
                    dve.tensor_scalar(prob[r][1][:, 0:n], prob[r][1][:, 0:n], w1[:, r:r + 1], None, ALU.mult).then_inc(weighed, 1)
                    wait(dve, weighed, i, 3 * UN, 3 * u + 3)
                    dve.scalar_tensor_tensor(out=prob[r][0][:, 0:n], in0=prob[r][0][:, 0:n], scalar=rinv[:, r, 0:1],
                                             in1=prob[r][1][:, 0:n], op0=ALU.mult, op1=ALU.add).then_inc(combined, 1)

                def take_o(i, g):
                    cols = slice(0, CTX) if g == 0 else slice(CTX + (g - 1) * 512, CTX + g * 512)
                    wait(dve, pv_done, i, 3, g + 1)
                    dve.tensor_scalar(tile(i, cols), ps[:, 7, 0:cols.stop - cols.start], 1.0, None, ALU.mult).then_inc(o_out, 1)

                def body(i):
                    rope(i, 0, q_f, lambda cols: tile(i, cols), DH ** -0.5)
                    rope(i, 1, k_f, lambda cols: tile(i + HEADS, cols), 1.0)
                    minus_max(i, 0, 0)
                    minus_max(i, 0, 1)
                    for u in range(UN):
                        if u + 1 < UN:
                            minus_max(i, u + 1, 0)
                        combine(i, u)
                        if u + 1 < UN:
                            minus_max(i, u + 1, 1)
                        if u == 2:
                            take_o(i, 0)
                        if u == 6:
                            take_o(i, 1)
                    take_o(i, 2)
                peeled(dve, body, HEADS)

            @block.gpsimd
            def _(pool):
                def body(i):
                    for n, (hi, lo, src) in enumerate(((q_hi, q_lo, q_f), (k_hi, k_lo, k_f))):
                        wait(pool, qk_high, i, 2, n + 1)
                        pool.tensor_tensor(lo[:], src[:], hi[:].bitcast(F32), ALU.subtract).then_inc(qk_low, 1)
                peeled(pool, body, HEADS)

                seqs = ((slice(0, CTX), PAD), (slice(CTX, T), PAD + CTX + 2 * PAD))
                step = 0

                def then(ins):
                    nonlocal step
                    step += 1
                    ins.then_inc(pool_step, 1)
                    pool.wait_ge(pool_step, step)
                then(pool.memset(win[0][:], 0.0))
                for g, w in enumerate(WINDOWS):
                    u = qkvu[:, 3 * HEADS + g]
                    for cols, at_col in seqs:
                        then(pool.tensor_copy(win[0][:, at_col:at_col + cols.stop - cols.start], u[:, cols]))
                    src, n = win[0], PADW
                    for b in range(w.bit_length() - 1):
                        dst = win[1 + b % 2]
                        n -= 1 << b
                        then(pool.tensor_tensor(dst[:, 0:n], src[:, 0:n], src[:, 1 << b:n + (1 << b)], ALU.add))
                        src = dst
                    then(pool.tensor_scalar(src[:, 0:n], src[:, 0:n], 1.0 / w, None, ALU.mult))
                    for cols, at_col in seqs:
                        first, m = at_col - w // 2, cols.stop - cols.start
                        for side, c0 in ((0, first), (1, first + m - PAD)):
                            then(pool.tensor_tensor(src[:, c0:c0 + PAD], src[:, c0:c0 + PAD], edge[:, g, side], ALU.mult))
                        then(pool.tensor_tensor(u[:, cols], src[:, first:first + m], u[:, cols], ALU.subtract))

            @block.tensor
            def _(pe):
                def scores(i, u, between):
                    q = slice(u * QB, (u + 1) * QB)
                    keys = [slice(0, CTX)] if u == 0 else [slice(CTX + c * CW, CTX + (c + 1) * CW) for c in range(NC)]
                    for a in range(2):
                        rows = slice(a * DH, (a + 1) * DH)
                        wait(pe, exped, i, H2, 2 * (u - 1) + a + 1)
                        for c, cols in enumerate(keys):
                            acc = ps[:, 3 * a + c, 0:cols.stop - cols.start]
                            pe.matmul(acc, q_hi[rows, q], k_hi[rows, cols], start=True, stop=False)
                            pe.matmul(acc, q_hi[rows, q], k_lo[rows, cols], start=False, stop=False)
                            mm = pe.matmul(acc, q_lo[rows, q], k_hi[rows, cols], start=False, stop=True)
                            if c == len(keys) - 1:
                                mm.then_inc(scored, 1)
                            if a == 1 and between:
                                between.pop(0)()
                    while between:
                        between.pop(0)()

                def turning(i, u):
                    def round_(r):
                        n = 0 if u == 0 else 1 + 3 * (u - 1) + r
                        if r == 0:
                            wait(pe, combined, i, UN, u + 1)
                        wait(pe, at_out, i, ROUNDS, n)
                        for b in range(1 if u == 0 else 3):
                            mm = pe.transpose(ps[:, 6, b * P:(b + 1) * P],
                                              prob[u % 2][0][:, (3 * r + b) * P:(3 * r + b + 1) * P], ident[:])
                        mm.then_inc(turned, 1)
                    return [lambda r=r: round_(r) for r in range(1 if u == 0 else 3)]

                def values(i, g):
                    wait(pe, at_out, i, ROUNDS, 1 if g == 0 else 1 + 3 * GROUP * g)
                    wait(pe, v_out, i, 4, 4)
                    wait(pe, o_out, i, 3, g)
                    if g == 0:
                        pe.matmul(ps[:, 7, 0:CTX], v_tok[:, 0], at_ctx[:], start=True, stop=True).then_inc(pv_done, 1)
                        return
                    for kt in range(NT):
                        mm = pe.matmul(ps[:, 7], v_tok[:, kt + 1], at_buf[g - 1][:, kt], start=(kt == 0), stop=(kt == NT - 1))
                    mm.then_inc(pv_done, 1)

                def body(i):
                    wait(pe, exped, i, H2, 0)
                    wait(pe, v_copied, i, 1, 1)
                    wait(pe, at_out, i, ROUNDS, 0)
                    for n in range(2):
                        for b in range(2):
                            mm = pe.matmul(ps[:, 2 * n + b], rot_t[:], tile(i + n * HEADS, slice(CTX + b * 512, CTX + (b + 1) * 512)),
                                           start=True, stop=True)
                        mm.then_inc(rotated, 1)
                    for t in range(NT):
                        mm = pe.transpose(ps[:, 4 + t // 3, (t % 3) * P:(t % 3 + 1) * P], v_head[:, t * P:(t + 1) * P], ident[:])
                    mm.then_inc(v_turned, 1)
                    wait(pe, qk_low, i, 2, 2)
                    wait(pe, v_out, i, 4, 4)
                    scores(i, 0, [])
                    for u in range(1, UN):
                        scores(i, u, turning(i, u - 1))
                        if u == 2:
                            values(i, 0)
                        if u == 6:
                            values(i, 1)
                    for r in turning(i, UN - 1):
                        r()
                    values(i, 2)
                peeled(pe, body, HEADS)

    def even_output(qkvu, w_off):
        s, sem, ps, k = stage()
        with s:
            sq = [at(f"sq{k}_{j}", [P, T], F32, w_off + j * 4 * T) for j in range(2)]
            std = [at(f"std{k}_{j}", [P, T], F32, w_off + (2 + j) * 4 * T) for j in range(2)]
            rstd = at(f"rstd{k}", [P, T], F32, w_off + 16 * T)
            w_pool = at(f"w_pool{k}", [P, HEADS, P], F32, w_off + 20 * T)
            w_in, squared, averaged, rooted = sem("w_in"), sem("squared"), sem("averaged"), sem("rooted")
            inverted, ready, high, low = sem("inverted"), sem("ready"), sem("high"), sem("low")
            mixed, pooled = sem("mixed"), sem("pooled")
            tri = lambda ap: ap.rearrange("p (b n) -> p b n", b=NC)
            block = s.enter_context(nc.Block())

            @block.sync
            def _(sp):
                sp.dma_start(w_pool[:], inp["w_pool"]).then_inc(w_in, 16)

            @block.tensor
            def _(pe):
                pe.wait_ge(w_in, 16)
                for h in range(HEADS):
                    if h >= 1:
                        pe.wait_ge(rooted, h)
                        pe.wait_ge(pooled, h)
                    for c in range(NC):
                        mm = pe.matmul(ps[:, 3 + c, 0:CW], w_pool[:, h], qkvu[:, 3 * HEADS + h, cs[c]], start=True, stop=True)
                    mm.then_inc(mixed, 1)
                    pe.wait_ge(squared, h + 1)
                    for c in range(NC):
                        mm = pe.matmul(ps[:, c, 0:CW], ones[:], sq[h % 2][:, cs[c]], start=True, stop=True)
                    mm.then_inc(averaged, 1)

            @block.scalar
            def _(act):
                def square(h):
                    if h >= 2:
                        act.wait_ge(averaged, h - 1)
                    act.activation(sq[h % 2][:], qkvu[:, h], ACT.Square).then_inc(squared, 1)
                square(0)
                for h in range(HEADS):
                    if h + 1 < HEADS:
                        square(h + 1)
                    act.wait_ge(averaged, h + 1)
                    if h >= 2:
                        act.wait_ge(inverted, h - 1)
                    act.activation(tri(std[h % 2][:]), ps[:, 0:NC, 0:CW], ACT.Sqrt, bias=eps[:], scale=1.0 / P).then_inc(rooted, 1)
                for n in range(2 * HEADS):
                    act.wait_ge(pooled if n % 2 else ready, n // 2 + 1)
                    src = qkvu[:, n // 2 + (n % 2) * 3 * HEADS]
                    act.activation(hh[:, n // 2 + (n % 2) * HEADS], src, ACT.Copy).then_inc(high, 1)

            @block.vector
            def _(dve):
                for h in range(HEADS):
                    dve.wait_ge(rooted, h + 1)
                    if h >= 1:
                        dve.wait_ge(ready, h)
                    dve.reciprocal(rstd[:], std[h % 2][:]).then_inc(inverted, 1)
                    dve.wait_ge(inverted, h + 1)
                    dve.scalar_tensor_tensor(out=qkvu[:, h], in0=qkvu[:, h], scalar=subg[:, h:h + 1], in1=rstd[:],
                                             op0=ALU.mult, op1=ALU.mult).then_inc(ready, 1)
                    dve.wait_ge(mixed, h + 1)
                    dve.tensor_scalar(tri(qkvu[:, 3 * HEADS + h]), ps[:, 3:3 + NC, 0:CW], pscale[:, h:h + 1], None,
                                      ALU.mult).then_inc(pooled, 1)

            @block.gpsimd
            def _(pool):
                for n in range(2 * HEADS):
                    pool.wait_ge(high, n + 1)
                    ft = n // 2 + (n % 2) * HEADS
                    pool.tensor_tensor(hl[:, ft], qkvu[:, n // 2 + (n % 2) * 3 * HEADS], hh[:, ft].bitcast(F32), ALU.subtract).then_inc(low, 1)

    def gla(gd, o_all):
        s, sem, ps, k = stage()
        with s:
            o = HH0
            head = at(f"head{k}", [P, 6, T], F32, o)
            o += 24 * T
            v_tok = at(f"v_tok{k}", [P, NT, 2 * P], F32, o)
            o += 8 * NT * P
            state = [at(f"state{k}_{d}", [P, NCHUNK, 2 * P], F32, o + d * 8 * NCHUNK * P) for d in range(2)]
            o += 16 * NCHUNK * P
            assert o <= X0
            o = W0
            names = ["log_part", "gate", "decay_sum", "grow", "shrink", "to_end"]
            log_part, gate, decay_sum, grow, shrink, to_end = [at(f"{n}{k}", [P, T], F32, o + j * 4 * T)
                                                                for j, n in enumerate(names)]
            squares = at(f"squares{k}", [P, 2, T], F32, o + 4 * 4 * T)
            o += 24 * T
            q_t = [at(f"q_t{k}_{d}", [P, T], F32, o + d * 4 * T) for d in range(2)]
            k_t = [at(f"k_t{k}_{d}", [P, T], F32, o + (2 + d) * 4 * T) for d in range(2)]
            a_t = [at(f"a_t{k}_{d}", [P, NT, P], F32, o + (4 + d) * 4 * T) for d in range(2)]
            k_end = at(f"k_end{k}", [P, T], F32, o + 24 * T)
            k_end_tok = at(f"k_end_tok{k}", [P, NT, P], F32, o + 28 * T)
            scan_mask = at(f"scan_mask{k}", [P, T], F32, o + 32 * T)
            o += 36 * T
            up = at(f"up{k}", [48, P], F32, o)
            o += 4 * P
            assert o <= GD0, (o, GD0)

            mask_in, head_in, up_in, state_in = sem("mask_in"), sem("head_in"), sem("up_in"), sem("state_in")
            states_out = sem("states_out")
            v_turned, v_out = sem("v_turned"), sem("v_out")
            z_done, gate_act, gate_min, gate_sum, scanned = (sem("z_done"), sem("gate_act"), sem("gate_min"),
                                                             sem("gate_sum"), sem("scanned"))
            grown, to_go, ended = sem("grown"), sem("to_go"), sem("ended")
            q_ready, k_ready, k_end_ready = sem("q_ready"), sem("k_ready"), sem("k_end_ready")
            k_end_turned, k_end_out = sem("k_end_turned"), sem("k_end_out")
            kv_done, stepped = sem("kv_done"), sem("stepped")
            a_done, a_out = sem("a_done"), sem("a_out")
            o_done, o_out, silu_r = sem("o_done"), sem("o_out"), sem("silu_r")
            squared, averaged, rooted, inverted, scaled, finished = (sem("squared"), sem("averaged"), sem("rooted"),
                                                                     sem("inverted"), sem("scaled"), sem("finished"))
            NPAIR = NCHUNK // 2
            STEPS = 2 + 2 * (NPAIR - 1) - 1
            pair_order = [list(range(NPAIR)), [0] + list(range(NPAIR - 1, 0, -1))]
            last_of = lambda ap, d: (ap.rearrange("p (n c) -> p n c", c=GCH)[:, :, GCH - 1:GCH] if d == 0 else
                                     ap.rearrange("p (n c) -> p n c", c=GCH)[:, :, 0:1])
            tri = lambda ap: ap.rearrange("p (b n) -> p b n", b=NC)

            def state_steps(d):
                first, second = (0, 1) if d == 0 else (1, 0)
                steps = [(None, first, second), (second, second, first)]
                for q in pair_order[d][1:]:
                    for n in ((2 * q, 2 * q + 1) if d == 0 else (2 * q + 1, 2 * q)):
                        dst = n + 1 if d == 0 else n - 1
                        if 2 <= dst < NCHUNK:
                            steps.append((n, n, dst))
                assert len(steps) == STEPS
                return steps
            block = s.enter_context(nc.Block())

            @block.sync
            def _(sp):
                sp.dma_start(scan_mask[:], inp["c_scan"]).then_inc(mask_in, 16)

                def body(i):
                    wait(sp, finished, i, 2, 0)
                    sp.dma_start(head[:], gla_dram[bass.ds(i * 6, 6)].rearrange("m p t -> p m t")).then_inc(head_in, 16)
                    sp.dma_start(up[:], inp["w_up"][bass.ds(i, 1)].rearrange("o p n -> p (o n)")).then_inc(up_in, 16)
                    for d in range(2):
                        sp.dma_start(state[d][:, 2 if d == 0 else NCHUNK - 1],
                                     inp["state"][d, bass.ds(i, 1)].rearrange("o p n -> p (o n)")).then_inc(state_in, 16)
                    for d in range(2):
                        wait(sp, stepped, i, 2 * STEPS, d * STEPS + 2)
                        sp.dma_start(out["new_state"][d, bass.ds(i, 1)].rearrange("o p n -> p (o n)"),
                                     state[d][:, d]).then_inc(states_out, 16)
                peeled(sp, body, HEADS)
                sp.wait_ge(states_out, 32 * HEADS)

            @block.scalar
            def _(act):
                def body(i):
                    wait(act, v_turned, i, 1, 1)
                    flat = v_tok[:].rearrange("p n m -> p (n m)")
                    for b in range(5):
                        n = min(512, NT * 2 * P - 512 * b)
                        act.activation(flat[:, 512 * b:512 * b + n], ps[:, b, 0:n], ACT.Copy).then_inc(v_out, 1)
                    for d in range(2):
                        wait(act, z_done, i, 2, d + 1)
                        wait(act, gate_sum, i, 2, d)
                        act.activation(tri(log_part[:]), ps[:, 0:NC, 0:CW], ACT.Abs,
                                       bias=bgate[:, d, bass.ds(i, 1)]).then_inc(gate_act, 1)
                        wait(act, gate_act, i, 6, 3 * d + 1)
                        act.activation(log_part[:], log_part[:], ACT.Exp, scale=-1.0).then_inc(gate_act, 1)
                        wait(act, gate_act, i, 6, 3 * d + 2)
                        act.activation(log_part[:], log_part[:], ACT.Ln, bias=ones[:, 0:1]).then_inc(gate_act, 1)
                        wait(act, scanned, i, 2, d + 1)
                        wait(act, stepped, i, 2 * STEPS, d * STEPS)
                        if d == 0:
                            wait(act, averaged, i, 1, 0)
                        act.activation(grow[:], decay_sum[:], ACT.Exp, scale=1.0 / GATE_TEMP).then_inc(grown, 1)
                        wait(act, k_ready, i, 2, d)
                        act.activation(shrink[:], decay_sum[:], ACT.Exp, scale=-1.0 / GATE_TEMP).then_inc(grown, 1)
                        wait(act, to_go, i, 2, d + 1)
                        wait(act, k_end_ready, i, 2, d)
                        act.activation(to_end[:], gate[:], ACT.Exp, scale=1.0 / GATE_TEMP).then_inc(ended, 1)
                        wait(act, k_end_turned, i, 2, d + 1)
                        wait(act, kv_done, i, 2 * NPAIR, d * NPAIR)
                        flat = k_end_tok[:].rearrange("p n m -> p (n m)")
                        for b in range(3):
                            n = min(512, NT * P - 512 * b)
                            act.activation(flat[:, 512 * b:512 * b + n], ps[:, 3 + b, 0:n], ACT.Copy).then_inc(k_end_out, 1)
                    act.activation(head[:, 4:6], head[:, 4:6], ACT.Silu).then_inc(silu_r, 1)
                    wait(act, o_out, i, 6, 6)
                    act.activation(squares[:], head[:, 0:2], ACT.Square).then_inc(squared, 1)
                    wait(act, averaged, i, 1, 1)
                    act.activation(tri(log_part[:]), ps[:, 3:3 + NC, 0:CW], ACT.Sqrt, bias=eps[:], scale=1.0 / (2 * P)).then_inc(rooted, 1)
                peeled(act, body, HEADS)

            @block.vector
            def _(dve):
                dve.wait_ge(mask_in, 16)

                def body(i):
                    for d in range(2):
                        wait(dve, gate_act, i, 6, 3 * d + 1)
                        wait(dve, ended, i, 2, d)
                        if d == 0:
                            wait(dve, scaled, i, 1, 0)
                        dve.tensor_scalar(tri(gate[:]), ps[:, 0:NC, 0:CW], bgate[:, d, bass.ds(i, 1)], 0.0,
                                          ALU.add, ALU.min).then_inc(gate_min, 1)
                        wait(dve, gate_act, i, 6, 3 * d + 3)
                        wait(dve, gate_min, i, 2, d + 1)
                        dve.tensor_tensor(gate[:], gate[:], log_part[:], ALU.subtract).then_inc(gate_sum, 1)
                        wait(dve, gate_sum, i, 2, d + 1)
                        wait(dve, grown, i, 4, 2 * d)
                        src, dst = (gate[:], decay_sum[:]) if d == 0 else (gate[:, ::-1], decay_sum[:, ::-1])
                        dve.tensor_tensor_scan(dst, scan_mask[:], src, 0.0, ALU.mult, ALU.add).then_inc(scanned, 1)
                        wait(dve, scanned, i, 2, d + 1)
                        dve.tensor_tensor(gate[:].rearrange("p (n c) -> p n c", c=GCH),
                                          last_of(decay_sum[:], d).broadcast_to([P, NCHUNK, GCH]),
                                          decay_sum[:].rearrange("p (n c) -> p n c", c=GCH), ALU.subtract).then_inc(to_go, 1)
                        wait(dve, grown, i, 4, 2 * d + 1)
                        wait(dve, head_in, i, 16, 16)
                        wait(dve, o_done, i, 6, 0)
                        dve.scalar_tensor_tensor(out=q_t[d][:], in0=head[:, 0], scalar=DK_SCALE, in1=grow[:],
                                                 op0=ALU.mult, op1=ALU.mult).then_inc(q_ready, 1)
                        for b in range(3):
                            wait(dve, a_done, i, 6, 3 * d + b + 1)
                            dve.tensor_tensor(a_t[d][:, 3 * b:3 * b + 3], ps[:, b, 0:3 * P].rearrange("p (b n) -> p b n", b=3),
                                              mask_gla[:, d:d + 1].broadcast_to([P, 3, P]), ALU.mult).then_inc(a_out, 1)
                        if d == 0:
                            wait(dve, state_in, i, 32, 32)
                        steps = state_steps(d)
                        for n, (src_n, chunk, dst_n) in enumerate(steps):
                            p = pair_order[d].index(chunk // 2)
                            kv = ps[:, (6, 3)[p % 2] + chunk % 2, 0:2 * P]
                            wait(dve, kv_done, i, 2 * NPAIR, d * NPAIR + p + 1)
                            if src_n is None:
                                if d == 0:
                                    wait(dve, states_out, i, 32, 0)
                                dve.tensor_scalar(state[d][:, dst_n], kv, 1.0, None, ALU.mult).then_inc(stepped, 1)
                            else:
                                wait(dve, stepped, i, 2 * STEPS, d * STEPS + n)
                                col = chunk * GCH + (GCH - 1 if d == 0 else 0)
                                dve.scalar_tensor_tensor(out=state[d][:, dst_n], in0=state[d][:, src_n], scalar=grow[:, col:col + 1],
                                                         in1=kv, op0=ALU.mult, op1=ALU.add).then_inc(stepped, 1)
                    wait(dve, k_end_ready, i, 2, 2)
                    for n, (j, b) in enumerate([(j, b) for j in range(2) for b in range(3)]):
                        w = min(512, T - 512 * b)
                        wait(dve, o_done, i, 6, n + 1)
                        dve.tensor_copy(head[:, j, 512 * b:512 * b + w], ps[:, 3 * (1 - j) + b, 0:w]).then_inc(o_out, 1)
                    wait(dve, rooted, i, 1, 1)
                    dve.reciprocal(gate[:], log_part[:]).then_inc(inverted, 1)
                    wait(dve, inverted, i, 1, 1)
                    dve.tensor_tensor(head[:, 0:2], head[:, 0:2], gate[:].unsqueeze(1).broadcast_to([P, 2, T]), ALU.mult).then_inc(scaled, 1)
                    wait(dve, scaled, i, 1, 1)
                    wait(dve, silu_r, i, 1, 1)
                    for j in range(2):
                        dve.scalar_tensor_tensor(out=o_all[:, bass.ds(i * 2 + j, 1)].rearrange("p o t -> p (o t)"), in0=head[:, j],
                                                 scalar=vnorm[:, bass.ds(i * 2 + j, 1)], in1=head[:, 4 + j],
                                                 op0=ALU.mult, op1=ALU.mult).then_inc(finished, 1)
                peeled(dve, body, HEADS)

            @block.gpsimd
            def _(pool):
                def body(i):
                    for d in range(2):
                        wait(pool, grown, i, 4, 2 * d + 2)
                        wait(pool, head_in, i, 16, 16)
                        wait(pool, a_done, i, 6, 3 * d - 3)
                        pool.tensor_tensor(k_t[d][:], head[:, 1], shrink[:], ALU.mult).then_inc(k_ready, 1)
                        wait(pool, ended, i, 2, d + 1)
                        wait(pool, k_end_turned, i, 2, d)
                        pool.tensor_tensor(k_end[:], head[:, 1], to_end[:], ALU.mult).then_inc(k_end_ready, 1)
                peeled(pool, body, HEADS)

            @block.tensor
            def _(pe):
                def body(i):
                    wait(pe, head_in, i, 16, 16)
                    wait(pe, o_out, i, 6, 0)
                    wait(pe, rooted, i, 1, 0)
                    for n in range(2 * NT):
                        t, j = n // 2, n % 2
                        mm = pe.transpose(ps[:, n // 4, (n % 4) * P:(n % 4 + 1) * P], head[:, 2 + j, t * P:(t + 1) * P], ident[:])
                    mm.then_inc(v_turned, 1)
                    wait(pe, up_in, i, 16, 16)
                    for d in range(2):
                        wait(pe, v_out, i, 5, 5)
                        wait(pe, a_out, i, 6, 3 * d)
                        for c in range(NC):
                            rows = slice(32 * d, 32 * d + 16)
                            mm = pe.matmul(ps[:, c, 0:CW], up[rows, :], gd[rows, cs[c]], start=True, stop=True)
                        mm.then_inc(z_done, 1)
                        wait(pe, k_end_ready, i, 2, d + 1)
                        wait(pe, stepped, i, 2 * STEPS, d * STEPS)
                        for t in range(NT):
                            mm = pe.transpose(ps[:, 3 + t // 4, (t % 4) * P:(t % 4 + 1) * P], k_end[:, t * P:(t + 1) * P], ident[:])
                        mm.then_inc(k_end_turned, 1)
                        wait(pe, gate_min, i, 2, d + 1)
                        wait(pe, q_ready, i, 2, d + 1)
                        wait(pe, k_ready, i, 2, d + 1)
                        for t in range(NT):
                            tok = slice(t * P, (t + 1) * P)
                            mm = pe.matmul(ps[:, t // 3, (t % 3) * P:(t % 3 + 1) * P], k_t[d][:, tok], q_t[d][:, tok],
                                           start=True, stop=True)
                            if t % 3 == 2:
                                mm.then_inc(a_done, 1)
                        wait(pe, k_end_out, i, 6, 3 * d + 3)
                        done = 0
                        for n, p in enumerate(pair_order[d]):
                            if n >= 2:
                                done = sum(1 for _, chunk, _ in state_steps(d) if pair_order[d].index(chunk // 2) <= n - 2)
                                wait(pe, stepped, i, 2 * STEPS, d * STEPS + done)
                            else:
                                wait(pe, stepped, i, 2 * STEPS, d * STEPS)
                            for e in range(2):
                                rows = slice(e * GCH, (e + 1) * GCH)
                                mm = pe.matmul(ps[:, (6, 3)[n % 2] + e, 0:2 * P], k_end_tok[rows, p, :], v_tok[rows, p, :],
                                               start=True, stop=True)
                            mm.then_inc(kv_done, 1)
                    wait(pe, a_out, i, 6, 6)
                    wait(pe, stepped, i, 2 * STEPS, 2 * STEPS)
                    for j in range(2):
                        dv = slice(j * P, (j + 1) * P)
                        for t in range(NT):
                            tok = slice(t * P, (t + 1) * P)
                            bank, c0 = 3 * (1 - j) + t // 4, (t % 4) * P
                            pe.matmul(ps[:, bank, c0:c0 + P], v_tok[:, t, dv], a_t[0][:, t], start=True, stop=False,
                                      skip_group_check=True)
                            inter = [(d, n) for d in range(2) for n in (2 * t, 2 * t + 1) if (d, n) not in ((0, 0), (1, 1))]
                            for d, n in inter:
                                c1 = c0 + (n % 2) * GCH
                                pe.matmul(ps[:, bank, c1:c1 + GCH], state[d][:, n, dv], q_t[d][:, n * GCH:(n + 1) * GCH],
                                          start=False, stop=False, skip_group_check=True)
                            mm = pe.matmul(ps[:, bank, c0:c0 + P], v_tok[:, t, dv], a_t[1][:, t], start=False, stop=True,
                                           skip_group_check=True)
                            if t % 4 == 3 or t == NT - 1:
                                mm.then_inc(o_done, 1)
                    wait(pe, squared, i, 1, 1)
                    for c in range(NC):
                        for j in range(2):
                            mm = pe.matmul(ps[:, 3 + c, 0:CW], ones[:], squares[:, j, cs[c]], start=(j == 0), stop=(j == 1))
                    mm.then_inc(averaged, 1)
                peeled(pe, body, HEADS)

    def split(src):
        s, sem, ps, k = stage()
        with s:
            high = sem("high")
            block = s.enter_context(nc.Block())

            @block.scalar
            def _(act):
                for ft in range(KT):
                    act.activation(hh[:, ft], src[:, ft], ACT.Copy).then_inc(high, 1)

            @block.vector
            def _(dve):
                for ft in range(KT):
                    dve.wait_ge(high, ft + 1)
                    dve.tensor_tensor(hl[:, ft], src[:, ft], hh[:, ft].bitcast(F32), ALU.subtract)

    QK0 = X0
    WQ = X0 + 4 * EVEN_TILES * T
    qkvu = at("qkvu", [P, EVEN_TILES, T], F32, QK0)

    o_all = at("o_all", [P, KT, T], F32, X0)
    gd = at("gd", [DH, T], F32, GD0)

    modulation()
    norm(0, layer=0, shift=SHIFT1, load=inp["x"])
    projection(inp["w_in_even"], EVEN_TILES, WQ, result=qkvu)
    attention(qkvu, WQ)
    even_output(qkvu, WQ)
    projection(inp["w_out_even"], KT, W0, residual=(inp["x"], 0, GATE1))
    norm(1, layer=0, shift=SHIFT2)
    ffn(0)
    recycle()
    norm(2, layer=1, shift=SHIFT1, spill=True)
    projection(inp["w_in_odd"], ODD_TILES, W0, spill=gla_dram, extra=(inp["w_gd"], DH, gd))
    gla(gd, o_all)
    split(o_all)
    projection(inp["w_out_odd"], KT, W0, residual=(xs_dram, 1, GATE1))
    norm(3, layer=1, shift=SHIFT2)
    ffn(1)
    norm(4, final=out["y"])

    ctx.close()


def layout(a):
    import numpy as np

    def cols(v):
        v = np.asarray(v)
        return np.moveaxis(v.reshape(*v.shape[:-1], v.shape[-1] // P, P), -1, 0)

    def tiles(w):
        kk, n = w.shape
        return w.reshape(kk // P, P, n // P, P).transpose(2, 1, 0, 3).reshape(n // P, P, kk)

    f = lambda v: np.ascontiguousarray(v, dtype=np.float32)
    x_t = np.concatenate([a["x_prompt"][0], a["x_sample"][0]], axis=0)
    r = {"x": x_t.T.reshape(KT, P, T).transpose(1, 0, 2)}
    r["cond"] = np.moveaxis(cols(np.stack([a["c_ctx"], a["c"][0]])), 1, 2)
    r["w_mod"] = np.concatenate([tiles(a["w_mod"][l]) for l in range(2)])
    r["b_mod"] = cols(a["b_mod"])
    r["gnorm"] = cols(np.stack([a["norm1_g"][0], a["norm2_g"][0], a["norm1_g"][1], a["norm2_g"][1], a["final_g"]]))
    r["lam"] = np.broadcast_to(a["lam_params"], (P, 4, DH))
    r["subln"] = cols(a["subln_g"][0])
    r["pscale"] = cols(a["pool_scale"][0])
    r["bgate"] = cols(a["b_gate"][0])
    r["gla_norm"] = cols(a["gla_norm_g"][0])
    r["w_in_even"] = tiles(a["w_in_even"][0])
    r["w_out_even"] = tiles(a["w_out_even"][0])
    w = a["w_in_odd"][0]
    order = []
    for h in range(HEADS):
        order += [h, 4 + h, 8 + 2 * h, 9 + 2 * h, 16 + 2 * h, 17 + 2 * h]
    r["w_in_odd"] = tiles(w[:, :ODD_TILES * P])[order]
    gd = np.zeros((D, DH), np.float32)
    gd[:, 0:16], gd[:, 32:48] = w[:, ODD_TILES * P:ODD_TILES * P + 16], w[:, ODD_TILES * P + 16:]
    r["w_gd"] = gd.reshape(KT, P, DH).transpose(1, 0, 2).reshape(P, KT * DH)
    up = np.zeros((HEADS, 48, P), np.float32)
    for d in range(2):
        up[:, 32 * d:32 * d + 16] = a["w_gate_up"][0, d].reshape(16, HEADS, P).transpose(1, 0, 2)
    r["w_up"] = up
    r["w_out_odd"] = tiles(a["w_out_odd"][0])
    r["w_pool"] = a["w_pool"][0].transpose(1, 0, 2)
    fin, fout = [], []
    for l in range(2):
        t = tiles(a["w_ffn_in"][l])
        n = HIDDEN // P
        fin.append(np.stack([t[:n], t[n:]], axis=2).reshape(n, P, 2 * D))
        fout.append(a["w_ffn_out"][l].reshape(FFN_PAIRS, 2, P, D).transpose(0, 2, 1, 3).reshape(FFN_PAIRS, P, 2 * D))
    r["w_ffn_in"], r["w_ffn_out"] = np.stack(fin), np.stack(fout)
    r["cache_k"] = a["cache_attn_k"][0, 0].reshape(CTX, HEADS, P).transpose(2, 1, 0)
    r["cache_v"] = a["cache_attn_v"][0, 0]
    r["state"] = a["state_gla"][0, 0]

    r["c_ident"] = np.eye(P)
    q = np.arange(P)
    rot = np.zeros((P, P))
    lower = q % 32 < 16
    rot[q[lower], q[lower] + 16] = -1.0
    rot[q[~lower], q[~lower] - 16] = 1.0
    r["c_rot"] = rot.T
    j, i = np.meshgrid(q, q, indexing="ij")
    same = j // GCH == i // GCH
    r["c_mask"] = np.stack([same & (j <= i), same & (j >= i)], axis=1)
    inv = (1.0 / (10000.0 ** (np.arange(0, 32, 2, dtype=np.float32) / np.float32(32)))).astype(np.float32)
    t = np.arange(LAT)
    place = np.where((q[:, None] // 32) % 2 == 0, t // 64, t % 64).astype(np.float32)
    ang = place * inv[q % 16][:, None]
    r["c_cos"], r["c_sin"] = np.cos(ang), np.sin(ang)
    e = np.ones((P, len(WINDOWS), 2, PAD), np.float32)
    for n, w in enumerate(WINDOWS):
        k = np.arange(PAD)
        e[:, n, 0] = w / np.minimum(w, k + w // 2)
        e[:, n, 1] = w / np.minimum(w, PAD - k + w // 2)
    r["c_edge"] = e
    scan = np.ones((P, T), np.float32)
    scan[:, ::GCH] = 0.0
    r["c_scan"] = scan
    return {n: f(v) for n, v in r.items()}


_OUTS = {"y": (P, KT, T), "new_k": (HEADS, P, CTX), "new_v": (HEADS, P, CTX), "new_state": (2, HEADS, P, 2 * P)}


def kernel(**inputs):
    import concourse.bacc as _bacc
    import numpy as _np
    from concourse.bass_utils import run_bass_kernel_spmd as _run

    nc = _bacc.Bacc("TRN2", target_bir_lowering=False, num_devices=1)
    arrays, inp, out = {}, {}, {}
    for name, v in layout({n: _np.asarray(v) for n, v in inputs.items()}).items():
        arrays[f"in_{name}_dram"] = v
        inp[name] = nc.dram_tensor(f"in_{name}_dram", v.shape, F32, kind="ExternalInput").ap()
    for name, shape in _OUTS.items():
        out[name] = nc.dram_tensor(f"out_{name}_dram", shape, F32, kind="ExternalOutput").ap()
    build(nc, inp, out)
    got = _run(nc, [arrays], core_ids=[0]).results[0]
    y = got["out_y_dram"].transpose(2, 1, 0).reshape(T, D)
    new_k = got["out_new_k_dram"].transpose(2, 0, 1).reshape(1, 1, CTX, HEADS, 2, DH)
    new_v = got["out_new_v_dram"].transpose(2, 0, 1).reshape(1, 1, CTX, HEADS, P)
    state = got["out_new_state_dram"].reshape(1, 1, 2, HEADS, P, 2 * P)
    return (y[None, :CTX], y[None, CTX:], new_k, new_v, state)
```

```python
from contextlib import ExitStack

import concourse.bass as bass
from concourse import mybir

F32 = mybir.dt.float32
F32R = mybir.dt.float32r
ALU = mybir.AluOpType
ACT = mybir.ActivationFunctionType
AX_X = mybir.AxisListType.X

P = 128
D = 1024
KT = D // P
CTX = 128
LAT = 1024
T = CTX + LAT
NC = 3
CW = T // NC
EPS = 1e-6
HEADS = 4
HIDDEN = 2816
FFN_PAIRS = HIDDEN // (2 * P)
LAM_INIT = 0.2
DH = 64
WINDOWS = (2, 4, 8, 16)
GCH = 64
NCHUNK = T // GCH
NT = T // P
GATE_TEMP = 16.0
DK_SCALE = float(P) ** -0.5
SHIFT1, SCALE1, GATE1, SHIFT2, SCALE2, GATE2 = range(6)
PAD = 8
PADW = PAD + CTX + 2 * PAD + LAT + PAD
EVEN_TILES = 16
U0, Q0, K0, V0 = 0, 4, 8, 12
MOD_FIRST = 2 * KT
MOD_GLA = 4
ODD_TILES = 24


def wait(eng, sem, i, per, n):
    if isinstance(i, int):
        if i * per + n > 0:
            eng.wait_ge(sem, i * per + n)
    else:
        eng.wait_ge(sem, i * per + n)


def peeled(eng, body, n):
    body(0)
    if n > 1:
        with eng.Fori(1, n) as i:
            body(i)


def build(nc, inp, out):
    base = (nc.sbuf_base + 63) // 64 * 64

    def at(name, shape, dtype, offset):
        return nc.alloc_sbuf_tensor_at(name, shape, dtype, offset=base + offset)

    XB = 4 * KT * T
    C0 = 6656
    HH0, HL0, X0, W0 = C0, C0 + XB, C0 + 2 * XB, C0 + 3 * XB
    END = nc.sbuf_usable_end - base
    GD0 = END // 32 * 32 - 4 * T

    ctx = ExitStack()

    pos = [0]

    def const(name, shape, dtype=F32):
        t = at(name, shape, dtype, pos[0])
        n = 4
        for s in shape[1:]:
            n *= s
        pos[0] += (n + 31) // 32 * 32
        assert pos[0] <= C0, pos[0]
        return t

    ident = const("ident", [P, P])
    ones = const("ones", [P, P])
    rot_t = const("rot_t", [P, P])
    mask_gla = const("mask_gla", [P, 2, P])
    cond = const("cond", [P, KT, 2])
    silu_c = const("silu_c", [P, KT, 2])
    bmod = const("bmod", [P, 2, 6 * KT])
    mod = const("mod", [P, 2, 6 * KT, 2])
    gnorm = const("gnorm", [P, 5, KT])
    amod = const("amod", [P, 4, KT, 2])
    eps = const("eps", [P, 1])
    lamp = const("lamp", [P, 4, DH])
    lamw = const("lamw", [P, 8])
    neglam = const("neglam", [P, 1])
    subg = const("subg", [P, HEADS])
    pscale = const("pscale", [P, HEADS])
    edge = const("edge", [P, len(WINDOWS), 2, PAD])
    bgate = const("bgate", [P, 2, HEADS])
    nbgate = const("nbgate", [P, 2, HEADS])
    vnorm = const("vnorm", [P, 2 * HEADS])

    hh = at("hh", [P, KT, T], F32R, HH0)
    hl = at("hl", [P, KT, T], F32R, HL0)
    x = at("x", [P, KT, T], F32, X0)

    xs_dram = nc.dram_tensor("x_spill", [P, KT, T], F32, kind="Internal").ap()
    gla_dram = nc.dram_tensor("gla_spill", [ODD_TILES, P, T], F32, kind="Internal").ap()

    nstage = [0]
    semaphores = []

    def stage():
        s = ExitStack()
        nstage[0] += 1
        k = nstage[0]
        psum = s.enter_context(nc.psum_tensor(f"ps{k}", [P, 8, 512], F32))

        def sem(name):
            semaphores.append(nc.alloc_semaphore(f"s{k}_{name}"))
            return semaphores[-1]
        return s, sem, psum, k

    def recycle():
        nc.clear_and_free_semaphores(semaphores)
        semaphores.clear()
        nc.all_engine_barrier()

    cs = [slice(c * CW, (c + 1) * CW) for c in range(NC)]
    pieces = [[(slice(0, CTX), 0), (slice(CTX, CW), 1)]] + [[(cs[c], 1)] for c in range(1, NC)]

    def scale_columns(dve, n):
        kind = (SCALE1, SCALE2)[n % 2]
        dve.scalar_tensor_tensor(out=amod[:, n], in0=mod[:, n // 2, kind * KT:(kind + 1) * KT, :], scalar=1.0,
                                 in1=gnorm[:, n].unsqueeze(2).broadcast_to([P, KT, 2]), op0=ALU.add, op1=ALU.mult)

    def modulation():
        s, sem, ps, k = stage()
        SL = 8
        NM = MOD_FIRST
        with s:
            wm = at("wm", [P, SL, KT, P], F32, W0)
            consts_in = sem("consts_in")
            w_in = [sem(f"w_in{j}") for j in range(SL)]
            w_used = sem("w_used")
            silu_done = sem("silu_done")
            mod_done = sem("mod_done")
            dve_step = sem("dve_step")
            lam_exp = sem("lam_exp")
            small = [(ident, "c_ident"), (rot_t, "c_rot"), (mask_gla, "c_mask"), (cond, "cond"), (bmod, "b_mod"),
                     (gnorm, "gnorm"), (lamp, "lam"), (subg, "subln"), (pscale, "pscale"), (edge, "c_edge"),
                     (bgate, "bgate"), (vnorm, "gla_norm")]
            block = s.enter_context(nc.Block())

            @block.scalar
            def _(act):
                for t, name in small:
                    act.dma_start(t[:], inp[name]).then_inc(consts_in, 16)
                act.wait_ge(consts_in, 16 * len(small))
                act.activation(silu_c[:], cond[:], ACT.Silu).then_inc(silu_done, 1)
                act.wait_ge(dve_step, 2)
                act.activation(lamw[:, 2:4], lamw[:, 0:2], ACT.Exp).then_inc(lam_exp, 1)

            @block.sync
            def _(sp):
                def body(i):
                    for j in range(SL):
                        wait(sp, w_used, i, SL, j + 1 - SL)
                        m = i * SL + j
                        src = inp["w_mod"][m] if isinstance(m, int) else inp["w_mod"][bass.ds(m, 1)].rearrange("o p n -> p (o n)")
                        sp.dma_start(wm[:, j].rearrange("p k n -> p (k n)"), src).then_inc(w_in[j], 16)
                peeled(sp, body, NM // SL)

            @block.tensor
            def _(pe):
                pe.wait_ge(silu_done, 1)

                def body(i):
                    for j in range(SL):
                        wait(pe, w_in[j], i, 16, 16)
                        for kk in range(KT):
                            mm = pe.matmul(ps[:, 0, bass.ds((i * SL + j) * 2, 2)], wm[:, j, kk, :], silu_c[:, kk, :],
                                           start=(kk == 0), stop=(kk == KT - 1))
                        mm.then_inc(w_used, 1)
                peeled(pe, body, NM // SL)

            @block.gpsimd
            def _(pool):
                pool.memset(ones[:], 1.0)
                pool.memset(eps[:], EPS)

            @block.vector
            def _(dve):
                dve.wait_ge(consts_in, 16 * len(small))
                dve.tensor_tensor(lamp[:, 0:3:2], lamp[:, 0:3:2], lamp[:, 1:4:2], ALU.mult).then_inc(dve_step, 1)
                dve.wait_ge(dve_step, 1)
                dve.tensor_reduce(lamw[:, 0:2], lamp[:, 0:3:2], AX_X, ALU.add).then_inc(dve_step, 1)
                dve.wait_ge(lam_exp, 1)
                dve.tensor_tensor(lamw[:, 4:5], lamw[:, 3:4], lamw[:, 2:3], ALU.subtract).then_inc(dve_step, 1)
                dve.wait_ge(dve_step, 3)
                dve.tensor_scalar(neglam[:], lamw[:, 4:5], -LAM_INIT, None, ALU.add)
                dve.tensor_scalar(subg[:], subg[:], 1.0 - LAM_INIT, None, ALU.mult)
                dve.wait_ge(w_used, NM)
                dve.tensor_tensor(mod[:, 0, 0:NM], ps[:, 0, 0:2 * NM].rearrange("p (m v) -> p m v", v=2),
                                  bmod[:, 0, 0:NM].unsqueeze(2).broadcast_to([P, NM, 2]), ALU.add).then_inc(mod_done, 1)
                dve.wait_ge(mod_done, 1)
                scale_columns(dve, 0)

    mod_flat = mod[:].rearrange("p l m v -> p (l m) v")
    bmod_flat = bmod[:].rearrange("p l m -> p (l m)")
    MSL = 4

    def more_modulation(sem, k, ps, bank, offset, m0, n, scales=()):
        wm = at(f"wm{k}", [P, MSL, KT, P], F32, offset)
        assert offset + 4 * MSL * D <= END
        wm_in = [sem(f"wm_in{j}") for j in range(MSL)]
        wm_used, mod_taken = sem("wm_used"), sem("mod_taken")

        def load(sp):
            for j in range(n):
                if j >= MSL:
                    sp.wait_ge(wm_used, j + 1 - MSL)
                sp.dma_start(wm[:, j % MSL].rearrange("p k n -> p (k n)"), inp["w_mod"][m0 + j]).then_inc(wm_in[j % MSL], 16)

        def multiply(pe, a, b):
            for j in range(a, b):
                pe.wait_ge(wm_in[j % MSL], 16 * (j // MSL + 1))
                for kk in range(KT):
                    mm = pe.matmul(ps[:, bank, 2 * j:2 * j + 2], wm[:, j % MSL, kk], silu_c[:, kk],
                                   start=(kk == 0), stop=(kk == KT - 1))
                mm.then_inc(wm_used, 1)

        def take(dve):
            dve.wait_ge(wm_used, n)
            dve.tensor_tensor(mod_flat[:, m0:m0 + n], ps[:, bank, 0:2 * n].rearrange("p (m v) -> p m v", v=2),
                              bmod_flat[:, m0:m0 + n].unsqueeze(2).broadcast_to([P, n, 2]), ALU.add).then_inc(mod_taken, 1)
            if scales:
                dve.wait_ge(mod_taken, 1)
            for j in scales:
                scale_columns(dve, j)
        return load, multiply, take

    def norm(n, layer=None, shift=None, load=None, spill=False, final=None, mods=None):
        s, sem, ps, k = stage()
        with s:
            sq = [at(f"sq{k}_{j}", [P, KT, CW], F32, W0 + j * 4 * KT * CW) for j in range(2)]
            xn = [at(f"xn{k}_{j}", [P, KT, CW], F32, W0 + (2 + j) * 4 * KT * CW) for j in range(2)]
            ssq = at(f"ssq{k}", [P, NC, CW], F32, W0 + 16 * KT * CW)
            std = at(f"std{k}", [P, NC, CW], F32, W0 + 16 * KT * CW + 4 * T)
            rstd = at(f"rstd{k}", [P, NC, CW], F32, W0 + 16 * KT * CW + 8 * T)
            x_in = [sem(f"x_in{c}") for c in range(NC)]
            y_out = [sem(f"y_out{j}") for j in range(2)]
            squared, summed, averaged, rooted = sem("squared"), sem("summed"), sem("averaged"), sem("rooted")
            inverted, scaled, modulated, high, low, stored = (sem("inverted"), sem("scaled"), sem("modulated"),
                                                              sem("high"), sem("low"), sem("stored"))
            if mods is not None:
                mod_load, mod_multiply, mod_take = more_modulation(sem, k, ps, 4, W0 + 16 * KT * CW + 12 * T, *mods)
            block = s.enter_context(nc.Block())

            @block.sync
            def _(sp):
                sent = 0
                if load is not None:
                    for c in range(NC):
                        sp.dma_start(x[:, :, cs[c]], load[:, :, cs[c]]).then_inc(x_in[c], 16)
                if spill:
                    if load is not None:
                        for c in range(NC):
                            sp.wait_ge(x_in[c], 16)
                    sp.dma_start(xs_dram, x[:]).then_inc(stored, 16)
                    sent += 16
                if mods is not None:
                    mod_load(sp)
                if final is not None:
                    for c in range(NC):
                        sp.wait_ge(modulated, c + 1)
                        sp.dma_start(final[:, :, cs[c]], xn[c % 2][:]).then_inc(y_out[c % 2], 16)
                    sp.wait_ge(y_out[0], 32)
                    sp.wait_ge(y_out[1], 16)
                if sent:
                    sp.wait_ge(stored, sent)

            @block.scalar
            def _(act):
                def square(c):
                    if load is not None:
                        act.wait_ge(x_in[c], 16)
                    if c >= 2:
                        act.wait_ge(summed, c - 1)
                    act.activation(sq[c % 2][:], x[:, :, cs[c]], ACT.Square).then_inc(squared, 1)

                def root(c):
                    act.wait_ge(averaged, c + 1)
                    act.activation(std[:, c], ps[:, c, 0:CW], ACT.Sqrt, bias=eps[:], scale=1.0 / D).then_inc(rooted, 1)

                square(0)
                square(1)
                root(0)
                for c in range(NC):
                    if c + 1 < NC:
                        root(c + 1)
                    if c == 0:
                        square(2)
                    act.wait_ge(scaled, c + 1)
                    for ft in range(KT):
                        for cols, v in pieces[c]:
                            loc = slice(cols.start - c * CW, cols.stop - c * CW)
                            xi = xn[c % 2][:, ft, loc]
                            if final is not None:
                                last = act.activation(xi, xi, ACT.Identity, scale=gnorm[:, n, ft:ft + 1])
                            else:
                                last = act.activation(xi, xi, ACT.Identity, scale=amod[:, n, ft, v:v + 1],
                                                      bias=mod[:, layer, shift * KT + ft, v:v + 1])
                    last.then_inc(modulated, 1)
                    if final is None:
                        act.wait_ge(modulated, c + 1)
                        act.activation(hh[:, :, cs[c]], xn[c % 2][:], ACT.Copy).then_inc(high, 1)

            @block.vector
            def _(dve):
                def total(c):
                    dve.wait_ge(squared, c + 1)
                    dve.tensor_reduce(ssq[:, c], sq[c % 2][:].rearrange("p f t -> p t f"), AX_X, ALU.add).then_inc(summed, 1)
                total(0)
                for c in range(NC):
                    dve.wait_ge(rooted, c + 1)
                    dve.reciprocal(rstd[:, c], std[:, c]).then_inc(inverted, 1)
                    if c + 1 < NC:
                        total(c + 1)
                    dve.wait_ge(inverted, c + 1)
                    if c >= 2:
                        if final is None:
                            dve.wait_ge(low, c - 1)
                        else:
                            dve.wait_ge(y_out[c % 2], 16)
                    dve.tensor_tensor(xn[c % 2][:], x[:, :, cs[c]], rstd[:, c].unsqueeze(1).broadcast_to([P, KT, CW]),
                                      ALU.mult).then_inc(scaled, 1)
                if mods is not None:
                    mod_take(dve)

            @block.tensor
            def _(pe):
                for c in range(NC):
                    if mods is not None:
                        mod_multiply(pe, 2 * c, 2 * c + 2)
                    pe.wait_ge(summed, c + 1)
                    pe.matmul(ps[:, c, 0:CW], ones[:], ssq[:, c], start=True, stop=True).then_inc(averaged, 1)
                if mods is not None:
                    mod_multiply(pe, 2 * NC, mods[1])

            @block.gpsimd
            def _(pool):
                if final is None:
                    for c in range(NC):
                        pool.wait_ge(high, c + 1)
                        pool.tensor_tensor(hl[:, :, cs[c]], xn[c % 2][:], hh[:, :, cs[c]].bitcast(F32),
                                           ALU.subtract).then_inc(low, 1)

    def product(pe, acc, w_hi, w_lo, in_hi, in_lo, first, last):
        pe.matmul(acc, w_hi, in_hi, start=first, stop=False)
        pe.matmul(acc, w_hi, in_lo, start=False, stop=False)
        return pe.matmul(acc, w_lo, in_hi, start=False, stop=last)

    def projection(w_dram, n_tiles, w_off, result=None, spill=None, residual=None, extra=None, pooling=False):
        s, sem, ps, k = stage()
        with s:
            WB = 4 * D
            raw = [at(f"raw{k}_{j}", [P, D], F32, w_off + j * WB) for j in range(2)]
            whi = [at(f"whi{k}_{j}", [P, KT, P], F32R, w_off + (2 + j) * WB) for j in range(2)]
            wlo = [at(f"wlo{k}_{j}", [P, KT, P], F32R, w_off + (4 + j) * WB) for j in range(2)]
            turn = [at(f"turn{k}_{j}", [P, T], F32, w_off + 6 * WB + j * 4 * T) for j in range(2)] if spill is not None else None
            w_in = [sem(f"w_in{j}") for j in range(2)]
            w_high, w_low = sem("w_high"), sem("w_low")
            multiplied, taken = sem("multiplied"), sem("taken")
            x_in, tile_out = sem("x_in"), [sem(f"tile_out{j}") for j in range(2)]
            extra_w, extra_hi, extra_lo, extra_mm, extra_out = (sem("extra_w"), sem("extra_hi"), sem("extra_lo"),
                                                                sem("extra_mm"), sem("extra_out"))
            pairs = n_tiles // 2
            if pooling:
                pool_step = sem("pool_step")
                win = [at(f"win{k}_{j}", [P, PADW], F32, w_off + 6 * WB + j * 4 * PADW) for j in range(3)]
            if extra is not None:
                ex_dram, ex_n, ex_dst = extra
                ex_raw = at(f"exraw{k}", [P, KT * ex_n], F32, w_off + 6 * WB + 8 * T)
                ex_hi = at(f"exhi{k}", [P, KT, ex_n], F32R, w_off + 6 * WB + 8 * T + 4 * KT * ex_n)
                ex_lo = at(f"exlo{k}", [P, KT, ex_n], F32R, w_off + 6 * WB + 8 * T + 8 * KT * ex_n)
            block = s.enter_context(nc.Block())

            @block.sync
            def _(sp):
                if extra is not None:
                    sp.dma_start(ex_raw[:], ex_dram).then_inc(extra_w, 16)

                def body(i):
                    for j in range(2):
                        wait(sp, w_low, i, 2, j - 1)
                        m = i * 2 + j
                        sp.dma_start(raw[j][:], w_dram[bass.ds(m, 1)].rearrange("o p n -> p (o n)")).then_inc(w_in[j], 16)
                    if residual is not None and isinstance(i, int):
                        for c in range(NC):
                            sp.dma_start(x[:, :, cs[c]], residual[0][:, :, cs[c]]).then_inc(x_in, 16)
                    if spill is not None and not isinstance(i, int):
                        store(i - 1)

                def store(i):
                    for j in range(2):
                        wait(sp, taken, i, 2 * NC, NC * (j + 1))
                        sp.dma_start(spill[bass.ds(i * 2 + j, 1)].rearrange("o p n -> p (o n)"), turn[j][:]).then_inc(tile_out[j], 16)
                peeled(sp, body, pairs)
                if spill is not None:
                    store(pairs - 1)
                    for j in range(2):
                        sp.wait_ge(tile_out[j], 16 * pairs)

            @block.scalar
            def _(act):
                if extra is not None:
                    act.wait_ge(extra_w, 16)
                    act.activation(ex_hi[:].rearrange("p k n -> p (k n)"), ex_raw[:], ACT.Copy).then_inc(extra_hi, 1)

                def body(i):
                    for j in range(2):
                        wait(act, w_in[j], i, 16, 16)
                        wait(act, multiplied, i, 2 * NC, NC * (j + 1) - 2 * NC)
                        act.activation(whi[j][:].rearrange("p k n -> p (k n)"), raw[j][:], ACT.Copy).then_inc(w_high, 1)
                peeled(act, body, pairs)

            @block.gpsimd
            def _(pool):
                if extra is not None:
                    pool.wait_ge(extra_hi, 1)
                    pool.tensor_tensor(ex_lo[:].rearrange("p k n -> p (k n)"), ex_raw[:],
                                       ex_hi[:].rearrange("p k n -> p (k n)").bitcast(F32), ALU.subtract).then_inc(extra_lo, 1)

                def body(i):
                    for j in range(2):
                        wait(pool, w_high, i, 2, j + 1)
                        pool.tensor_tensor(wlo[j][:].rearrange("p k n -> p (k n)"), raw[j][:],
                                           whi[j][:].rearrange("p k n -> p (k n)").bitcast(F32), ALU.subtract).then_inc(w_low, 1)
                if not pooling:
                    peeled(pool, body, pairs)
                    return

                seqs = ((slice(0, CTX), PAD), (slice(CTX, T), PAD + CTX + 2 * PAD))
                step = 0

                def then(ins):
                    nonlocal step
                    step += 1
                    ins.then_inc(pool_step, 1)
                    pool.wait_ge(pool_step, step)

                def fill(g):
                    u = result[:, U0 + g]
                    pool.wait_ge(taken, NC * (U0 + g + 1))
                    for cols, at_col in seqs:
                        then(pool.tensor_copy(win[0][:, at_col:at_col + cols.stop - cols.start], u[:, cols]))
                    double(g, 0)

                def double(g, b):
                    src, dst, n = win[0 if b == 0 else 1 + (b - 1) % 2], win[1 + b % 2], PADW + 1 - (2 << b)
                    then(pool.tensor_tensor(dst[:, 0:n], src[:, 0:n], src[:, 1 << b:n + (1 << b)], ALU.add))

                def average(g):
                    w = WINDOWS[g]
                    b = w.bit_length() - 2
                    src, n, u = win[1 + b % 2], PADW + 1 - w, result[:, U0 + g]
                    then(pool.tensor_scalar(src[:, 0:n], src[:, 0:n], 1.0 / w, None, ALU.mult))
                    for cols, at_col in seqs:
                        first, m = at_col - w // 2, cols.stop - cols.start
                        for side, c0 in ((0, first), (1, first + m - PAD)):
                            then(pool.tensor_tensor(src[:, c0:c0 + PAD], src[:, c0:c0 + PAD], edge[:, g, side], ALU.mult))
                        then(pool.tensor_tensor(u[:, cols], src[:, first:first + m], u[:, cols], ALU.subtract))
                pieces_ = [lambda: (fill(0), average(0)), lambda: (fill(1), double(1, 1), average(1)),
                           lambda: (fill(2), double(2, 1)), lambda: (double(2, 2), average(2)),
                           lambda: (fill(3), double(3, 1), double(3, 2)), lambda: (double(3, 3), average(3))]
                then(pool.memset(win[0][:], 0.0))
                for i in range(pairs):
                    body(i)
                    if i >= 2:
                        pieces_[i - 2]()

            @block.tensor
            def _(pe):
                if extra is not None:
                    pe.wait_ge(extra_lo, 1)
                    for c in range(NC):
                        if c >= 2:
                            pe.wait_ge(extra_out, c - 1)
                        for kk in range(KT):
                            mm = product(pe, ps[0:ex_n, 6 + c % 2, 0:CW], ex_hi[:, kk, :], ex_lo[:, kk, :],
                                         hh[:, kk, cs[c]], hl[:, kk, cs[c]], kk == 0, kk == KT - 1)
                        mm.then_inc(extra_mm, 1)

                def body(i):
                    for j in range(2):
                        wait(pe, w_low, i, 2, j + 1)
                        for c in range(NC):
                            bank = ps[:, NC * j + c]
                            wait(pe, taken, i, 2 * NC, NC * j + c + 1 - 2 * NC)
                            for kk in range(KT):
                                mm = product(pe, bank[:, 0:CW], whi[j][:, kk, :], wlo[j][:, kk, :],
                                             hh[:, kk, cs[c]], hl[:, kk, cs[c]], kk == 0, kk == KT - 1)
                            mm.then_inc(multiplied, 1)
                peeled(pe, body, pairs)

            @block.vector
            def _(dve):
                if extra is not None:
                    for c in range(NC):
                        dve.wait_ge(extra_mm, c + 1)
                        dve.tensor_copy(ex_dst[:, cs[c]], ps[0:ex_n, 6 + c % 2, 0:CW]).then_inc(extra_out, 1)
                if residual is not None:
                    dve.wait_ge(x_in, 16 * NC)

                def body(i):
                    for j in range(2):
                        m = i * 2 + j
                        for c in range(NC):
                            acc = ps[:, NC * j + c]
                            wait(dve, multiplied, i, 2 * NC, NC * j + c + 1)
                            if residual is not None:
                                _, layer, kind = residual
                                for cols, v in pieces[c]:
                                    loc = slice(cols.start - c * CW, cols.stop - c * CW)
                                    xo = x[:, bass.ds(m, 1), cols].rearrange("p o t -> p (o t)")
                                    last = dve.scalar_tensor_tensor(
                                        out=xo, in0=acc[:, loc], scalar=mod[:, layer, bass.ds(m + kind * KT, 1), v],
                                        in1=xo, op0=ALU.mult, op1=ALU.add)
                            elif spill is not None:
                                if c == 0:
                                    wait(dve, tile_out[j], i, 16, 0)
                                last = dve.tensor_copy(turn[j][:, cs[c]], acc[:, 0:CW])
                            else:
                                last = dve.tensor_copy(result[:, bass.ds(m, 1), cs[c]].rearrange("p o t -> p (o t)"), acc[:, 0:CW])
                            last.then_inc(taken, 1)
                peeled(dve, body, pairs)

    def ffn(layer):
        s, sem, ps, k = stage()
        with s:
            o = W0
            raw_in = at(f"raw_in{k}", [P, 2, 2 * D], F32, o)
            raw_out = at(f"raw_out{k}", [P, 2 * D], F32, o + 16 * D)
            wi_hi = at(f"wi_hi{k}", [P, 2, 2, KT, P], F32R, o + 24 * D)
            wi_lo = at(f"wi_lo{k}", [P, 2, 2, KT, P], F32R, o + 40 * D)
            wo_hi = at(f"wo_hi{k}", [P, 2, KT, P], F32R, o + 56 * D)
            wo_lo = at(f"wo_lo{k}", [P, 2, KT, P], F32R, o + 64 * D)
            o += 72 * D
            hid_hi = at(f"hid_hi{k}", [P, NC, 2, CW], F32R, o)
            hid_lo = at(f"hid_lo{k}", [P, NC, 2, CW], F32R, o + 8 * T)
            hid = at(f"hid{k}", [P, 2, CW], F32, o + 16 * T)
            assert o + 16 * T + 8 * CW <= END
            win_in = [sem("win_in0"), sem("win_in1")]
            wout_in = sem("wout_in")
            win_high, win_low, wout_high, wout_low = sem("win_high"), sem("win_low"), sem("wout_high"), sem("wout_low")
            ab_done, silu_done, hid_done, hid_high, hid_low = (sem("ab_done"), sem("silu_done"), sem("hid_done"),
                                                               sem("hid_high"), sem("hid_low"))
            out_acc, added = sem("out_acc"), sem("added")
            N = FFN_PAIRS
            w_in, w_out = inp["w_ffn_in"][layer], inp["w_ffn_out"][layer]
            block = s.enter_context(nc.Block())

            @block.sync
            def _(sp):
                def body(i):
                    for t in range(2):
                        wait(sp, win_low, i, 2, t - 1)
                        sp.dma_start(raw_in[:, t], w_in[bass.ds(i * 2 + t, 1)].rearrange("o p n -> p (o n)")).then_inc(win_in[t], 16)
                    wait(sp, wout_low, i, 1, 0)
                    sp.dma_start(raw_out[:], w_out[bass.ds(i, 1)].rearrange("o p n -> p (o n)")).then_inc(wout_in, 16)
                peeled(sp, body, N)

            @block.scalar
            def _(act):
                def cast_in(i, t):
                    wait(act, win_in[t], i, 16, 16)
                    wait(act, ab_done, i, 6, -(1 - t))
                    act.activation(wi_hi[:, t].rearrange("p a k n -> p (a k n)"), raw_in[:, t], ACT.Copy).then_inc(win_high, 1)

                def body(i, last=False):
                    cast_in(i, 1)
                    for c in range(NC):
                        for t in range(2):
                            wait(act, ab_done, i, 6, 2 * c + t + 1)
                            wait(act, hid_low, i, 3, c)
                            act.activation(hid[:, t], ps[:, 2 * t, 0:CW], ACT.Silu).then_inc(silu_done, 1)
                            if c == NC - 1 and t == 0 and not last:
                                cast_in(i + 1, 0)
                        wait(act, hid_done, i, 6, 2 * c + 2)
                        wait(act, out_acc, i, 3 * KT, KT * (c + 1 - NC))
                        act.activation(hid_hi[:, c], hid[:], ACT.Copy).then_inc(hid_high, 1)
                        if c == 0:
                            wait(act, wout_in, i, 16, 16)
                            wait(act, out_acc, i, 3 * KT, 0)
                            act.activation(wo_hi[:].rearrange("p t k n -> p (t k n)"), raw_out[:], ACT.Copy).then_inc(wout_high, 1)
                cast_in(0, 0)
                body(0)
                with act.Fori(1, N - 1) as i:
                    body(i)
                body(N - 1, last=True)

            @block.gpsimd
            def _(pool):
                def split_in(i, t):
                    wait(pool, win_high, i, 2, t + 1)
                    pool.tensor_tensor(wi_lo[:, t].rearrange("p a k n -> p (a k n)"), raw_in[:, t],
                                       wi_hi[:, t].rearrange("p a k n -> p (a k n)").bitcast(F32), ALU.subtract).then_inc(win_low, 1)

                def body(i):
                    for t in range(2):
                        split_in(i, t)
                    wait(pool, wout_high, i, 1, 1)
                    pool.tensor_tensor(wo_lo[:].rearrange("p t k n -> p (t k n)"), raw_out[:],
                                       wo_hi[:].rearrange("p t k n -> p (t k n)").bitcast(F32), ALU.subtract).then_inc(wout_low, 1)
                peeled(pool, body, N)

            @block.tensor
            def _(pe):
                def contract(i, c):
                    wait(pe, hid_low, i, 3, c + 1)
                    wait(pe, wout_low, i, 1, 1)
                    for ft in range(KT):
                        acc = ps[:, 4 + ft % 4, 0:CW]
                        wait(pe, added, i, 3 * KT, KT * c + ft - 3)
                        for t in range(2):
                            mm = product(pe, acc, wo_hi[:, t, ft], wo_lo[:, t, ft], hid_hi[:, c, t], hid_lo[:, c, t],
                                         t == 0, t == 1)
                        mm.then_inc(out_acc, 1)

                def body(i, first=False):
                    for c in range(NC):
                        for t in range(2):
                            if c == 0:
                                wait(pe, win_low, i, 2, t + 1)
                            wait(pe, hid_done, i, 6, 2 * c + t + 1 - 2)
                            for ab in range(2):
                                for kk in range(KT):
                                    mm = product(pe, ps[:, 2 * t + ab, 0:CW], wi_hi[:, t, ab, kk], wi_lo[:, t, ab, kk],
                                                 hh[:, kk, cs[c]], hl[:, kk, cs[c]], kk == 0, kk == KT - 1)
                            mm.then_inc(ab_done, 1)
                        if c == 0 and first:
                            continue
                        contract(i - 1 if c == 0 else i, (c - 1) % NC)
                body(0, first=True)
                with pe.Fori(1, N) as i:
                    body(i)
                contract(N - 1, NC - 1)

            @block.vector
            def _(dve):
                def add(i, c):
                    for ft in range(KT):
                        wait(dve, out_acc, i, 3 * KT, KT * c + ft + 1)
                        for cols, v in pieces[c]:
                            loc = slice(cols.start - c * CW, cols.stop - c * CW)
                            last = dve.scalar_tensor_tensor(
                                out=x[:, ft, cols], in0=ps[:, 4 + ft % 4, loc],
                                scalar=mod[:, layer, GATE2 * KT + ft, v:v + 1], in1=x[:, ft, cols],
                                op0=ALU.mult, op1=ALU.add)
                        last.then_inc(added, 1)

                def body(i, first=False):
                    for c in range(NC):
                        for t in range(2):
                            wait(dve, silu_done, i, 6, 2 * c + t + 1)
                            dve.tensor_tensor(hid[:, t], ps[:, 2 * t + 1, 0:CW], hid[:, t], ALU.mult).then_inc(hid_done, 1)
                        wait(dve, hid_high, i, 3, c + 1)
                        dve.tensor_tensor(hid_lo[:, c], hid[:], hid_hi[:, c].bitcast(F32), ALU.subtract).then_inc(hid_low, 1)
                        if c == 0 and first:
                            continue
                        add(i - 1 if c == 0 else i, (c - 1) % NC)
                body(0, first=True)
                with dve.Fori(1, N) as i:
                    body(i)
                add(N - 1, NC - 1)

    def attention(qkvu, w_off):
        s, sem, ps, k = stage()
        KALL = T + CTX
        QB = P
        UN = T // QB
        GROUP = 4
        with s:
            o = HH0
            at_buf = [at(f"at{k}_{g}", [P, NT, GROUP * QB], F32, o + g * 4 * NT * GROUP * QB) for g in range(2)]
            o += 8 * NT * GROUP * QB
            prob = [[at(f"prob{k}_{r}{a}", [P, T], F32, o + (2 * r + a) * 4 * T) for a in range(2)] for r in range(2)]
            o += 16 * T
            at_ctx = at(f"at_ctx{k}", [P, QB], F32, o)
            o += 4 * QB
            v_tok = at(f"v_tok{k}", [P, NT + 1, P], F32, o)
            o += 4 * (NT + 1) * P
            v_head = at(f"v_head{k}", [P, T], F32, o)
            o += 4 * T
            rot_cos = at(f"rot_cos{k}", [P, LAT], F32, o)
            rot_sin = at(f"rot_sin{k}", [P, LAT], F32, o + 4 * LAT)
            o += 8 * LAT
            assert o <= X0
            o = w_off
            cos = at(f"cos{k}", [P, LAT], F32, o)
            sin = at(f"sin{k}", [P, LAT], F32, o + 4 * LAT)
            o += 8 * LAT
            q_f = at(f"q_f{k}", [P, T], F32, o)
            k_f = at(f"k_f{k}", [P, KALL], F32, o + 4 * T)
            o += 4 * (T + KALL)
            q_hi = at(f"q_hi{k}", [P, T], F32R, o)
            q_lo = at(f"q_lo{k}", [P, T], F32R, o + 4 * T)
            o += 8 * T
            k_hi = at(f"k_hi{k}", [P, KALL], F32R, o)
            k_lo = at(f"k_lo{k}", [P, KALL], F32R, o + 4 * KALL)
            o += 8 * KALL
            ck = at(f"ck{k}", [P, HEADS, CTX], F32, o)
            cv = at(f"cv{k}", [P, HEADS, P], F32, o + 4 * HEADS * CTX)
            o += 8 * HEADS * P
            nmax = at(f"nmax{k}", [P, 2, 2], F32, o)
            esum = at(f"esum{k}", [P, 2, 2], F32, o + 32)
            rinv = at(f"rinv{k}", [P, 2, 2], F32, o + 64)
            w1 = at(f"w1{k}", [P, 2], F32, o + 96)
            assert o + 128 <= END, (o, END)

            loaded, stored = sem("loaded"), sem("stored")
            rotated, v_turned = sem("rotated"), sem("v_turned")
            v_copied, v_out = sem("v_copied"), sem("v_out")
            rope_part, roped = sem("rope_part"), sem("roped")
            qk_high, qk_low = sem("qk_high"), sem("qk_low")
            scored, maxed, exped = sem("scored"), sem("maxed"), sem("exped")
            weighed, combined = sem("weighed"), sem("combined")
            turned, at_out = sem("turned"), sem("at_out")
            pv_done, o_out = sem("pv_done"), sem("o_out")
            H2 = 2 * UN
            ROUNDS = 1 + 3 * (UN - 1)
            tile = lambda n, cols: qkvu[:, bass.ds(n, 1), cols].rearrange("p o t -> p (o t)")
            lat = slice(CTX, T)
            block = s.enter_context(nc.Block())

            @block.sync
            def _(sp):
                for dst, src in ((cos, inp["c_cos"]), (sin, inp["c_sin"]), (ck, inp["cache_k"]), (cv, inp["cache_v"])):
                    sp.dma_start(dst[:], src).then_inc(loaded, 16)
                sp.dma_start(out["new_k"].rearrange("h p t -> p h t"), qkvu[:, K0:K0 + HEADS, 0:CTX]).then_inc(stored, 16)
                sp.dma_start(out["new_v"].rearrange("h p t -> p h t"), qkvu[:, V0:V0 + HEADS, 0:CTX]).then_inc(stored, 16)

                sp.wait_ge(stored, 32)

            @block.scalar
            def _(act):
                act.wait_ge(loaded, 64)

                def exps(i, u, a):
                    r = u % 2
                    if a == 0:
                        wait(act, combined, i, UN, -u if u < 2 else u - 1)
                    wait(act, maxed, i, H2, 2 * u + a + 1)
                    if u == 0:
                        act.activation(prob[r][a][:, 0:CTX], ps[:, 3 * a, 0:CTX], ACT.Exp, bias=nmax[:, r, a:a + 1],
                                       accum_out=esum[:, r, a:a + 1]).then_inc(exped, 1)
                    else:
                        act.activation(prob[r][a][:].rearrange("p (b n) -> p b n", b=3), ps[:, 3 * a:3 * a + 3, 0:CW],
                                       ACT.Exp, bias=nmax[:, r, a:a + 1], accum_out=esum[:, r, a:a + 1]).then_inc(exped, 1)

                def out_of_psum(i, u, r):
                    if u == 0:
                        if r == 0:
                            wait(act, turned, i, ROUNDS, 1)
                            wait(act, pv_done, i, 3, -2)
                            act.activation(at_ctx[:], ps[:, 6, 0:QB], ACT.Copy).then_inc(at_out, 1)
                        return
                    g, j = (u - 1) // GROUP, (u - 1) % GROUP
                    wait(act, turned, i, ROUNDS, 1 + 3 * (u - 1) + r + 1)
                    if j == 0 and r == 0:
                        wait(act, pv_done, i, 3, g + 2 - 3)
                    act.activation(at_buf[g][:, 3 * r:3 * r + 3, j * QB:(j + 1) * QB],
                                   ps[:, 6 + (3 * (u - 1) + r + 1) % 2, 0:3 * QB].rearrange("p (b n) -> p b n", b=3), ACT.Copy).then_inc(at_out, 1)

                def body(i):
                    wait(act, v_turned, i, 1, 0)
                    act.activation(v_head[:], tile(i + V0, slice(0, T)), ACT.Copy).then_inc(v_copied, 1)
                    wait(act, pv_done, i, 3, 0)
                    act.activation(v_tok[:, NT], cv[:, bass.ds(i, 1)].rearrange("p o t -> p (o t)"), ACT.Copy).then_inc(v_out, 1)
                    wait(act, v_turned, i, 1, 1)
                    for r in range(3):
                        act.activation(v_tok[:, 3 * r:3 * r + 3].rearrange("p b n -> p (b n)"), ps[:, 4 + r, 0:3 * P],
                                       ACT.Copy).then_inc(v_out, 1)
                    wait(act, scored, i, H2, 0)
                    wait(act, roped, i, 2, 1)
                    act.activation(q_hi[:], q_f[:], ACT.Copy).then_inc(qk_high, 1)
                    wait(act, roped, i, 2, 2)
                    act.activation(k_hi[:], k_f[:], ACT.Copy).then_inc(qk_high, 1)
                    for u in range(UN):
                        exps(i, u, 0)
                        exps(i, u, 1)
                        for r in range(3 if u >= 1 else 0):
                            out_of_psum(i, u - 1, r)
                    for r in range(3):
                        out_of_psum(i, UN - 1, r)
                peeled(act, body, HEADS)

            @block.vector
            def _(dve):
                dve.wait_ge(loaded, 64)

                def rope(i, n, dst, src, scale):
                    wait(dve, rotated, i, 2, n + 1)
                    wait(dve, roped, i, 2, n)
                    dve.scalar_tensor_tensor(out=rot_cos[:], in0=src(lat), scalar=scale, in1=cos[:],
                                             op0=ALU.mult, op1=ALU.mult).then_inc(rope_part, 1)
                    dve.scalar_tensor_tensor(out=rot_sin[:].rearrange("p (b n) -> p b n", b=2), in0=ps[:, 2 * n:2 * n + 2],
                                             scalar=scale, in1=sin[:].rearrange("p (b n) -> p b n", b=2),
                                             op0=ALU.mult, op1=ALU.mult).then_inc(rope_part, 1)
                    wait(dve, qk_low, i, 2, n + 1 - 2)
                    dve.tensor_scalar(dst[:, 0:CTX], src(slice(0, CTX)), scale, None, ALU.mult)
                    if n == 1:
                        dve.tensor_copy(dst[:, T:KALL], ck[:, bass.ds(i, 1)].rearrange("p o t -> p (o t)"))
                    wait(dve, rope_part, i, 4, 2 * n + 2)
                    dve.tensor_tensor(dst[:, CTX:T], rot_cos[:], rot_sin[:], ALU.add).then_inc(roped, 1)

                def minus_max(i, u, a):
                    r = u % 2
                    wait(dve, scored, i, H2, 2 * u + a + 1)
                    if a == 0:
                        wait(dve, exped, i, H2, 2 * (u - 1))
                    src = ps[:, 3 * a, 0:CTX] if u == 0 else ps[:, 3 * a:3 * a + 3, 0:CW]
                    dve.tensor_reduce(nmax[:, r, a:a + 1], src, AX_X if u == 0 else mybir.AxisListType.XY, ALU.max,
                                      negate=True).then_inc(maxed, 1)

                def combine(i, u):
                    r = u % 2
                    n = CTX if u == 0 else T
                    wait(dve, exped, i, H2, 2 * u + 2)
                    dve.reciprocal(rinv[:, r], esum[:, r]).then_inc(weighed, 1)
                    wait(dve, weighed, i, 3 * UN, 3 * u + 1)
                    dve.tensor_scalar(w1[:, r:r + 1], rinv[:, r, 1:2], neglam[:, 0:1], None, ALU.mult).then_inc(weighed, 1)
                    wait(dve, weighed, i, 3 * UN, 3 * u + 2)
                    dve.tensor_scalar(prob[r][1][:, 0:n], prob[r][1][:, 0:n], w1[:, r:r + 1], None, ALU.mult).then_inc(weighed, 1)
                    wait(dve, weighed, i, 3 * UN, 3 * u + 3)
                    dve.scalar_tensor_tensor(out=prob[r][0][:, 0:n], in0=prob[r][0][:, 0:n], scalar=rinv[:, r, 0:1],
                                             in1=prob[r][1][:, 0:n], op0=ALU.mult, op1=ALU.add).then_inc(combined, 1)

                def take_o(i, g):
                    cols = slice(0, CTX) if g == 0 else slice(CTX + (g - 1) * 512, CTX + g * 512)
                    wait(dve, pv_done, i, 3, g + 1)
                    dve.tensor_scalar(tile(i + Q0, cols), ps[:, 7, 0:cols.stop - cols.start], 1.0, None, ALU.mult).then_inc(o_out, 1)

                def body(i):
                    rope(i, 0, q_f, lambda cols: tile(i + Q0, cols), DH ** -0.5)
                    rope(i, 1, k_f, lambda cols: tile(i + K0, cols), 1.0)
                    minus_max(i, 0, 0)
                    minus_max(i, 0, 1)
                    for u in range(UN):
                        if u + 1 < UN:
                            minus_max(i, u + 1, 0)
                        combine(i, u)
                        if u + 1 < UN:
                            minus_max(i, u + 1, 1)
                        if u == 1:
                            take_o(i, 0)
                        if u == 5:
                            take_o(i, 1)
                    take_o(i, 2)
                peeled(dve, body, HEADS)

            @block.gpsimd
            def _(pool):
                def body(i):
                    for n, (hi, lo, src) in enumerate(((q_hi, q_lo, q_f), (k_hi, k_lo, k_f))):
                        wait(pool, qk_high, i, 2, n + 1)
                        pool.tensor_tensor(lo[:], src[:], hi[:].bitcast(F32), ALU.subtract).then_inc(qk_low, 1)
                peeled(pool, body, HEADS)

            @block.tensor
            def _(pe):
                def scores(i, u):
                    q = slice(u * QB, (u + 1) * QB)
                    keys = [slice(0, CTX)] if u == 0 else [slice(CTX + c * CW, CTX + (c + 1) * CW) for c in range(NC)]
                    for a in range(2):
                        rows = slice(a * DH, (a + 1) * DH)
                        wait(pe, exped, i, H2, 2 * (u - 1) + a + 1)
                        for c, cols in enumerate(keys):
                            acc = ps[:, 3 * a + c, 0:cols.stop - cols.start]
                            pe.matmul(acc, q_hi[rows, q], k_hi[rows, cols], start=True, stop=False)
                            pe.matmul(acc, q_hi[rows, q], k_lo[rows, cols], start=False, stop=False)
                            mm = pe.matmul(acc, q_lo[rows, q], k_hi[rows, cols], start=False, stop=True)
                        mm.then_inc(scored, 1)

                def turning(i, u, outs):
                    for r in range(1 if u == 0 else 3):
                        n = 0 if u == 0 else 1 + 3 * (u - 1) + r
                        if r == 0:
                            wait(pe, combined, i, UN, u + 1)
                        wait(pe, at_out, i, ROUNDS, n - 1 if n else 0)
                        if n % 2:
                            wait(pe, o_out, i, 3, outs)
                        for b in range(1 if u == 0 else 3):
                            mm = pe.transpose(ps[:, 6 + n % 2, b * P:(b + 1) * P],
                                              prob[u % 2][0][:, (3 * r + b) * P:(3 * r + b + 1) * P], ident[:])
                        mm.then_inc(turned, 1)

                def values(i, g):
                    wait(pe, at_out, i, ROUNDS, 1 if g == 0 else 1 + 3 * GROUP * g)
                    wait(pe, v_out, i, 4, 4)
                    wait(pe, o_out, i, 3, g)
                    if g == 0:
                        pe.matmul(ps[:, 7, 0:CTX], v_tok[:, 0], at_ctx[:], start=True, stop=True).then_inc(pv_done, 1)
                        return
                    for kt in range(NT):
                        mm = pe.matmul(ps[:, 7], v_tok[:, kt + 1], at_buf[g - 1][:, kt], start=(kt == 0), stop=(kt == NT - 1))
                    mm.then_inc(pv_done, 1)

                def body(i):
                    wait(pe, exped, i, H2, 0)
                    wait(pe, v_copied, i, 1, 1)
                    wait(pe, at_out, i, ROUNDS, 0)
                    for n in range(2):
                        for b in range(2):
                            mm = pe.matmul(ps[:, 2 * n + b], rot_t[:], tile(i + (Q0, K0)[n], slice(CTX + b * 512, CTX + (b + 1) * 512)),
                                           start=True, stop=True)
                        mm.then_inc(rotated, 1)
                    for t in range(NT):
                        mm = pe.transpose(ps[:, 4 + t // 3, (t % 3) * P:(t % 3 + 1) * P], v_head[:, t * P:(t + 1) * P], ident[:])
                    mm.then_inc(v_turned, 1)
                    wait(pe, qk_low, i, 2, 2)
                    wait(pe, v_out, i, 4, 4)
                    outs = 0
                    scores(i, 0)
                    for u in range(1, UN):
                        scores(i, u)
                        if u in (2, 6):
                            values(i, outs)
                            outs += 1
                        turning(i, u - 1, outs)
                    turning(i, UN - 1, outs)
                    values(i, 2)
                peeled(pe, body, HEADS)

    def even_output(qkvu, w_off, mods):
        s, sem, ps, k = stage()
        with s:
            sq = [at(f"sq{k}_{j}", [P, T], F32, w_off + j * 4 * T) for j in range(2)]
            std = [at(f"std{k}_{j}", [P, T], F32, w_off + (2 + j) * 4 * T) for j in range(2)]
            rstd = at(f"rstd{k}", [P, T], F32, w_off + 16 * T)
            w_pool = at(f"w_pool{k}", [P, HEADS, P], F32, w_off + 20 * T)
            w_in, squared, averaged, rooted = sem("w_in"), sem("squared"), sem("averaged"), sem("rooted")
            inverted, ready, high, low = sem("inverted"), sem("ready"), sem("high"), sem("low")
            mixed, pooled = sem("mixed"), sem("pooled")
            mod_load, mod_multiply, mod_take = more_modulation(sem, k, ps, 6, w_off + 20 * T + 4 * HEADS * P, *mods)
            tri = lambda ap: ap.rearrange("p (b n) -> p b n", b=NC)
            block = s.enter_context(nc.Block())

            @block.sync
            def _(sp):
                sp.dma_start(w_pool[:], inp["w_pool"]).then_inc(w_in, 16)
                mod_load(sp)

            @block.tensor
            def _(pe):
                pe.wait_ge(w_in, 16)
                for h in range(HEADS):
                    if h >= 1:
                        pe.wait_ge(rooted, h)
                        pe.wait_ge(pooled, h)
                    for c in range(NC):
                        mm = pe.matmul(ps[:, 3 + c, 0:CW], w_pool[:, h], qkvu[:, U0 + h, cs[c]], start=True, stop=True)
                    mm.then_inc(mixed, 1)
                    pe.wait_ge(squared, h + 1)
                    for c in range(NC):
                        mm = pe.matmul(ps[:, c, 0:CW], ones[:], sq[h % 2][:, cs[c]], start=True, stop=True)
                    mm.then_inc(averaged, 1)
                    mod_multiply(pe, 2 * h, 2 * h + 2)
                mod_multiply(pe, 2 * HEADS, mods[1])

            @block.scalar
            def _(act):
                def square(h):
                    if h >= 2:
                        act.wait_ge(averaged, h - 1)
                    act.activation(sq[h % 2][:], qkvu[:, Q0 + h], ACT.Square).then_inc(squared, 1)
                square(0)
                for h in range(HEADS):
                    if h + 1 < HEADS:
                        square(h + 1)
                    act.wait_ge(averaged, h + 1)
                    if h >= 2:
                        act.wait_ge(inverted, h - 1)
                    act.activation(tri(std[h % 2][:]), ps[:, 0:NC, 0:CW], ACT.Sqrt, bias=eps[:], scale=1.0 / P).then_inc(rooted, 1)
                for n in range(2 * HEADS):
                    act.wait_ge(pooled if n % 2 else ready, n // 2 + 1)
                    src = qkvu[:, (U0 if n % 2 else Q0) + n // 2]
                    act.activation(hh[:, n // 2 + (n % 2) * HEADS], src, ACT.Copy).then_inc(high, 1)

            @block.vector
            def _(dve):
                for h in range(HEADS):
                    dve.wait_ge(rooted, h + 1)
                    if h >= 1:
                        dve.wait_ge(ready, h)
                    dve.reciprocal(rstd[:], std[h % 2][:]).then_inc(inverted, 1)
                    dve.wait_ge(inverted, h + 1)
                    dve.scalar_tensor_tensor(out=qkvu[:, Q0 + h], in0=qkvu[:, Q0 + h], scalar=subg[:, h:h + 1], in1=rstd[:],
                                             op0=ALU.mult, op1=ALU.mult).then_inc(ready, 1)
                    dve.wait_ge(mixed, h + 1)
                    dve.tensor_scalar(tri(qkvu[:, U0 + h]), ps[:, 3:3 + NC, 0:CW], pscale[:, h:h + 1], None,
                                      ALU.mult).then_inc(pooled, 1)
                mod_take(dve)

            @block.gpsimd
            def _(pool):
                for n in range(2 * HEADS):
                    pool.wait_ge(high, n + 1)
                    ft = n // 2 + (n % 2) * HEADS
                    pool.tensor_tensor(hl[:, ft], qkvu[:, (U0 if n % 2 else Q0) + n // 2], hh[:, ft].bitcast(F32), ALU.subtract).then_inc(low, 1)

    def gla(gd, o_all):
        s, sem, ps, k = stage()
        with s:
            o = HH0
            head = at(f"head{k}", [P, 6, T], F32, o)
            o += 24 * T
            v_tok = at(f"v_tok{k}", [P, NT, 2 * P], F32, o)
            o += 8 * NT * P
            state = [at(f"state{k}_{d}", [P, NCHUNK, 2 * P], F32, o + d * 8 * NCHUNK * P) for d in range(2)]
            o += 16 * NCHUNK * P
            assert o <= X0
            o = W0
            log_part = at(f"log_part{k}", [P, T], F32, o)
            gate = [at(f"gate{k}_{d}", [P, T], F32, o + (1 + d) * 4 * T) for d in range(2)]
            squares = at(f"squares{k}", [P, 2, T], F32, o + 4 * T)
            decay_sum = [at(f"decay_sum{k}_{d}", [P, T], F32, o + (3 + d) * 4 * T) for d in range(2)]
            q_t = [at(f"q_t{k}_{d}", [P, T], F32, o + (5 + d) * 4 * T) for d in range(2)]
            k_t = [at(f"k_t{k}_{d}", [P, T], F32, o + (7 + d) * 4 * T) for d in range(2)]
            k_end = [at(f"k_end{k}_{d}", [P, T], F32, o + (9 + d) * 4 * T) for d in range(2)]
            a_t = [at(f"a_t{k}_{d}", [P, NT, P], F32, o + (11 + d) * 4 * T) for d in range(2)]
            k_end_tok = [at(f"k_end_tok{k}_{d}", [P, NT, P], F32, o + (13 + d) * 4 * T) for d in range(2)]
            scan_mask = at(f"scan_mask{k}", [P, T], F32, o + 15 * 4 * T)
            o += 16 * 4 * T
            up = at(f"up{k}", [48, P], F32, o)
            decay = at(f"decay{k}", [P, 2, NCHUNK], F32, o + 4 * P)
            o += 4 * P + 192
            wm = at(f"wm{k}", [P, MOD_GLA, KT, P], F32, o)
            o += 4 * MOD_GLA * D
            assert o <= GD0, (o, GD0)
            std, rstd = log_part, decay_sum[0]

            mask_in, qk_in, v_in, r_in = sem("mask_in"), sem("qk_in"), sem("v_in"), sem("r_in")
            up_in, state_in, states_out = sem("up_in"), sem("state_in"), sem("states_out")
            v_turned, v_out = sem("v_turned"), sem("v_out")
            z_done, gate_act, gate_min, gate_sum, scanned = (sem("z_done"), sem("gate_act"), sem("gate_min"),
                                                             sem("gate_sum"), sem("scanned"))
            grown, shrunk, decayed, to_go, ended = (sem("grown"), sem("shrunk"), sem("decayed"), sem("to_go"),
                                                    sem("ended"))
            q_ready, k_ready, k_end_ready = sem("q_ready"), sem("k_ready"), sem("k_end_ready")
            k_end_turned, k_end_out = sem("k_end_turned"), sem("k_end_out")
            kv_done, stepped = sem("kv_done"), sem("stepped")
            a_done, a_out = sem("a_done"), sem("a_out")
            o_done, o_out, silu_r = sem("o_done"), sem("o_out"), sem("silu_r")
            squared, averaged, rooted, inverted, scaled, finished = (sem("squared"), sem("averaged"), sem("rooted"),
                                                                     sem("inverted"), sem("scaled"), sem("finished"))
            wm_in, wm_used, mod_taken = [sem(f"wm_in{j}") for j in range(MOD_GLA)], sem("wm_used"), sem("mod_taken")
            MOD0 = 12 * KT - HEADS * MOD_GLA
            NPAIR = NCHUNK // 2
            KVS = 2 * NPAIR
            OB = 5
            GROUP = [4, 4, 4, 4, 2]
            Z_BANKS, V_BANKS, O_BANK0 = (0, 1, 2), (0, 1, 2, 0, 1), 3
            KE_BANKS, A_BANKS, M_BANK0 = ((3, 4, 5), (6, 7, 2)), ((0, 1, 3), (7, 2, 0)), 4
            KV_BANKS = ((4, 5), (6, 3), (1, 7), (2, 0))
            pair_order = [list(range(NPAIR)), [0] + list(range(NPAIR - 1, 0, -1))]
            chunk_of = lambda ap: ap.rearrange("p (n c) -> p n c", c=GCH)
            last_of = lambda ap, d: chunk_of(ap)[:, :, GCH - 1:GCH] if d == 0 else chunk_of(ap)[:, :, 0:1]
            tri = lambda ap: ap.rearrange("p (b n) -> p b n", b=NC)

            updates, count, latest = [], 0, [0, 0]
            for n in range(KVS):
                d, q = n % 2, pair_order[n % 2][n // 2]
                first, second = (2 * q, 2 * q + 1) if d == 0 else (2 * q + 1, 2 * q)
                if n < 2:
                    todo = [(None, first, second), (second, second, first)]
                else:
                    todo = [(m, m, m + 1 if d == 0 else m - 1) for m in (first, second)
                            if 2 <= (m + 1 if d == 0 else m - 1) < NCHUNK]
                group = []
                for src, m, dst in todo:
                    group.append((d, src, m, dst, latest[d]))
                    count += 1
                    latest[d] = count
                updates.append(group)
            STEPS = count
            after = [sum(len(g) for g in updates[:n + 1]) for n in range(KVS)]
            block = s.enter_context(nc.Block())

            @block.sync
            def _(sp):
                def part(i, ahead, j):
                    return gla_dram[bass.ds(i * 6 + 6 * ahead + j, 2)].rearrange("m p t -> p m t")

                def load_qkv(i, ahead):
                    sp.dma_start(up[:], inp["w_up"][bass.ds(i + ahead, 1)].rearrange("o p n -> p (o n)")).then_inc(up_in, 16)
                    sp.dma_start(head[:, 0:2], part(i, ahead, 0)).then_inc(qk_in, 16)
                    sp.dma_start(head[:, 2:4], part(i, ahead, 2)).then_inc(v_in, 16)

                def load_states(i, ahead):
                    for d in range(2):
                        sp.dma_start(state[d][:, 2 if d == 0 else NCHUNK - 1],
                                     inp["state"][d, bass.ds(i + ahead, 1)].rearrange("o p n -> p (o n)")).then_inc(state_in, 16)

                def load_mod(i, ahead):
                    for j in range(MOD_GLA):
                        sp.dma_start(wm[:, j].rearrange("p k n -> p (k n)"),
                                     inp["w_mod"][bass.ds(i * MOD_GLA + MOD_GLA * ahead + MOD0 + j, 1)].rearrange("o p n -> p (o n)")
                                     ).then_inc(wm_in[j], 16)

                def body(i, last=False):
                    if not last:
                        wait(sp, a_done, i, 6, 6)
                        load_qkv(i, 1)
                    wait(sp, stepped, i, STEPS, after[1])
                    for d in range(2):
                        sp.dma_start(out["new_state"][d, bass.ds(i, 1)].rearrange("o p n -> p (o n)"),
                                     state[d][:, d]).then_inc(states_out, 16)
                    wait(sp, finished, i, 2, 0)
                    sp.dma_start(head[:, 4:6], part(i, 0, 4)).then_inc(r_in, 16)
                    if not last:
                        wait(sp, o_done, i, OB, OB)
                        load_states(i, 1)
                        wait(sp, wm_used, i, MOD_GLA, MOD_GLA)
                        load_mod(i, 1)
                sp.dma_start(scan_mask[:], inp["c_scan"]).then_inc(mask_in, 16)
                load_qkv(0, 0)
                load_states(0, 0)
                load_mod(0, 0)
                body(0)
                with sp.Fori(1, HEADS - 1) as i:
                    body(i)
                body(HEADS - 1, last=True)
                sp.wait_ge(states_out, 32 * HEADS)

            @block.scalar
            def _(act):
                def gates(i, ahead):
                    for d in range(2):
                        wait(act, z_done, i, 2, 2 * ahead + d + 1)
                        wait(act, gate_sum, i, 2, 2 * ahead + d)
                        if d == 0:
                            wait(act, inverted, i, 1, ahead - 1)
                        act.activation(tri(log_part[:]), ps[:, 0:NC, 0:CW], ACT.Abs,
                                       bias=bgate[:, d, bass.ds(i + ahead, 1)]).then_inc(gate_act, 1)
                        wait(act, gate_act, i, 6, 6 * ahead + 3 * d + 1)
                        act.activation(log_part[:], log_part[:], ACT.Exp, scale=-1.0).then_inc(gate_act, 1)
                        wait(act, gate_act, i, 6, 6 * ahead + 3 * d + 2)
                        act.activation(log_part[:], log_part[:], ACT.Ln, bias=ones[:, 0:1]).then_inc(gate_act, 1)
                        wait(act, scanned, i, 2, 2 * ahead + d + 1)
                        wait(act, a_done, i, 6, 6 * ahead + 3 * d - 3)
                        act.activation(k_t[d][:], decay_sum[d][:], ACT.Exp, scale=-1.0 / GATE_TEMP).then_inc(shrunk, 1)
                        wait(act, stepped, i, STEPS, STEPS * ahead)
                        act.activation(decay[:, d].unsqueeze(2), last_of(decay_sum[d][:], d), ACT.Exp,
                                       scale=1.0 / GATE_TEMP).then_inc(decayed, 1)
                        wait(act, to_go, i, 2, 2 * ahead + d + 1)
                        wait(act, k_end_turned, i, 6, 6 * ahead + 3 * d - 3)
                        act.activation(k_end[d][:], gate[d][:], ACT.Exp, scale=1.0 / GATE_TEMP).then_inc(ended, 1)

                def square(i, back):
                    wait(act, o_out, i, OB, OB * (1 - back))
                    act.activation(squares[:], o_all[:, bass.ds(i * 2 - 2 * back, 2)], ACT.Square).then_inc(squared, 1)

                def root(i, back):
                    wait(act, averaged, i, 1, 1 - back)
                    act.activation(tri(std[:]), ps[:, M_BANK0:M_BANK0 + NC, 0:CW], ACT.Sqrt, bias=eps[:],
                                   scale=1.0 / (2 * P)).then_inc(rooted, 1)
                    wait(act, r_in, i, 16, 16 * (1 - back))
                    act.activation(head[:, 4:6], head[:, 4:6], ACT.Silu).then_inc(silu_r, 1)

                def body(i, first=False, last=False):
                    wait(act, o_done, i, OB, 0)
                    for d in range(2):
                        act.activation(q_t[d][:], decay_sum[d][:], ACT.Exp, scale=1.0 / GATE_TEMP).then_inc(grown, 1)
                    flat, t0 = v_tok[:].rearrange("p n m -> p (n m)"), 0
                    for r, n in enumerate(GROUP):
                        wait(act, v_turned, i, OB, r + 1)
                        act.activation(flat[:, t0 * P:(t0 + n) * P], ps[:, V_BANKS[r], 0:n * P], ACT.Copy).then_inc(v_out, 1)
                        t0 += n
                    for d in range(2):
                        for b in range(3):
                            wait(act, k_end_turned, i, 6, 3 * d + b + 1)
                            act.activation(k_end_tok[d][:, 3 * b:3 * b + 3].rearrange("p n m -> p (n m)"),
                                           ps[:, KE_BANKS[d][b], 0:3 * P], ACT.Copy).then_inc(k_end_out, 1)
                        if d == 0 and not first:
                            square(i, 1)
                    if not first:
                        root(i, 1)
                    if not last:
                        gates(i, 1)
                gates(0, 0)
                body(0, first=True)
                with act.Fori(1, HEADS - 1) as i:
                    body(i)
                body(HEADS - 1, last=True)
                square(HEADS - 1, 0)
                root(HEADS - 1, 0)

            @block.vector
            def _(dve):
                dve.wait_ge(mask_in, 16)

                def gates(i, ahead, d):
                    wait(dve, gate_act, i, 6, 6 * ahead + 3 * d + 1)
                    wait(dve, ended, i, 2, 2 * ahead + d - 1)
                    if d == 0:
                        wait(dve, averaged, i, 1, ahead - 1)
                    dve.tensor_scalar(tri(gate[d][:]), ps[:, 0:NC, 0:CW], bgate[:, d, bass.ds(i + ahead, 1)], 0.0,
                                      ALU.add, ALU.min).then_inc(gate_min, 1)
                    wait(dve, gate_act, i, 6, 6 * ahead + 3 * d + 3)
                    wait(dve, gate_min, i, 2, 2 * ahead + d + 1)
                    dve.tensor_tensor(gate[d][:], gate[d][:], log_part[:], ALU.subtract).then_inc(gate_sum, 1)
                    wait(dve, gate_sum, i, 2, 2 * ahead + d + 1)
                    wait(dve, grown, i, 2, 2 * ahead + d - 1)
                    if d == 0:
                        wait(dve, scaled, i, 1, ahead - 1)
                    src, dst = (gate[d][:], decay_sum[d][:]) if d == 0 else (gate[d][:, ::-1], decay_sum[d][:, ::-1])
                    dve.tensor_tensor_scan(dst, scan_mask[:], src, 0.0, ALU.mult, ALU.add).then_inc(scanned, 1)
                    wait(dve, scanned, i, 2, 2 * ahead + d + 1)
                    dve.tensor_tensor(chunk_of(gate[d][:]), last_of(decay_sum[d][:], d).broadcast_to([P, NCHUNK, GCH]),
                                      chunk_of(decay_sum[d][:]), ALU.subtract).then_inc(to_go, 1)

                def take_mod(i, back):
                    wait(dve, wm_used, i, MOD_GLA, MOD_GLA * (1 - back))
                    m0 = i * MOD_GLA + (MOD0 - MOD_GLA * back)
                    dve.tensor_tensor(mod_flat[:, bass.ds(m0, MOD_GLA)],
                                      ps[:, 2, 0:2 * MOD_GLA].rearrange("p (m v) -> p m v", v=2),
                                      bmod_flat[:, bass.ds(m0, MOD_GLA)].unsqueeze(2).broadcast_to([P, MOD_GLA, 2]),
                                      ALU.add).then_inc(mod_taken, 1)

                def invert(i, back):
                    wait(dve, rooted, i, 1, 1 - back)
                    dve.reciprocal(rstd[:], std[:]).then_inc(inverted, 1)

                def finish(i, back):
                    wait(dve, scaled, i, 1, 1 - back)
                    for j in range(2):
                        o_j = o_all[:, bass.ds(i * 2 - 2 * back + j, 1)].rearrange("p o t -> p (o t)")
                        dve.scalar_tensor_tensor(out=o_j, in0=o_j, scalar=vnorm[:, bass.ds(i * 2 - 2 * back + j, 1)],
                                                 in1=head[:, 4 + j], op0=ALU.mult, op1=ALU.mult).then_inc(finished, 1)

                def step(i, n):
                    wait(dve, kv_done, i, KVS, n + 1)
                    for e, (d, src, chunk, dst, before) in enumerate(updates[n]):
                        kv = ps[:, KV_BANKS[n % 4][chunk % 2], 0:2 * P]
                        if src is None:
                            if d == 0:
                                wait(dve, states_out, i, 32, 0)
                            dve.tensor_scalar(state[d][:, dst], kv, 1.0, None, ALU.mult).then_inc(stepped, 1)
                        else:
                            if before:
                                wait(dve, stepped, i, STEPS, before)
                            if n == 2 and e == 0:
                                wait(dve, state_in, i, 32, 32)
                            dve.scalar_tensor_tensor(out=state[d][:, dst], in0=state[d][:, src], scalar=decay[:, d, chunk:chunk + 1],
                                                     in1=kv, op0=ALU.mult, op1=ALU.add).then_inc(stepped, 1)

                def outputs(i, a, b):
                    for n in range(a, b):
                        w = GROUP[n] * P
                        wait(dve, o_done, i, OB, n + 1)
                        flat = o_all[:, bass.ds(i * 2, 2)].rearrange("p m t -> p (m t)")
                        dve.tensor_scalar(flat[:, 512 * n:512 * n + w], ps[:, O_BANK0 + n, 0:w], 1.0, None, ALU.mult).then_inc(o_out, 1)

                def body(i, first=False, last=False):
                    wait(dve, qk_in, i, 16, 16)
                    for d in range(2):
                        wait(dve, grown, i, 2, d + 1)
                        dve.scalar_tensor_tensor(out=q_t[d][:], in0=head[:, 0], scalar=DK_SCALE, in1=q_t[d][:],
                                                 op0=ALU.mult, op1=ALU.mult).then_inc(q_ready, 1)
                    if not first:
                        take_mod(i, 1)
                    for d in range(2):
                        for b in range(3):
                            wait(dve, a_done, i, 6, 3 * d + b + 1)
                            dve.tensor_tensor(a_t[d][:, 3 * b:3 * b + 3],
                                              ps[:, A_BANKS[d][b], 0:3 * P].rearrange("p (b n) -> p b n", b=3),
                                              mask_gla[:, d:d + 1].broadcast_to([P, 3, P]), ALU.mult).then_inc(a_out, 1)
                    wait(dve, decayed, i, 2, 2)
                    for n in range(KVS):
                        step(i, n)
                        if n == 3 and not first:
                            invert(i, 1)
                        if n == 12 and not first:
                            finish(i, 1)
                    if not last:
                        gates(i, 1, 0)
                    outputs(i, 0, 1)
                    if not last:
                        gates(i, 1, 1)
                    outputs(i, 1, OB)
                for d in range(2):
                    gates(0, 0, d)
                body(0, first=True)
                with dve.Fori(1, HEADS - 1) as i:
                    body(i)
                body(HEADS - 1, last=True)
                take_mod(HEADS - 1, 0)
                invert(HEADS - 1, 0)
                finish(HEADS - 1, 0)
                dve.wait_ge(mod_taken, HEADS)
                scale_columns(dve, 3)

            @block.gpsimd
            def _(pool):
                def keys(i, ahead):
                    wait(pool, qk_in, i, 16, 16 * ahead + 16)
                    for d in range(2):
                        wait(pool, shrunk, i, 2, 2 * ahead + d + 1)
                        pool.tensor_tensor(k_t[d][:], head[:, 1], k_t[d][:], ALU.mult).then_inc(k_ready, 1)
                        wait(pool, ended, i, 2, 2 * ahead + d + 1)
                        pool.tensor_tensor(k_end[d][:], head[:, 1], k_end[d][:], ALU.mult).then_inc(k_end_ready, 1)

                def rescale(i, back):
                    wait(pool, silu_r, i, 1, 1 - back)
                    wait(pool, inverted, i, 1, 1 - back)
                    pool.tensor_tensor(head[:, 4:6], head[:, 4:6], rstd[:].unsqueeze(1).broadcast_to([P, 2, T]),
                                       ALU.mult).then_inc(scaled, 1)

                def body(i, first=False, last=False):
                    if not first:
                        rescale(i, 1)
                    if not last:
                        keys(i, 1)
                keys(0, 0)
                body(0, first=True)
                with pool.Fori(1, HEADS - 1) as i:
                    body(i)
                body(HEADS - 1, last=True)
                rescale(HEADS - 1, 0)

            @block.tensor
            def _(pe):
                def gate_inputs(i, ahead, d):
                    rows = slice(32 * d, 32 * d + 16)
                    for c in range(NC):
                        mm = pe.matmul(ps[:, Z_BANKS[c], 0:CW], up[rows, :], gd[rows, cs[c]], start=True, stop=True)
                    mm.then_inc(z_done, 1)

                def scores(i, d):
                    wait(pe, q_ready, i, 2, d + 1)
                    wait(pe, k_ready, i, 2, d + 1)
                    for t in range(NT):
                        if t == 6 and d == 1:
                            wait(pe, a_out, i, 6, 1)
                        tok = slice(t * P, (t + 1) * P)
                        mm = pe.matmul(ps[:, A_BANKS[d][t // 3], (t % 3) * P:(t % 3 + 1) * P], k_t[d][:, tok], q_t[d][:, tok],
                                       start=True, stop=True)
                        if t % 3 == 2:
                            mm.then_inc(a_done, 1)

                def mean(i, back):
                    wait(pe, squared, i, 1, 1 - back)
                    for c in range(NC):
                        for j in range(2):
                            mm = pe.matmul(ps[:, M_BANK0 + c, 0:CW], ones[:], squares[:, j, cs[c]], start=(j == 0), stop=(j == 1))
                    mm.then_inc(averaged, 1)

                def outputs(i, a, b):
                    for n in range(a, b):
                        for m in range(GROUP[n]):
                            j, t = divmod(4 * n + m, NT)
                            dv, bank, c0 = slice(j * P, (j + 1) * P), O_BANK0 + n, m * P
                            pe.matmul(ps[:, bank, c0:c0 + P], v_tok[:, t, dv], a_t[0][:, t], start=True, stop=False,
                                      skip_group_check=True)
                            inter = [(d, c) for d in range(2) for c in (2 * t, 2 * t + 1) if (d, c) not in ((0, 0), (1, 1))]
                            for d, c in inter:
                                c1 = c0 + (c % 2) * GCH
                                pe.matmul(ps[:, bank, c1:c1 + GCH], state[d][:, c, dv], q_t[d][:, c * GCH:(c + 1) * GCH],
                                          start=False, stop=False, skip_group_check=True)
                            mm = pe.matmul(ps[:, bank, c0:c0 + P], v_tok[:, t, dv], a_t[1][:, t], start=False, stop=True,
                                           skip_group_check=True)
                        mm.then_inc(o_done, 1)

                def body(i, first=False, last=False):
                    wait(pe, v_in, i, 16, 16)
                    wait(pe, gate_min, i, 2, 2)
                    n = 0
                    for r, tiles in enumerate(GROUP):
                        if r == 2:
                            wait(pe, mod_taken, i, 1, 0)
                        if r >= 3:
                            wait(pe, v_out, i, OB, r - 2)
                        for m in range(tiles):
                            t, j = divmod(n, 2)
                            n += 1
                            mm = pe.transpose(ps[:, V_BANKS[r], m * P:(m + 1) * P], head[:, 2 + j, t * P:(t + 1) * P], ident[:])
                        mm.then_inc(v_turned, 1)
                    for d in range(2):
                        wait(pe, k_end_ready, i, 2, d + 1)
                        if d == 0:
                            wait(pe, o_out, i, OB, 0)
                        for t in range(NT):
                            if d == 1 and t == 6:
                                wait(pe, v_out, i, OB, 3)
                            mm = pe.transpose(ps[:, KE_BANKS[d][t // 3], (t % 3) * P:(t % 3 + 1) * P],
                                              k_end[d][:, t * P:(t + 1) * P], ident[:])
                            if t % 3 == 2:
                                mm.then_inc(k_end_turned, 1)
                    wait(pe, v_out, i, OB, OB)
                    wait(pe, k_end_out, i, 6, 1)
                    scores(i, 0)
                    wait(pe, k_end_out, i, 6, 4)
                    if not first:
                        mean(i, 1)
                    wait(pe, k_end_out, i, 6, 6)
                    scores(i, 1)
                    for n in range(KVS):
                        if n == 0:
                            wait(pe, rooted, i, 1, 0)
                        elif n < 4:
                            wait(pe, a_out, i, 6, (0, 3, 4, 6)[n])
                        else:
                            wait(pe, stepped, i, STEPS, after[n - 4])
                        d, q = n % 2, pair_order[n % 2][n // 2]
                        for e in range(2):
                            rows = slice(e * GCH, (e + 1) * GCH)
                            mm = pe.matmul(ps[:, KV_BANKS[n % 4][e], 0:2 * P], k_end_tok[d][rows, q, :], v_tok[rows, q, :],
                                           start=True, stop=True)
                        mm.then_inc(kv_done, 1)
                    if not last:
                        wait(pe, up_in, i, 16, 32)
                        wait(pe, stepped, i, STEPS, after[KVS - 3])
                        gate_inputs(i, 1, 0)
                    wait(pe, stepped, i, STEPS, STEPS)
                    outputs(i, 0, 1)
                    if not last:
                        wait(pe, gate_min, i, 2, 3)
                        gate_inputs(i, 1, 1)
                    outputs(i, 1, OB)
                    if not last:
                        wait(pe, gate_min, i, 2, 4)
                    for j in range(MOD_GLA):
                        wait(pe, wm_in[j], i, 16, 16)
                        for kk in range(KT):
                            mm = pe.matmul(ps[:, 2, 2 * j:2 * j + 2], wm[:, j, kk], silu_c[:, kk],
                                           start=(kk == 0), stop=(kk == KT - 1))
                        mm.then_inc(wm_used, 1)
                pe.wait_ge(up_in, 16)
                gate_inputs(0, 0, 0)
                pe.wait_ge(gate_min, 1)
                gate_inputs(0, 0, 1)
                body(0, first=True)
                with pe.Fori(1, HEADS - 1) as i:
                    body(i)
                body(HEADS - 1, last=True)
                mean(HEADS - 1, 0)

    def split(src):
        s, sem, ps, k = stage()
        with s:
            high = sem("high")
            block = s.enter_context(nc.Block())

            @block.scalar
            def _(act):
                for ft in range(KT):
                    act.activation(hh[:, ft], src[:, ft], ACT.Copy).then_inc(high, 1)

            @block.vector
            def _(dve):
                for ft in range(KT):
                    dve.wait_ge(high, ft + 1)
                    dve.tensor_tensor(hl[:, ft], src[:, ft], hh[:, ft].bitcast(F32), ALU.subtract)

    QK0 = X0
    WQ = X0 + 4 * EVEN_TILES * T
    qkvu = at("qkvu", [P, EVEN_TILES, T], F32, QK0)

    o_all = at("o_all", [P, KT, T], F32, X0)
    gd = at("gd", [DH, T], F32, GD0)

    modulation()
    norm(0, layer=0, shift=SHIFT1, load=inp["x"], mods=(2 * KT, 2 * KT))
    projection(inp["w_in_even"], EVEN_TILES, WQ, result=qkvu, pooling=True)
    attention(qkvu, WQ)
    even_output(qkvu, WQ, mods=(4 * KT, 2 * KT, (1,)))
    projection(inp["w_out_even"], KT, W0, residual=(inp["x"], 0, GATE1))
    norm(1, layer=0, shift=SHIFT2, mods=(6 * KT, 2 * KT, (2,)))
    ffn(0)
    recycle()
    norm(2, layer=1, shift=SHIFT1, spill=True, mods=(8 * KT, 2 * KT))
    projection(inp["w_in_odd"], ODD_TILES, W0, spill=gla_dram, extra=(inp["w_gd"], DH, gd))
    gla(gd, o_all)
    split(o_all)
    projection(inp["w_out_odd"], KT, W0, residual=(xs_dram, 1, GATE1))
    norm(3, layer=1, shift=SHIFT2)
    ffn(1)
    norm(4, final=out["y"])

    ctx.close()


def layout(a):
    import numpy as np

    def cols(v):
        v = np.asarray(v)
        return np.moveaxis(v.reshape(*v.shape[:-1], v.shape[-1] // P, P), -1, 0)

    def tiles(w):
        kk, n = w.shape
        return w.reshape(kk // P, P, n // P, P).transpose(2, 1, 0, 3).reshape(n // P, P, kk)

    f = lambda v: np.ascontiguousarray(v, dtype=np.float32)
    x_t = np.concatenate([a["x_prompt"][0], a["x_sample"][0]], axis=0)
    r = {"x": x_t.T.reshape(KT, P, T).transpose(1, 0, 2)}
    r["cond"] = np.moveaxis(cols(np.stack([a["c_ctx"], a["c"][0]])), 1, 2)
    r["w_mod"] = np.concatenate([tiles(a["w_mod"][l]) for l in range(2)])
    r["b_mod"] = cols(a["b_mod"])
    r["gnorm"] = cols(np.stack([a["norm1_g"][0], a["norm2_g"][0], a["norm1_g"][1], a["norm2_g"][1], a["final_g"]]))
    r["lam"] = np.broadcast_to(a["lam_params"], (P, 4, DH))
    r["subln"] = cols(a["subln_g"][0])
    r["pscale"] = cols(a["pool_scale"][0])
    r["bgate"] = cols(a["b_gate"][0])
    r["gla_norm"] = cols(a["gla_norm_g"][0])
    r["w_in_even"] = np.roll(tiles(a["w_in_even"][0]), HEADS, axis=0)
    r["w_out_even"] = tiles(a["w_out_even"][0])
    w = a["w_in_odd"][0]
    order = []
    for h in range(HEADS):
        order += [h, 4 + h, 8 + 2 * h, 9 + 2 * h, 16 + 2 * h, 17 + 2 * h]
    r["w_in_odd"] = tiles(w[:, :ODD_TILES * P])[order]
    gd = np.zeros((D, DH), np.float32)
    gd[:, 0:16], gd[:, 32:48] = w[:, ODD_TILES * P:ODD_TILES * P + 16], w[:, ODD_TILES * P + 16:]
    r["w_gd"] = gd.reshape(KT, P, DH).transpose(1, 0, 2).reshape(P, KT * DH)
    up = np.zeros((HEADS, 48, P), np.float32)
    for d in range(2):
        up[:, 32 * d:32 * d + 16] = a["w_gate_up"][0, d].reshape(16, HEADS, P).transpose(1, 0, 2)
    r["w_up"] = up
    r["w_out_odd"] = tiles(a["w_out_odd"][0])
    r["w_pool"] = a["w_pool"][0].transpose(1, 0, 2)
    fin, fout = [], []
    for l in range(2):
        t = tiles(a["w_ffn_in"][l])
        n = HIDDEN // P
        fin.append(np.stack([t[:n], t[n:]], axis=2).reshape(n, P, 2 * D))
        fout.append(a["w_ffn_out"][l].reshape(FFN_PAIRS, 2, P, D).transpose(0, 2, 1, 3).reshape(FFN_PAIRS, P, 2 * D))
    r["w_ffn_in"], r["w_ffn_out"] = np.stack(fin), np.stack(fout)
    r["cache_k"] = a["cache_attn_k"][0, 0].reshape(CTX, HEADS, P).transpose(2, 1, 0)
    r["cache_v"] = a["cache_attn_v"][0, 0]
    r["state"] = a["state_gla"][0, 0]

    r["c_ident"] = np.eye(P)
    q = np.arange(P)
    rot = np.zeros((P, P))
    lower = q % 32 < 16
    rot[q[lower], q[lower] + 16] = -1.0
    rot[q[~lower], q[~lower] - 16] = 1.0
    r["c_rot"] = rot.T
    j, i = np.meshgrid(q, q, indexing="ij")
    same = j // GCH == i // GCH
    r["c_mask"] = np.stack([same & (j <= i), same & (j >= i)], axis=1)
    inv = (1.0 / (10000.0 ** (np.arange(0, 32, 2, dtype=np.float32) / np.float32(32)))).astype(np.float32)
    t = np.arange(LAT)
    place = np.where((q[:, None] // 32) % 2 == 0, t // 64, t % 64).astype(np.float32)
    ang = place * inv[q % 16][:, None]
    r["c_cos"], r["c_sin"] = np.cos(ang), np.sin(ang)
    e = np.ones((P, len(WINDOWS), 2, PAD), np.float32)
    for n, w in enumerate(WINDOWS):
        k = np.arange(PAD)
        e[:, n, 0] = w / np.minimum(w, k + w // 2)
        e[:, n, 1] = w / np.minimum(w, PAD - k + w // 2)
    r["c_edge"] = e
    scan = np.ones((P, T), np.float32)
    scan[:, ::GCH] = 0.0
    r["c_scan"] = scan
    return {n: f(v) for n, v in r.items()}


_OUTS = {"y": (P, KT, T), "new_k": (HEADS, P, CTX), "new_v": (HEADS, P, CTX), "new_state": (2, HEADS, P, 2 * P)}


def kernel(**inputs):
    import concourse.bacc as _bacc
    import numpy as _np
    from concourse.bass_utils import run_bass_kernel_spmd as _run

    nc = _bacc.Bacc("TRN2", target_bir_lowering=False, num_devices=1)
    arrays, inp, out = {}, {}, {}
    for name, v in layout({n: _np.asarray(v) for n, v in inputs.items()}).items():
        arrays[f"in_{name}_dram"] = v
        inp[name] = nc.dram_tensor(f"in_{name}_dram", v.shape, F32, kind="ExternalInput").ap()
    for name, shape in _OUTS.items():
        out[name] = nc.dram_tensor(f"out_{name}_dram", shape, F32, kind="ExternalOutput").ap()
    build(nc, inp, out)
    got = _run(nc, [arrays], core_ids=[0]).results[0]
    y = got["out_y_dram"].transpose(2, 1, 0).reshape(T, D)
    new_k = got["out_new_k_dram"].transpose(2, 0, 1).reshape(1, 1, CTX, HEADS, 2, DH)
    new_v = got["out_new_v_dram"].transpose(2, 0, 1).reshape(1, 1, CTX, HEADS, P)
    state = got["out_new_state_dram"].reshape(1, 1, 2, HEADS, P, 2 * P)
    return (y[None, :CTX], y[None, CTX:], new_k, new_v, state)
```

```python
from contextlib import ExitStack
from functools import partial

import concourse.bass as bass
from concourse import mybir

F32 = mybir.dt.float32
F32R = mybir.dt.float32r
ALU = mybir.AluOpType
ACT = mybir.ActivationFunctionType
AX_X = mybir.AxisListType.X

P = 128
D = 1024
KT = D // P
CTX = 128
LAT = 1024
T = CTX + LAT
NC = 3
CW = T // NC
EPS = 1e-6
HEADS = 4
HIDDEN = 2816
FFN_PAIRS = HIDDEN // (2 * P)
LAM_INIT = 0.2
DH = 64
WINDOWS = (2, 4, 8, 16)
GCH = 64
NCHUNK = T // GCH
NT = T // P
GATE_TEMP = 16.0
DK_SCALE = float(P) ** -0.5
SHIFT1, SCALE1, GATE1, SHIFT2, SCALE2, GATE2 = range(6)
PAD = 8
PADW = PAD + CTX + 2 * PAD + LAT + PAD
EVEN_TILES = 16
U0, Q0, K0, V0 = 0, 4, 8, 12
MOD_FIRST = 2 * KT
ODD_TILES = 24


def wait(eng, sem, i, per, n):
    if isinstance(i, int):
        if i * per + n > 0:
            eng.wait_ge(sem, i * per + n)
    else:
        eng.wait_ge(sem, i * per + n)


def peeled(eng, body, n):
    body(0)
    if n > 1:
        with eng.Fori(1, n) as i:
            body(i)


def build(nc, inp, out):
    base = (nc.sbuf_base + 63) // 64 * 64

    def at(name, shape, dtype, offset):
        return nc.alloc_sbuf_tensor_at(name, shape, dtype, offset=base + offset)

    XB = 4 * KT * T
    C0 = 6656
    HH0, HL0, X0, W0 = C0, C0 + XB, C0 + 2 * XB, C0 + 3 * XB
    END = nc.sbuf_usable_end - base
    GD0 = END // 32 * 32 - 4 * T

    ctx = ExitStack()

    pos = [0]

    def const(name, shape, dtype=F32):
        t = at(name, shape, dtype, pos[0])
        n = 4
        for s in shape[1:]:
            n *= s
        pos[0] += (n + 31) // 32 * 32
        assert pos[0] <= C0, pos[0]
        return t

    ident = const("ident", [P, P])
    ones = const("ones", [P, P])
    rot_t = const("rot_t", [P, P])
    mask_gla = const("mask_gla", [P, 2, P])
    cond = const("cond", [P, KT, 2])
    silu_c = const("silu_c", [P, KT, 2])
    bmod = const("bmod", [P, 2, 6 * KT])
    mod = const("mod", [P, 2, 6 * KT, 2])
    gnorm = const("gnorm", [P, 5, KT])
    amod = const("amod", [P, 4, KT, 2])
    eps = const("eps", [P, 1])
    lamp = const("lamp", [P, 4, DH])
    lamw = const("lamw", [P, 8])
    neglam = const("neglam", [P, 1])
    subg = const("subg", [P, HEADS])
    pscale = const("pscale", [P, HEADS])
    edge = const("edge", [P, len(WINDOWS), 2, PAD])
    bgate = const("bgate", [P, 2, HEADS])
    nbgate = const("nbgate", [P, 2, HEADS])
    vnorm = const("vnorm", [P, 2 * HEADS])

    hh = at("hh", [P, KT, T], F32R, HH0)
    hl = at("hl", [P, KT, T], F32R, HL0)
    hh_f32 = at("hh_f32", [P, KT, T], F32, HH0)
    hl_f32 = at("hl_f32", [P, KT, T], F32, HL0)
    x = at("x", [P, KT, T], F32, X0)

    xs_dram = nc.dram_tensor("x_spill", [P, KT, T], F32, kind="Internal").ap()
    gla_dram = nc.dram_tensor("gla_spill", [ODD_TILES, P, T], F32, kind="Internal").ap()

    nstage = [0]
    semaphores = []

    def stage():
        s = ExitStack()
        nstage[0] += 1
        k = nstage[0]
        psum = s.enter_context(nc.psum_tensor(f"ps{k}", [P, 8, 512], F32))

        def sem(name):
            semaphores.append(nc.alloc_semaphore(f"s{k}_{name}"))
            return semaphores[-1]
        return s, sem, psum, k

    def recycle():
        nc.clear_and_free_semaphores(semaphores)
        semaphores.clear()
        nc.all_engine_barrier()

    cs = [slice(c * CW, (c + 1) * CW) for c in range(NC)]
    pieces = [[(slice(0, CTX), 0), (slice(CTX, CW), 1)]] + [[(cs[c], 1)] for c in range(1, NC)]

    def scale_columns(dve, n):
        kind = (SCALE1, SCALE2)[n % 2]
        dve.scalar_tensor_tensor(out=amod[:, n], in0=mod[:, n // 2, kind * KT:(kind + 1) * KT, :], scalar=1.0,
                                 in1=gnorm[:, n].unsqueeze(2).broadcast_to([P, KT, 2]), op0=ALU.add, op1=ALU.mult)

    mod_flat = mod[:].rearrange("p l m v -> p (l m) v")
    bmod_flat = bmod[:].rearrange("p l m -> p (l m)")

    class ModulationBeside:
        SEGS = 4

        def __init__(self, sem, k, ps, offset, m0, per_pair, scales=()):
            self.m0, self.per_pair, self.scales = m0, per_pair, scales
            self.wmt = [at(f"wmt{k}_{j}", [P, D], F32, offset + j * 4 * D) for j in range(2)]
            self.silu_row = at(f"silu_row{k}", [P, 2, D], F32, offset + 8 * D)
            self.part = at(f"mpart{k}", [P, 4, 2, self.SEGS], F32, offset + 16 * D)
            self.acc = at(f"macc{k}", [P, 4, 2], F32, offset + 16 * D + 128)
            assert per_pair <= 4 and offset + 16 * D + 160 <= END, (offset + 16 * D + 160, END)
            self.row_in, self.row_silu = sem("row_in"), sem("row_silu")
            self.wmt_in, self.wmt_used = [sem(f"wmt_in{j}") for j in range(2)], sem("wmt_used")
            self.mod_taken, self.summed_up = sem("mod_taken"), sem("summed_up")
            self.unused = ps[:, 6:8].rearrange("p (s b) n -> p s (b n)", s=1)

        def load_row(self, sp):
            sp.dma_start(self.silu_row[:], inp["cond_row"]).then_inc(self.row_in, 16)

        def silu(self, act):
            act.wait_ge(self.row_in, 16)
            act.activation(self.silu_row[:], self.silu_row[:], ACT.Silu).then_inc(self.row_silu, 1)

        def load(self, sp, i):
            n = self.per_pair
            for t in range(n):
                wait(sp, self.wmt_used, i, 2 * n, 2 * (t - 1))
                sp.dma_start(self.wmt[t % 2][:], inp["w_mod_t"][bass.ds(i * n + self.m0 + t, 1)].rearrange("o p n -> p (o n)")
                             ).then_inc(self.wmt_in[t % 2], 16)

        def multiply(self, dve, i, t):
            n = self.per_pair
            wait(dve, self.wmt_in[t % 2], i, 16 * (n // 2), 16 * (t // 2 + 1))
            if isinstance(i, int) and t == 0:
                dve.wait_ge(self.row_silu, 1)
            if t == 0:
                wait(dve, self.mod_taken, i, 1, 0)
            w = D // self.SEGS
            for v in range(2):
                wait(dve, self.wmt_used, i, 2 * n, 2 * t + v)
                for g in range(self.SEGS):
                    seg = slice(g * w, (g + 1) * w)
                    last = dve.scalar_tensor_tensor(out=self.unused[:, 0, seg], in0=self.wmt[t % 2][:, seg], scalar=1.0,
                                                    in1=self.silu_row[:, v, seg], op0=ALU.mult, op1=ALU.mult,
                                                    accum_out=self.part[:, t, v, g:g + 1])
                last.then_inc(self.wmt_used, 1)

        def take(self, dve, i):
            n = self.per_pair
            wait(dve, self.wmt_used, i, 2 * n, 2 * n)
            dve.tensor_reduce(self.acc[:, 0:n], self.part[:, 0:n], AX_X, ALU.add).then_inc(self.summed_up, 1)
            wait(dve, self.summed_up, i, 1, 1)
            dve.tensor_tensor(mod_flat[:, bass.ds(i * n + self.m0, n)], self.acc[:, 0:n],
                              bmod_flat[:, bass.ds(i * n + self.m0, n)].unsqueeze(2).broadcast_to([P, n, 2]),
                              ALU.add).then_inc(self.mod_taken, 1)

        def finish(self, dve, pairs):
            if self.scales:
                dve.wait_ge(self.mod_taken, pairs)
            for n in self.scales:
                scale_columns(dve, n)

    def modulation():
        s, sem, ps, k = stage()
        SL = 6
        NM = 2 * SL
        with s:
            wm = at("wm", [P, SL, KT, P], F32, W0)
            consts_in = sem("consts_in")
            w_in = [sem(f"w_in{j}") for j in range(SL)]
            w_used = sem("w_used")
            silu_done = sem("silu_done")
            mod_done = sem("mod_done")
            dve_step = sem("dve_step")
            lam_exp, x_in = sem("lam_exp"), sem("x_in")
            small = [(ident, "c_ident"), (rot_t, "c_rot"), (mask_gla, "c_mask"), (cond, "cond"), (bmod, "b_mod"),
                     (gnorm, "gnorm"), (lamp, "lam"), (subg, "subln"), (pscale, "pscale"), (edge, "c_edge"),
                     (bgate, "bgate"), (vnorm, "gla_norm")]
            beside = ModulationBeside(sem, k, ps, W0 + 4 * SL * D, NM, MOD_FIRST - NM)
            block = s.enter_context(nc.Block())

            @block.scalar
            def _(act):
                beside.load_row(act)
                for t, name in small:
                    act.dma_start(t[:], inp[name]).then_inc(consts_in, 16)
                act.wait_ge(consts_in, 16 * len(small))
                act.activation(silu_c[:], cond[:], ACT.Silu).then_inc(silu_done, 1)
                beside.silu(act)
                act.wait_ge(dve_step, 2)
                act.activation(lamw[:, 2:4], lamw[:, 0:2], ACT.Exp).then_inc(lam_exp, 1)
                beside.load(act, 0)
                act.dma_start(x[:], inp["x"]).then_inc(x_in, 16)
                act.wait_ge(x_in, 16)

            @block.sync
            def _(sp):
                def body(i):
                    for j in range(SL):
                        wait(sp, w_used, i, SL, j + 1 - SL)
                        m = i * SL + j
                        src = inp["w_mod"][m] if isinstance(m, int) else inp["w_mod"][bass.ds(m, 1)].rearrange("o p n -> p (o n)")
                        sp.dma_start(wm[:, j].rearrange("p k n -> p (k n)"), src).then_inc(w_in[j], 16)
                peeled(sp, body, NM // SL)

            @block.tensor
            def _(pe):
                pe.wait_ge(silu_done, 1)

                def body(i):
                    for j in range(SL):
                        wait(pe, w_in[j], i, 16, 16)
                        for kk in range(KT):
                            mm = pe.matmul(ps[:, 0, bass.ds((i * SL + j) * 2, 2)], wm[:, j, kk, :], silu_c[:, kk, :],
                                           start=(kk == 0), stop=(kk == KT - 1))
                        mm.then_inc(w_used, 1)
                peeled(pe, body, NM // SL)

            @block.gpsimd
            def _(pool):
                pool.memset(ones[:], 1.0)
                pool.memset(eps[:], EPS)

            @block.vector
            def _(dve):
                dve.wait_ge(consts_in, 16 * len(small))
                dve.tensor_tensor(lamp[:, 0:3:2], lamp[:, 0:3:2], lamp[:, 1:4:2], ALU.mult).then_inc(dve_step, 1)
                dve.wait_ge(dve_step, 1)
                dve.tensor_reduce(lamw[:, 0:2], lamp[:, 0:3:2], AX_X, ALU.add).then_inc(dve_step, 1)
                dve.wait_ge(lam_exp, 1)
                dve.tensor_tensor(lamw[:, 4:5], lamw[:, 3:4], lamw[:, 2:3], ALU.subtract).then_inc(dve_step, 1)
                dve.wait_ge(dve_step, 3)
                dve.tensor_scalar(neglam[:], lamw[:, 4:5], -LAM_INIT, None, ALU.add)
                dve.tensor_scalar(subg[:], subg[:], 1.0 - LAM_INIT, None, ALU.mult)
                for t in range(beside.per_pair):
                    beside.multiply(dve, 0, t)
                beside.take(dve, 0)
                dve.wait_ge(w_used, NM)
                dve.tensor_tensor(mod[:, 0, 0:NM], ps[:, 0, 0:2 * NM].rearrange("p (m v) -> p m v", v=2),
                                  bmod[:, 0, 0:NM].unsqueeze(2).broadcast_to([P, NM, 2]), ALU.add).then_inc(mod_done, 1)
                dve.wait_ge(mod_done, 1)
                dve.wait_ge(beside.mod_taken, 1)
                scale_columns(dve, 0)

    HALF = KT // 2
    halves = [slice(0, HALF), slice(HALF, KT)]

    class Norm:
        order = range(KT)
        bytes = 4 * T

        def __init__(self, sem, k, ps, offset, n, layer=None, shift=None, spill=False, final=None):
            self.n, self.layer, self.shift, self.spill, self.final = n, layer, shift, spill, final
            self.stat = at(f"stat{k}", [P, NC, CW], F32, offset)
            self.bank = [ps[:, 6 + c % 2, 0:CW] for c in range(NC)]
            self.sq = [hh_f32[:, :, cs[c]] for c in range(NC)]
            self.xn = [hl_f32[:, :, cs[c]] for c in range(NC)]
            self.squared = [sem(f"squared{c}") for c in range(NC)]
            self.summed, self.averaged, self.rooted = sem("summed"), sem("averaged"), sem("rooted")
            self.scaled, self.modulated, self.high, self.low = sem("scaled"), sem("modulated"), sem("high"), sem("low")
            self.logged, self.stored, self.y_out = sem("logged"), sem("stored"), sem("y_out")

        def loads(self, sp):
            if self.spill:
                sp.dma_start(xs_dram, x[:]).then_inc(self.stored, 16)

        def stores(self, sp):
            if self.final is not None:
                for c in range(NC):
                    sp.wait_ge(self.modulated, 2 * c + 2)
                    sp.dma_start(self.final[:, :, cs[c]], self.xn[c]).then_inc(self.y_out, 16)
                sp.wait_ge(self.y_out, 16 * NC)
            if self.spill:
                sp.wait_ge(self.stored, 16)

        def act_early(self, act):
            for c in range(2):
                act.activation(self.sq[c], x[:, :, cs[c]], ACT.Square).then_inc(self.squared[c], 1)

        def pool_early(self, pool):
            pool.tensor_tensor(self.sq[2], x[:, :, cs[2]], x[:, :, cs[2]], ALU.mult).then_inc(self.squared[2], 1)

        def act_late(self, act):
            n = self.n

            def root(c):
                act.wait_ge(self.averaged, c + 1)
                act.activation(self.stat[:, c], self.bank[c], ACT.Ln, bias=eps[:], scale=1.0 / D).then_inc(self.logged, 1)
                act.wait_ge(self.logged, c + 1)
                act.activation(self.stat[:, c], self.stat[:, c], ACT.Exp, scale=-0.5).then_inc(self.rooted, 1)
            root(0)
            for c in range(NC):
                if c + 1 < NC:
                    root(c + 1)
                for h in range(2):
                    act.wait_ge(self.scaled, 2 * c + h + 1)
                    for ft in range(h * HALF, (h + 1) * HALF):
                        for cols, v in pieces[c]:
                            loc = slice(cols.start - c * CW, cols.stop - c * CW)
                            xi = self.xn[c][:, ft, loc]
                            if self.final is not None:
                                last = act.activation(xi, xi, ACT.Identity, scale=gnorm[:, n, ft:ft + 1])
                            else:
                                last = act.activation(xi, xi, ACT.Identity, scale=amod[:, n, ft, v:v + 1],
                                                      bias=mod[:, self.layer, self.shift * KT + ft, v:v + 1])
                    last.then_inc(self.modulated, 1)
                    if self.final is None:
                        act.wait_ge(self.modulated, 2 * c + h + 1)
                        act.activation(hh[:, halves[h], cs[c]], self.xn[c][:, halves[h]], ACT.Copy).then_inc(self.high, 1)

        def vector(self, dve):
            def total(c):
                dve.wait_ge(self.squared[c], 1)
                dve.tensor_reduce(self.stat[:, c], self.sq[c].rearrange("p f t -> p t f"), AX_X, ALU.add).then_inc(self.summed, 1)
            total(0)
            for c in range(NC):
                if c + 1 < NC:
                    total(c + 1)
                dve.wait_ge(self.rooted, c + 1)
                for h in range(2):
                    dve.tensor_tensor(self.xn[c][:, halves[h]], x[:, halves[h], cs[c]],
                                      self.stat[:, c].unsqueeze(1).broadcast_to([P, HALF, CW]), ALU.mult).then_inc(self.scaled, 1)

        def tensor(self, pe):
            for c in range(NC):
                pe.wait_ge(self.summed, c + 1)
                if c == 2:
                    pe.wait_ge(self.logged, 1)
                pe.matmul(self.bank[c], ones[:], self.stat[:, c], start=True, stop=True).then_inc(self.averaged, 1)

        def pool_late(self, pool):
            for c in range(NC):
                for h in range(2):
                    pool.wait_ge(self.high, 2 * c + h + 1)
                    pool.tensor_tensor(hl[:, halves[h], cs[c]], self.xn[c][:, halves[h]], hh[:, halves[h], cs[c]].bitcast(F32),
                                       ALU.subtract).then_inc(self.low, 1)

        def ready(self, pe, c, kk):
            if kk % HALF == 0:
                pe.wait_ge(self.low, 2 * c + kk // HALF + 1)

        def all_ready(self, eng):
            eng.wait_ge(self.low, 2 * NC)

    def final_norm(n, dst):
        s, sem, ps, k = stage()
        with s:
            norm = Norm(sem, k, ps, W0, n, final=dst)
            block = s.enter_context(nc.Block())

            @block.sync
            def _(sp):
                norm.stores(sp)

            @block.scalar
            def _(act):
                norm.act_early(act)
                norm.act_late(act)

            @block.vector
            def _(dve):
                norm.vector(dve)

            @block.tensor
            def _(pe):
                norm.tensor(pe)

            @block.gpsimd
            def _(pool):
                norm.pool_early(pool)

    class EvenOutput:
        order = [f for h in range(HEADS) for f in (h, HEADS + h)]
        bytes = 8 * T + 4 * HEADS * P

        def __init__(self, sem, k, ps, offset):
            self.ps = ps
            self.rstd = [at(f"rstd{k}_{j}", [P, T], F32, offset + j * 4 * T) for j in range(2)]
            self.w_pool = at(f"w_pool{k}", [P, HEADS, P], F32, offset + 8 * T)
            self.w_pool_in, self.averaged, self.logged = sem("w_pool_in"), sem("averaged"), sem("logged")
            self.squared = sem("squared")
            self.inverted, self.normed, self.high, self.low = sem("inverted"), sem("normed"), sem("high"), sem("low")
            self.mixed, self.pooled = sem("mixed"), sem("pooled")
            self.squares = [hl_f32[:, h] for h in range(HEADS)]
            self.tri = lambda ap: ap.rearrange("p (b n) -> p b n", b=NC)

        def loads(self, sp):
            sp.dma_start(self.w_pool[:], inp["w_pool"]).then_inc(self.w_pool_in, 16)

        def stores(self, sp):
            pass

        def tensor(self, pe):
            pe.wait_ge(self.w_pool_in, 16)
            for h in range(HEADS):
                if h >= 1:
                    pe.wait_ge(self.pooled, h)
                for c in range(NC):
                    mm = pe.matmul(self.ps[:, 3 + c, 0:CW], self.w_pool[:, h], qkvu[:, U0 + h, cs[c]], start=True, stop=True)
                mm.then_inc(self.mixed, 1)
                pe.wait_ge(self.squared, h + 1)
                if h >= 1:
                    pe.wait_ge(self.logged, h)
                for c in range(NC):
                    mm = pe.matmul(self.ps[:, c, 0:CW], ones[:], self.squares[h][:, cs[c]], start=True, stop=True)
                mm.then_inc(self.averaged, 1)
            pe.wait_ge(self.logged, HEADS)

        def act_early(self, act):
            pass

        def act_late(self, act):
            def high(n):
                h = n // 2
                act.wait_ge(self.pooled if n % 2 else self.normed, h + 1)
                act.activation(hh[:, self.order[n]], qkvu[:, (U0 if n % 2 else Q0) + h], ACT.Copy).then_inc(self.high, 1)
            for h in range(HEADS):
                act.wait_ge(self.averaged, h + 1)
                if h >= 2:
                    act.wait_ge(self.normed, h - 1)
                rstd = self.rstd[h % 2]
                act.activation(self.tri(rstd[:]), self.ps[:, 0:NC, 0:CW], ACT.Ln, bias=eps[:], scale=1.0 / P).then_inc(self.logged, 1)
                act.wait_ge(self.logged, h + 1)
                act.activation(rstd[:], rstd[:], ACT.Exp, scale=-0.5).then_inc(self.inverted, 1)
                if h >= 1:
                    high(2 * h - 2)
                    high(2 * h - 1)
            high(2 * HEADS - 2)
            high(2 * HEADS - 1)

        def vector(self, dve):
            for h in range(HEADS):
                dve.wait_ge(self.mixed, h + 1)
                dve.tensor_scalar(self.tri(qkvu[:, U0 + h]), self.ps[:, 3:3 + NC, 0:CW], pscale[:, h:h + 1], None,
                                  ALU.mult).then_inc(self.pooled, 1)
                dve.wait_ge(self.inverted, h + 1)
                dve.scalar_tensor_tensor(out=qkvu[:, Q0 + h], in0=qkvu[:, Q0 + h], scalar=subg[:, h:h + 1], in1=self.rstd[h % 2][:],
                                         op0=ALU.mult, op1=ALU.mult).then_inc(self.normed, 1)

        def pool_early(self, pool):
            for h in range(HEADS):
                pool.tensor_tensor(self.squares[h], qkvu[:, Q0 + h], qkvu[:, Q0 + h], ALU.mult).then_inc(self.squared, 1)

        def pool_late(self, pool):
            for n, ft in enumerate(self.order):
                pool.wait_ge(self.high, n + 1)
                pool.tensor_tensor(hl[:, ft], qkvu[:, (U0 if n % 2 else Q0) + n // 2], hh[:, ft].bitcast(F32),
                                   ALU.subtract).then_inc(self.low, 1)

        def ready(self, pe, c, kk):
            if c == 0:
                pe.wait_ge(self.low, self.order.index(kk) + 1)

        def all_ready(self, eng):
            eng.wait_ge(self.low, KT)

    class Split:
        order = range(KT)
        bytes = 0

        def __init__(self, sem, k, ps, offset):
            self.high, self.low = sem("high"), [sem(f"low{ft}") for ft in range(KT)]

        def loads(self, sp):
            pass

        def stores(self, sp):
            pass

        def tensor(self, pe):
            pass

        def cast(self, act, fts):
            for ft in fts:
                act.activation(hh[:, ft], o_all[:, ft], ACT.Copy).then_inc(self.high, 1)

        def act_early(self, act):
            self.cast(act, range(3))

        def act_late(self, act):
            self.cast(act, range(3, KT))

        def subtract(self, eng, fts):
            for ft in fts:
                eng.wait_ge(self.high, ft + 1)
                eng.tensor_tensor(hl[:, ft], o_all[:, ft], hh[:, ft].bitcast(F32), ALU.subtract).then_inc(self.low[ft], 1)

        def vector(self, dve):
            self.subtract(dve, (0, 1, 2, 3, 5, 7))

        def pool_early(self, pool):
            pass

        def pool_late(self, pool):
            self.subtract(pool, (4, 6))

        def ready(self, pe, c, kk):
            if c == 0:
                pe.wait_ge(self.low[kk], 1)

        def all_ready(self, eng):
            for ft in range(KT):
                eng.wait_ge(self.low[ft], 1)

    def product(pe, acc, w_hi, w_lo, in_hi, in_lo, first, last):
        pe.matmul(acc, w_hi, in_hi, start=first, stop=False)
        pe.matmul(acc, w_hi, in_lo, start=False, stop=False)
        return pe.matmul(acc, w_lo, in_hi, start=False, stop=last)

    def projection(w_dram, n_tiles, w_off, result=None, spill=None, residual=None, extra=None, pooling=False,
                   prepare=None, mods=None):
        s, sem, ps, k = stage()
        with s:
            WB = 4 * D
            raw = [at(f"raw{k}_{j}", [P, D], F32, w_off + j * WB) for j in range(2)]
            whi = [at(f"whi{k}_{j}", [P, KT, P], F32R, w_off + (2 + j) * WB) for j in range(2)]
            wlo = [at(f"wlo{k}_{j}", [P, KT, P], F32R, w_off + (4 + j) * WB) for j in range(2)]
            turn = [at(f"turn{k}_{j}", [P, T], F32, w_off + 6 * WB + j * 4 * T) for j in range(2)] if spill is not None else None
            w_in = [sem(f"w_in{j}") for j in range(2)]
            w_high, w_low = sem("w_high"), sem("w_low")
            multiplied, taken = sem("multiplied"), sem("taken")
            x_in, tile_out = sem("x_in"), [sem(f"tile_out{j}") for j in range(2)]
            extra_w, extra_hi, extra_lo, extra_mm, extra_out = (sem("extra_w"), sem("extra_hi"), sem("extra_lo"),
                                                                sem("extra_mm"), sem("extra_out"))
            pairs = n_tiles // 2
            if pooling:
                pool_step = sem("pool_step")
                win = [at(f"win{k}_{j}", [P, PADW], F32, w_off + 6 * WB + j * 4 * PADW) for j in range(3)]
            off = w_off + 6 * WB
            if pooling:
                stat_off = off + 8 * PADW
                off += 12 * PADW
            if spill is not None:
                off += 8 * T
            if extra is not None:
                ex_dram, ex_n, ex_dst = extra
                ex_raw = at(f"exraw{k}", [P, KT * ex_n], F32, off)
                ex_hi = at(f"exhi{k}", [P, KT, ex_n], F32R, off + 4 * KT * ex_n)
                ex_lo = at(f"exlo{k}", [P, KT, ex_n], F32R, off + 8 * KT * ex_n)
                off += 12 * KT * ex_n
            if not pooling:
                stat_off = off
                off += prepare.func.bytes
            ahead = prepare(sem, k, ps, stat_off)
            if residual is not None:
                x_old = at(f"x_old{k}", [P, KT, T], F32, off)
                off += XB
            if mods is not None:
                mods = ModulationBeside(sem, k, ps, off, *mods)
            block = s.enter_context(nc.Block())

            @block.sync
            def _(sp):
                ahead.loads(sp)
                if extra is not None:
                    sp.dma_start(ex_raw[:], ex_dram).then_inc(extra_w, 16)

                def body(i):
                    for j in range(2):
                        wait(sp, w_low, i, 2, j - 1)
                        m = i * 2 + j
                        sp.dma_start(raw[j][:], w_dram[bass.ds(m, 1)].rearrange("o p n -> p (o n)")).then_inc(w_in[j], 16)
                    if residual is not None and isinstance(i, int):
                        for c in range(NC):
                            sp.dma_start(x_old[:, :, cs[c]], residual[0][:, :, cs[c]]).then_inc(x_in, 16)
                    if mods is not None:
                        if isinstance(i, int):
                            mods.load_row(sp)
                        mods.load(sp, i)
                    if spill is not None and not isinstance(i, int):
                        store(i - 1)

                def store(i):
                    for j in range(2):
                        wait(sp, taken, i, 2 * NC, NC * (j + 1))
                        sp.dma_start(spill[bass.ds(i * 2 + j, 1)].rearrange("o p n -> p (o n)"), turn[j][:]).then_inc(tile_out[j], 16)
                peeled(sp, body, pairs)
                if spill is not None:
                    store(pairs - 1)
                    for j in range(2):
                        sp.wait_ge(tile_out[j], 16 * pairs)
                ahead.stores(sp)

            @block.scalar
            def _(act):
                ahead.act_early(act)
                if extra is not None:
                    act.wait_ge(extra_w, 16)
                    act.activation(ex_hi[:].rearrange("p k n -> p (k n)"), ex_raw[:], ACT.Copy).then_inc(extra_hi, 1)

                def body(i):
                    for j in range(2):
                        wait(act, w_in[j], i, 16, 16)
                        wait(act, multiplied, i, 2 * NC, NC * (j + 1) - 2 * NC)
                        act.activation(whi[j][:].rearrange("p k n -> p (k n)"), raw[j][:], ACT.Copy).then_inc(w_high, 1)
                    if isinstance(i, int):
                        ahead.act_late(act)
                        if mods is not None:
                            mods.silu(act)
                peeled(act, body, pairs)

            @block.gpsimd
            def _(pool):
                ahead.pool_early(pool)
                if extra is not None:
                    pool.wait_ge(extra_hi, 1)
                    pool.tensor_tensor(ex_lo[:].rearrange("p k n -> p (k n)"), ex_raw[:],
                                       ex_hi[:].rearrange("p k n -> p (k n)").bitcast(F32), ALU.subtract).then_inc(extra_lo, 1)

                def body(i):
                    for j in range(2):
                        wait(pool, w_high, i, 2, j + 1)
                        pool.tensor_tensor(wlo[j][:].rearrange("p k n -> p (k n)"), raw[j][:],
                                           whi[j][:].rearrange("p k n -> p (k n)").bitcast(F32), ALU.subtract).then_inc(w_low, 1)
                    if isinstance(i, int) and i == 0:
                        ahead.pool_late(pool)
                if not pooling:
                    peeled(pool, body, pairs)
                    return

                seqs = ((slice(0, CTX), PAD), (slice(CTX, T), PAD + CTX + 2 * PAD))
                step = 0

                def then(ins):
                    nonlocal step
                    step += 1
                    ins.then_inc(pool_step, 1)
                    pool.wait_ge(pool_step, step)

                def fill(g):
                    u = result[:, U0 + g]
                    pool.wait_ge(taken, NC * (U0 + g + 1))
                    for cols, at_col in seqs:
                        then(pool.tensor_copy(win[0][:, at_col:at_col + cols.stop - cols.start], u[:, cols]))
                    double(g, 0)

                def double(g, b):
                    src, dst, n = win[0 if b == 0 else 1 + (b - 1) % 2], win[1 + b % 2], PADW + 1 - (2 << b)
                    then(pool.tensor_tensor(dst[:, 0:n], src[:, 0:n], src[:, 1 << b:n + (1 << b)], ALU.add))

                def average(g):
                    w = WINDOWS[g]
                    b = w.bit_length() - 2
                    src, n, u = win[1 + b % 2], PADW + 1 - w, result[:, U0 + g]
                    then(pool.tensor_scalar(src[:, 0:n], src[:, 0:n], 1.0 / w, None, ALU.mult))
                    for cols, at_col in seqs:
                        first, m = at_col - w // 2, cols.stop - cols.start
                        for side, c0 in ((0, first), (1, first + m - PAD)):
                            then(pool.tensor_tensor(src[:, c0:c0 + PAD], src[:, c0:c0 + PAD], edge[:, g, side], ALU.mult))
                        then(pool.tensor_tensor(u[:, cols], src[:, first:first + m], u[:, cols], ALU.subtract))
                pieces_ = [lambda: (fill(0), average(0)), lambda: (fill(1), double(1, 1), average(1)),
                           lambda: (fill(2), double(2, 1)), lambda: (double(2, 2), average(2)),
                           lambda: (fill(3), double(3, 1), double(3, 2)), lambda: (double(3, 3), average(3))]
                for i in range(pairs):
                    body(i)
                    if i == 0:
                        then(pool.memset(win[0][:], 0.0))
                    if i >= 2:
                        pieces_[i - 2]()

            @block.tensor
            def _(pe):
                ahead.tensor(pe)
                if extra is not None:
                    pe.wait_ge(extra_lo, 1)
                    for c in range(NC):
                        if c >= 2:
                            pe.wait_ge(extra_out, c - 1)
                        for kk in range(KT):
                            ahead.ready(pe, c, kk)
                            mm = product(pe, ps[0:ex_n, 7 - c % 2, 0:CW], ex_hi[:, kk, :], ex_lo[:, kk, :],
                                         hh[:, kk, cs[c]], hl[:, kk, cs[c]], kk == 0, kk == KT - 1)
                        mm.then_inc(extra_mm, 1)

                def body(i):
                    for j in range(2):
                        wait(pe, w_low, i, 2, j + 1)
                        for c in range(NC):
                            bank = ps[:, NC * j + c]
                            wait(pe, taken, i, 2 * NC, NC * j + c + 1 - 2 * NC)
                            for kk in ahead.order:
                                if extra is None and isinstance(i, int) and j == 0:
                                    ahead.ready(pe, c, kk)
                                mm = product(pe, bank[:, 0:CW], whi[j][:, kk, :], wlo[j][:, kk, :],
                                             hh[:, kk, cs[c]], hl[:, kk, cs[c]], kk == ahead.order[0], kk == ahead.order[-1])
                            mm.then_inc(multiplied, 1)
                peeled(pe, body, pairs)

            @block.vector
            def _(dve):
                ahead.vector(dve)
                ahead.all_ready(dve)
                if extra is not None:
                    for c in range(NC):
                        dve.wait_ge(extra_mm, c + 1)
                        dve.tensor_copy(ex_dst[:, cs[c]], ps[0:ex_n, 7 - c % 2, 0:CW]).then_inc(extra_out, 1)
                    dve.wait_ge(extra_out, NC)
                if residual is not None:
                    dve.wait_ge(x_in, 16 * NC)

                def body(i):
                    for j in range(2):
                        m = i * 2 + j
                        for c in range(NC):
                            acc = ps[:, NC * j + c]
                            wait(dve, multiplied, i, 2 * NC, NC * j + c + 1)
                            if residual is not None:
                                _, layer, kind = residual
                                for cols, v in pieces[c]:
                                    loc = slice(cols.start - c * CW, cols.stop - c * CW)
                                    xo, xi = [b[:, bass.ds(m, 1), cols].rearrange("p o t -> p (o t)") for b in (x, x_old)]
                                    last = dve.scalar_tensor_tensor(
                                        out=xo, in0=acc[:, loc], scalar=mod[:, layer, bass.ds(m + kind * KT, 1), v],
                                        in1=xi, op0=ALU.mult, op1=ALU.add)
                            elif spill is not None:
                                if c == 0:
                                    wait(dve, tile_out[j], i, 16, 0)
                                last = dve.tensor_copy(turn[j][:, cs[c]], acc[:, 0:CW])
                            else:
                                last = dve.tensor_copy(result[:, bass.ds(m, 1), cs[c]].rearrange("p o t -> p (o t)"), acc[:, 0:CW])
                            last.then_inc(taken, 1)
                            if mods is not None:
                                for t in range(mods.per_pair):
                                    if t * 2 * NC // mods.per_pair == NC * j + c:
                                        mods.multiply(dve, i, t)
                    if mods is not None:
                        mods.take(dve, i)
                peeled(dve, body, pairs)
                if mods is not None:
                    mods.finish(dve, pairs)

    def ffn(layer, norm):
        s, sem, ps, k = stage()
        with s:
            o = W0
            raw_in = at(f"raw_in{k}", [P, 2, 2 * D], F32, o)
            raw_out = at(f"raw_out{k}", [P, 2 * D], F32, o + 16 * D)
            wi_hi = at(f"wi_hi{k}", [P, 2, 2, KT, P], F32R, o + 24 * D)
            wi_lo = at(f"wi_lo{k}", [P, 2, 2, KT, P], F32R, o + 40 * D)
            wo_hi = at(f"wo_hi{k}", [P, 2, KT, P], F32R, o + 56 * D)
            wo_lo = at(f"wo_lo{k}", [P, 2, KT, P], F32R, o + 64 * D)
            o += 72 * D
            hid_hi = at(f"hid_hi{k}", [P, NC, 2, CW], F32R, o)
            hid_lo = at(f"hid_lo{k}", [P, NC, 2, CW], F32R, o + 8 * T)
            hid = at(f"hid{k}", [P, 2, CW], F32, o + 16 * T)
            assert o + 16 * T + 8 * CW <= END
            win_in = [sem("win_in0"), sem("win_in1")]
            wout_in = sem("wout_in")
            win_high, win_low, wout_high, wout_low = sem("win_high"), sem("win_low"), sem("wout_high"), sem("wout_low")
            ab_done, silu_done, hid_done, hid_high, hid_low = (sem("ab_done"), sem("silu_done"), sem("hid_done"),
                                                               sem("hid_high"), sem("hid_low"))
            out_acc, added = sem("out_acc"), sem("added")
            norm = Norm(sem, k, ps, W0 + 16 * D, **norm)
            N = FFN_PAIRS
            w_in, w_out = inp["w_ffn_in"][layer], inp["w_ffn_out"][layer]
            block = s.enter_context(nc.Block())

            @block.sync
            def _(sp):
                norm.loads(sp)

                def body(i):
                    for t in range(2):
                        wait(sp, win_low, i, 2, t - 1)
                        sp.dma_start(raw_in[:, t], w_in[bass.ds(i * 2 + t, 1)].rearrange("o p n -> p (o n)")).then_inc(win_in[t], 16)
                    wait(sp, wout_low, i, 1, 0)
                    if isinstance(i, int):
                        norm.all_ready(sp)
                    sp.dma_start(raw_out[:], w_out[bass.ds(i, 1)].rearrange("o p n -> p (o n)")).then_inc(wout_in, 16)
                peeled(sp, body, N)

            @block.scalar
            def _(act):
                def cast_in(i, t):
                    wait(act, win_in[t], i, 16, 16)
                    wait(act, ab_done, i, 6, -(1 - t))
                    act.activation(wi_hi[:, t].rearrange("p a k n -> p (a k n)"), raw_in[:, t], ACT.Copy).then_inc(win_high, 1)

                def body(i, first=False, last=False):
                    if not first:
                        cast_in(i, 1)
                    for c in range(NC):
                        for t in range(2):
                            wait(act, ab_done, i, 6, 2 * c + t + 1)
                            wait(act, hid_low, i, 3, c)
                            act.activation(hid[:, t], ps[:, 2 * t, 0:CW], ACT.Silu).then_inc(silu_done, 1)
                            if c == NC - 1 and t == 0 and not last:
                                cast_in(i + 1, 0)
                        wait(act, hid_done, i, 6, 2 * c + 2)
                        wait(act, out_acc, i, 3 * KT, KT * (c + 1 - NC))
                        act.activation(hid_hi[:, c], hid[:], ACT.Copy).then_inc(hid_high, 1)
                        if c == 0:
                            wait(act, wout_in, i, 16, 16)
                            wait(act, out_acc, i, 3 * KT, 0)
                            act.activation(wo_hi[:].rearrange("p t k n -> p (t k n)"), raw_out[:], ACT.Copy).then_inc(wout_high, 1)
                norm.act_early(act)
                cast_in(0, 0)
                cast_in(0, 1)
                norm.act_late(act)
                body(0, first=True)
                with act.Fori(1, N - 1) as i:
                    body(i)
                body(N - 1, last=True)

            @block.gpsimd
            def _(pool):
                def split_in(i, t):
                    wait(pool, win_high, i, 2, t + 1)
                    pool.tensor_tensor(wi_lo[:, t].rearrange("p a k n -> p (a k n)"), raw_in[:, t],
                                       wi_hi[:, t].rearrange("p a k n -> p (a k n)").bitcast(F32), ALU.subtract).then_inc(win_low, 1)

                def body(i):
                    for t in range(2):
                        split_in(i, t)
                    if isinstance(i, int):
                        norm.pool_late(pool)
                    wait(pool, wout_high, i, 1, 1)
                    pool.tensor_tensor(wo_lo[:].rearrange("p t k n -> p (t k n)"), raw_out[:],
                                       wo_hi[:].rearrange("p t k n -> p (t k n)").bitcast(F32), ALU.subtract).then_inc(wout_low, 1)
                norm.pool_early(pool)
                peeled(pool, body, N)

            @block.tensor
            def _(pe):
                def contract(i, c):
                    wait(pe, hid_low, i, 3, c + 1)
                    wait(pe, wout_low, i, 1, 1)
                    for ft in range(KT):
                        acc = ps[:, 4 + ft % 4, 0:CW]
                        wait(pe, added, i, 3 * KT, KT * c + ft - 3)
                        for t in range(2):
                            mm = product(pe, acc, wo_hi[:, t, ft], wo_lo[:, t, ft], hid_hi[:, c, t], hid_lo[:, c, t],
                                         t == 0, t == 1)
                        mm.then_inc(out_acc, 1)

                def body(i, first=False):
                    for c in range(NC):
                        for t in range(2):
                            if c == 0:
                                wait(pe, win_low, i, 2, t + 1)
                            wait(pe, hid_done, i, 6, 2 * c + t + 1 - 2)
                            for ab in range(2):
                                for kk in range(KT):
                                    if first and t == 0 and ab == 0:
                                        norm.ready(pe, c, kk)
                                    mm = product(pe, ps[:, 2 * t + ab, 0:CW], wi_hi[:, t, ab, kk], wi_lo[:, t, ab, kk],
                                                 hh[:, kk, cs[c]], hl[:, kk, cs[c]], kk == 0, kk == KT - 1)
                            mm.then_inc(ab_done, 1)
                        if c == 0 and first:
                            continue
                        contract(i - 1 if c == 0 else i, (c - 1) % NC)
                norm.tensor(pe)
                body(0, first=True)
                with pe.Fori(1, N) as i:
                    body(i)
                contract(N - 1, NC - 1)

            @block.vector
            def _(dve):
                def add(i, c):
                    for ft in range(KT):
                        wait(dve, out_acc, i, 3 * KT, KT * c + ft + 1)
                        for cols, v in pieces[c]:
                            loc = slice(cols.start - c * CW, cols.stop - c * CW)
                            last = dve.scalar_tensor_tensor(
                                out=x[:, ft, cols], in0=ps[:, 4 + ft % 4, loc],
                                scalar=mod[:, layer, GATE2 * KT + ft, v:v + 1], in1=x[:, ft, cols],
                                op0=ALU.mult, op1=ALU.add)
                        last.then_inc(added, 1)

                def body(i, first=False):
                    for c in range(NC):
                        for t in range(2):
                            wait(dve, silu_done, i, 6, 2 * c + t + 1)
                            dve.tensor_tensor(hid[:, t], ps[:, 2 * t + 1, 0:CW], hid[:, t], ALU.mult).then_inc(hid_done, 1)
                        wait(dve, hid_high, i, 3, c + 1)
                        dve.tensor_tensor(hid_lo[:, c], hid[:], hid_hi[:, c].bitcast(F32), ALU.subtract).then_inc(hid_low, 1)
                        if c == 0 and first:
                            continue
                        add(i - 1 if c == 0 else i, (c - 1) % NC)
                norm.vector(dve)
                norm.all_ready(dve)
                body(0, first=True)
                with dve.Fori(1, N) as i:
                    body(i)
                add(N - 1, NC - 1)

    def attention(qkvu, w_off):
        s, sem, ps, k = stage()
        KALL = T + CTX
        QB = P
        UN = T // QB
        GROUP = 4
        with s:
            o = HH0
            at_buf = [at(f"at{k}_{g}", [P, NT, GROUP * QB], F32, o + g * 4 * NT * GROUP * QB) for g in range(2)]
            o += 8 * NT * GROUP * QB
            prob0 = [at(f"prob0{k}_{r}", [P, T], F32, o + r * 4 * T) for r in range(2)]
            prob1 = [at(f"prob1{k}_{r}", [P, T], F32, o + (2 + r) * 4 * T) for r in range(2)]
            o += 16 * T
            at_ctx = at(f"at_ctx{k}", [P, QB], F32, o)
            o += 4 * QB
            v_tok = at(f"v_tok{k}", [P, NT + 1, P], F32, o)
            o += 4 * (NT + 1) * P
            v_head = at(f"v_head{k}", [P, T], F32, o)
            o += 4 * T
            rot_cos = at(f"rot_cos{k}", [P, LAT], F32, o)
            rot_sin = at(f"rot_sin{k}", [P, LAT], F32, o + 4 * LAT)
            o += 8 * LAT
            assert o <= X0
            o = w_off
            cos = at(f"cos{k}", [P, LAT], F32, o)
            sin = at(f"sin{k}", [P, LAT], F32, o + 4 * LAT)
            o += 8 * LAT
            q_f = at(f"q_f{k}", [P, T], F32, o)
            k_f = at(f"k_f{k}", [P, KALL], F32, o + 4 * T)
            o += 4 * (T + KALL)
            q_hi = at(f"q_hi{k}", [P, T], F32R, o)
            q_lo = at(f"q_lo{k}", [P, T], F32R, o + 4 * T)
            o += 8 * T
            k_hi = at(f"k_hi{k}", [P, KALL], F32R, o)
            k_lo = at(f"k_lo{k}", [P, KALL], F32R, o + 4 * KALL)
            o += 8 * KALL
            ck = at(f"ck{k}", [P, HEADS, CTX], F32, o)
            cv = at(f"cv{k}", [P, HEADS, P], F32, o + 4 * HEADS * CTX)
            o += 8 * HEADS * P
            prob0.append(at(f"prob0{k}_2", [P, T], F32, o))
            o += 4 * T
            nmax = at(f"nmax{k}", [P, 2, 2], F32, o)
            esum = at(f"esum{k}", [P, 2, 2], F32, o + 32)
            rinv = at(f"rinv{k}", [P, 2, 2], F32, o + 64)
            w1 = at(f"w1{k}", [P, 2], F32, o + 96)
            assert o + 128 <= END, (o, END)

            loaded, stored = sem("loaded"), sem("stored")
            rotated, v_turned = sem("rotated"), sem("v_turned")
            v_copied, v_out = sem("v_copied"), sem("v_out")
            rope_part, roped = sem("rope_part"), sem("roped")
            qk_high, qk_low = sem("qk_high"), sem("qk_low")
            scored, maxed, exped = sem("scored"), sem("maxed"), sem("exped")
            weighed, combined = sem("weighed"), sem("combined")
            turned, at_out = sem("turned"), sem("at_out")
            pv_done, o_out = sem("pv_done"), sem("o_out")
            H2 = 2 * UN
            ROUNDS = 1 + 3 * (UN - 1)
            tile = lambda n, cols: qkvu[:, bass.ds(n, 1), cols].rearrange("p o t -> p (o t)")
            lat = slice(CTX, T)
            block = s.enter_context(nc.Block())

            @block.sync
            def _(sp):
                for dst, src in ((cos, inp["c_cos"]), (sin, inp["c_sin"]), (ck, inp["cache_k"]), (cv, inp["cache_v"])):
                    sp.dma_start(dst[:], src).then_inc(loaded, 16)
                sp.dma_start(out["new_k"].rearrange("h p t -> p h t"), qkvu[:, K0:K0 + HEADS, 0:CTX]).then_inc(stored, 16)
                sp.dma_start(out["new_v"].rearrange("h p t -> p h t"), qkvu[:, V0:V0 + HEADS, 0:CTX]).then_inc(stored, 16)

                sp.wait_ge(stored, 32)

            @block.scalar
            def _(act):
                act.wait_ge(loaded, 64)

                def exps(i, u, a):
                    r = u % 2
                    if a == 0:
                        wait(act, combined, i, UN, -u if u < 2 else u - 1)
                        wait(act, turned, i, ROUNDS, 3 * u - 6 if u < 3 else 1 + 3 * (u - 3))
                    buf = prob0[u % 3] if a == 0 else prob1[r]
                    wait(act, maxed, i, H2, 2 * u + a + 1)
                    if u == 0:
                        act.activation(buf[:, 0:CTX], ps[:, 3 * a, 0:CTX], ACT.Exp, bias=nmax[:, r, a:a + 1],
                                       accum_out=esum[:, r, a:a + 1]).then_inc(exped, 1)
                    else:
                        act.activation(buf[:].rearrange("p (b n) -> p b n", b=3), ps[:, 3 * a:3 * a + 3, 0:CW],
                                       ACT.Exp, bias=nmax[:, r, a:a + 1], accum_out=esum[:, r, a:a + 1]).then_inc(exped, 1)

                def out_of_psum(i, u, r):
                    if u == 0:
                        if r == 0:
                            wait(act, turned, i, ROUNDS, 1)
                            wait(act, pv_done, i, 3, -2)
                            act.activation(at_ctx[:], ps[:, 6, 0:QB], ACT.Copy).then_inc(at_out, 1)
                        return
                    g, j = (u - 1) // GROUP, (u - 1) % GROUP
                    wait(act, turned, i, ROUNDS, 1 + 3 * (u - 1) + r + 1)
                    if j == 0 and r == 0:
                        wait(act, pv_done, i, 3, g + 2 - 3)
                    act.activation(at_buf[g][:, 3 * r:3 * r + 3, j * QB:(j + 1) * QB],
                                   ps[:, 6 + (3 * (u - 1) + r + 1) % 2, 0:3 * QB].rearrange("p (b n) -> p b n", b=3), ACT.Copy).then_inc(at_out, 1)

                def values_in(i, ahead):
                    wait(act, v_turned, i, 1, ahead)
                    act.activation(v_head[:], tile(i + V0 + ahead, slice(0, T)), ACT.Copy).then_inc(v_copied, 1)

                def high_parts(i, ahead):
                    wait(act, scored, i, H2, H2 * ahead)
                    wait(act, roped, i, 2, 2 * ahead + 1)
                    act.activation(q_hi[:], q_f[:], ACT.Copy).then_inc(qk_high, 1)
                    wait(act, roped, i, 2, 2 * ahead + 2)
                    act.activation(k_hi[:], k_f[:], ACT.Copy).then_inc(qk_high, 1)

                def values_out(i, ahead):
                    wait(act, pv_done, i, 3, 3 * ahead)
                    act.activation(v_tok[:, NT], cv[:, bass.ds(i + ahead, 1)].rearrange("p o t -> p (o t)"), ACT.Copy).then_inc(v_out, 1)
                    wait(act, v_turned, i, 1, ahead + 1)
                    for r in range(3):
                        act.activation(v_tok[:, 3 * r:3 * r + 3].rearrange("p b n -> p (b n)"), ps[:, 4 + r, 0:3 * P],
                                       ACT.Copy).then_inc(v_out, 1)

                def body(i, last=False):
                    for u in range(UN):
                        exps(i, u, 0)
                        if u >= 2:
                            out_of_psum(i, u - 2, 0)
                            out_of_psum(i, u - 2, 1)
                        exps(i, u, 1)
                        if u >= 2:
                            out_of_psum(i, u - 2, 2)
                    if not last:
                        values_in(i, 1)
                    for u in (UN - 2, UN - 1):
                        for r in range(3):
                            out_of_psum(i, u, r)
                    if not last:
                        high_parts(i, 1)
                        values_out(i, 1)
                values_in(0, 0)
                high_parts(0, 0)
                values_out(0, 0)
                body(0)
                with act.Fori(1, HEADS - 1) as i:
                    body(i)
                body(HEADS - 1, last=True)

            @block.vector
            def _(dve):
                dve.wait_ge(loaded, 64)

                def rope(i, ahead, n):
                    dst, scale = ((q_f, DH ** -0.5), (k_f, 1.0))[n]
                    src = lambda cols: tile(i + (Q0, K0)[n] + ahead, cols)
                    wait(dve, rotated, i, 2, 2 * ahead + n + 1)
                    wait(dve, roped, i, 2, 2 * ahead + n)
                    dve.scalar_tensor_tensor(out=rot_cos[:], in0=src(lat), scalar=scale, in1=cos[:],
                                             op0=ALU.mult, op1=ALU.mult).then_inc(rope_part, 1)
                    dve.scalar_tensor_tensor(out=rot_sin[:].rearrange("p (b n) -> p b n", b=2), in0=ps[:, 2 * n:2 * n + 2],
                                             scalar=scale, in1=sin[:].rearrange("p (b n) -> p b n", b=2),
                                             op0=ALU.mult, op1=ALU.mult).then_inc(rope_part, 1)
                    wait(dve, qk_low, i, 2, 2 * ahead + n - 1)
                    dve.tensor_scalar(dst[:, 0:CTX], src(slice(0, CTX)), scale, None, ALU.mult)
                    if n == 1:
                        dve.tensor_copy(dst[:, T:KALL], ck[:, bass.ds(i + ahead, 1)].rearrange("p o t -> p (o t)"))
                    wait(dve, rope_part, i, 4, 4 * ahead + 2 * n + 2)
                    dve.tensor_tensor(dst[:, CTX:T], rot_cos[:], rot_sin[:], ALU.add).then_inc(roped, 1)

                def minus_max(i, u, a):
                    r = u % 2
                    wait(dve, scored, i, H2, 2 * u + a + 1)
                    if a == 0:
                        wait(dve, exped, i, H2, 2 * (u - 1))
                    src = ps[:, 3 * a, 0:CTX] if u == 0 else ps[:, 3 * a:3 * a + 3, 0:CW]
                    dve.tensor_reduce(nmax[:, r, a:a + 1], src, AX_X if u == 0 else mybir.AxisListType.XY, ALU.max,
                                      negate=True).then_inc(maxed, 1)

                def combine(i, u):
                    r = u % 2
                    n = CTX if u == 0 else T
                    wait(dve, exped, i, H2, 2 * u + 2)
                    dve.reciprocal(rinv[:, r], esum[:, r]).then_inc(weighed, 1)
                    wait(dve, weighed, i, 3 * UN, 3 * u + 1)
                    dve.tensor_scalar(w1[:, r:r + 1], rinv[:, r, 1:2], neglam[:, 0:1], None, ALU.mult).then_inc(weighed, 1)
                    wait(dve, weighed, i, 3 * UN, 3 * u + 2)
                    dve.tensor_scalar(prob1[r][:, 0:n], prob1[r][:, 0:n], w1[:, r:r + 1], None, ALU.mult).then_inc(weighed, 1)
                    wait(dve, weighed, i, 3 * UN, 3 * u + 3)
                    dve.scalar_tensor_tensor(out=prob0[u % 3][:, 0:n], in0=prob0[u % 3][:, 0:n], scalar=rinv[:, r, 0:1],
                                             in1=prob1[r][:, 0:n], op0=ALU.mult, op1=ALU.add).then_inc(combined, 1)

                def take_o(i, g):
                    cols = slice(0, CTX) if g == 0 else slice(CTX + (g - 1) * 512, CTX + g * 512)
                    wait(dve, pv_done, i, 3, g + 1)
                    dve.tensor_scalar(tile(i + Q0, cols), ps[:, 7, 0:cols.stop - cols.start], 1.0, None, ALU.mult).then_inc(o_out, 1)

                def body(i, last=False):
                    minus_max(i, 0, 0)
                    minus_max(i, 0, 1)
                    for u in range(UN):
                        if u + 1 < UN:
                            minus_max(i, u + 1, 0)
                        combine(i, u)
                        if u == 2:
                            take_o(i, 0)
                        if u == 6:
                            take_o(i, 1)
                        if u + 1 < UN:
                            minus_max(i, u + 1, 1)
                    if not last:
                        rope(i, 1, 0)
                        rope(i, 1, 1)
                    take_o(i, 2)
                rope(0, 0, 0)
                rope(0, 0, 1)
                body(0)
                with dve.Fori(1, HEADS - 1) as i:
                    body(i)
                body(HEADS - 1, last=True)

            @block.gpsimd
            def _(pool):
                def body(i):
                    for n, (hi, lo, src) in enumerate(((q_hi, q_lo, q_f), (k_hi, k_lo, k_f))):
                        wait(pool, qk_high, i, 2, n + 1)
                        pool.tensor_tensor(lo[:], src[:], hi[:].bitcast(F32), ALU.subtract).then_inc(qk_low, 1)
                peeled(pool, body, HEADS)

            @block.tensor
            def _(pe):
                def scores(i, u, a):
                    q = slice(u * QB, (u + 1) * QB)
                    keys = [slice(0, CTX)] if u == 0 else [slice(CTX + c * CW, CTX + (c + 1) * CW) for c in range(NC)]
                    rows = slice(a * DH, (a + 1) * DH)
                    wait(pe, exped, i, H2, 2 * (u - 1) + a + 1)
                    for c, cols in enumerate(keys):
                        acc = ps[:, 3 * a + c, 0:cols.stop - cols.start]
                        pe.matmul(acc, q_hi[rows, q], k_hi[rows, cols], start=True, stop=False)
                        pe.matmul(acc, q_hi[rows, q], k_lo[rows, cols], start=False, stop=False)
                        mm = pe.matmul(acc, q_lo[rows, q], k_hi[rows, cols], start=False, stop=True)
                    mm.then_inc(scored, 1)

                def turning(i, u, outs, rounds=range(3)):
                    for r in rounds:
                        if u == 0 and r > 0:
                            continue
                        n = 0 if u == 0 else 1 + 3 * (u - 1) + r
                        if r == 0:
                            wait(pe, combined, i, UN, u + 1)
                        wait(pe, at_out, i, ROUNDS, n - 1 if n else 0)
                        if n % 2:
                            wait(pe, o_out, i, 3, outs)
                        for b in range(1 if u == 0 else 3):
                            mm = pe.transpose(ps[:, 6 + n % 2, b * P:(b + 1) * P],
                                              prob0[u % 3][:, (3 * r + b) * P:(3 * r + b + 1) * P], ident[:])
                        mm.then_inc(turned, 1)

                def values(i, g):
                    wait(pe, at_out, i, ROUNDS, 1 if g == 0 else 1 + 3 * GROUP * g)
                    wait(pe, v_out, i, 4, 4)
                    wait(pe, o_out, i, 3, g)
                    if g == 0:
                        pe.matmul(ps[:, 7, 0:CTX], v_tok[:, 0], at_ctx[:], start=True, stop=True).then_inc(pv_done, 1)
                        return
                    for kt in range(NT):
                        mm = pe.matmul(ps[:, 7], v_tok[:, kt + 1], at_buf[g - 1][:, kt], start=(kt == 0), stop=(kt == NT - 1))
                    mm.then_inc(pv_done, 1)

                def rotate(i, ahead):
                    wait(pe, exped, i, H2, H2 * ahead)
                    for n in range(2):
                        for b in range(2):
                            mm = pe.matmul(ps[:, 2 * n + b], rot_t[:], tile(i + (Q0, K0)[n] + ahead, slice(CTX + b * 512, CTX + (b + 1) * 512)),
                                           start=True, stop=True)
                        mm.then_inc(rotated, 1)

                def turn_values(i, ahead):
                    wait(pe, v_copied, i, 1, ahead + 1)
                    wait(pe, at_out, i, ROUNDS, ROUNDS * ahead)
                    for t in range(NT):
                        mm = pe.transpose(ps[:, 4 + t // 3, (t % 3) * P:(t % 3 + 1) * P], v_head[:, t * P:(t + 1) * P], ident[:])
                    mm.then_inc(v_turned, 1)

                def body(i, last=False):
                    wait(pe, qk_low, i, 2, 2)
                    outs = 0
                    scores(i, 0, 0)
                    scores(i, 0, 1)
                    wait(pe, v_out, i, 4, 4)
                    for u in range(1, UN):
                        scores(i, u, 0)
                        if u in (3, 7):
                            values(i, outs)
                            outs += 1
                        if u >= 2:
                            turning(i, u - 2, outs, (0, 1))
                        scores(i, u, 1)
                        if u >= 2:
                            turning(i, u - 2, outs, (2,))
                    turning(i, UN - 2, outs)
                    if not last:
                        rotate(i, 1)
                    turning(i, UN - 1, outs)
                    values(i, 2)
                    if not last:
                        turn_values(i, 1)
                rotate(0, 0)
                turn_values(0, 0)
                body(0)
                with pe.Fori(1, HEADS - 1) as i:
                    body(i)
                body(HEADS - 1, last=True)

    def gla(gd, o_all):
        s, sem, ps, k = stage()
        with s:
            o = HH0
            head = at(f"head{k}", [P, 6, T], F32, o)
            o += 24 * T
            v_tok = at(f"v_tok{k}", [P, NT, 2 * P], F32, o)
            o += 8 * NT * P
            state = [at(f"state{k}_{d}", [P, NCHUNK, 2 * P], F32, o + d * 8 * NCHUNK * P) for d in range(2)]
            o += 16 * NCHUNK * P
            assert o <= X0
            o = W0
            log_part = at(f"log_part{k}", [P, T], F32, o)
            gate = [at(f"gate{k}_{d}", [P, T], F32, o + (1 + d) * 4 * T) for d in range(2)]
            squares = at(f"squares{k}", [P, 2, T], F32, o + 4 * T)
            decay_sum = [at(f"decay_sum{k}_{d}", [P, T], F32, o + (3 + d) * 4 * T) for d in range(2)]
            q_t = [at(f"q_t{k}_{d}", [P, T], F32, o + (5 + d) * 4 * T) for d in range(2)]
            k_t = [at(f"k_t{k}_{d}", [P, T], F32, o + (7 + d) * 4 * T) for d in range(2)]
            k_end = [at(f"k_end{k}_{d}", [P, T], F32, o + (9 + d) * 4 * T) for d in range(2)]
            a_t = [at(f"a_t{k}_{d}", [P, NT, P], F32, o + (11 + d) * 4 * T) for d in range(2)]
            k_end_tok = [at(f"k_end_tok{k}_{d}", [P, NT, P], F32, o + (13 + d) * 4 * T) for d in range(2)]
            scan_mask = at(f"scan_mask{k}", [P, T], F32, o + 15 * 4 * T)
            o += 16 * 4 * T
            up = at(f"up{k}", [48, P], F32, o)
            decay = at(f"decay{k}", [P, 2, NCHUNK], F32, o + 4 * P)
            o += 4 * P + 192
            assert o <= GD0, (o, GD0)
            rstd = decay_sum[0]

            mask_in, qk_in, v_in, r_in = sem("mask_in"), sem("qk_in"), sem("v_in"), sem("r_in")
            up_in, state_in, states_out = sem("up_in"), sem("state_in"), sem("states_out")
            v_turned, v_out = sem("v_turned"), sem("v_out")
            z_done, gate_act, gate_min, gate_sum, scanned = (sem("z_done"), sem("gate_act"), sem("gate_min"),
                                                             sem("gate_sum"), sem("scanned"))
            grown, shrunk, decayed, to_go, ended = (sem("grown"), sem("shrunk"), sem("decayed"), sem("to_go"),
                                                    sem("ended"))
            q_ready, k_ready, k_end_ready = sem("q_ready"), sem("k_ready"), sem("k_end_ready")
            k_end_turned, k_end_out = sem("k_end_turned"), sem("k_end_out")
            kv_done, stepped = sem("kv_done"), sem("stepped")
            a_done, a_out, a_joined = sem("a_done"), sem("a_out"), sem("a_joined")
            o_done, o_out, silu_r = sem("o_done"), sem("o_out"), sem("silu_r")
            squared, averaged, rooted, inverted, scaled, finished = (sem("squared"), sem("averaged"), sem("rooted"),
                                                                     sem("inverted"), sem("scaled"), sem("finished"))
            NPAIR = NCHUNK // 2
            KVS = 2 * NPAIR
            OB = 5
            GROUP = [4, 4, 4, 4, 2]
            Z_BANKS, V_BANKS, O_BANK0 = (0, 1, 2), (0, 1, 2, 0, 1), 3
            KE_BANKS, A_BANKS, M_BANK0 = ((3, 4, 5), (6, 7, 2)), ((0, 1, 3), (7, 2, 0)), 4
            KV_BANKS = ((4, 5), (6, 3), (1, 7), (2, 0))
            pair_order = [list(range(NPAIR)), [0] + list(range(NPAIR - 1, 0, -1))]
            chunk_of = lambda ap: ap.rearrange("p (n c) -> p n c", c=GCH)
            last_of = lambda ap, d: chunk_of(ap)[:, :, GCH - 1:GCH] if d == 0 else chunk_of(ap)[:, :, 0:1]
            tri = lambda ap: ap.rearrange("p (b n) -> p b n", b=NC)

            updates, count, latest = [], 0, [0, 0]
            for n in range(KVS):
                d, q = n % 2, pair_order[n % 2][n // 2]
                first, second = (2 * q, 2 * q + 1) if d == 0 else (2 * q + 1, 2 * q)
                if n < 2:
                    todo = [(None, first, second), (second, second, first)]
                else:
                    todo = [(m, m, m + 1 if d == 0 else m - 1) for m in (first, second)
                            if 2 <= (m + 1 if d == 0 else m - 1) < NCHUNK]
                group = []
                for src, m, dst in todo:
                    group.append((d, src, m, dst, latest[d]))
                    count += 1
                    latest[d] = count
                updates.append(group)
            STEPS = count
            after = [sum(len(g) for g in updates[:n + 1]) for n in range(KVS)]
            block = s.enter_context(nc.Block())

            @block.sync
            def _(sp):
                def part(i, ahead, j):
                    return gla_dram[bass.ds(i * 6 + 6 * ahead + j, 2)].rearrange("m p t -> p m t")

                def load_qkv(i, ahead):
                    sp.dma_start(up[:], inp["w_up"][bass.ds(i + ahead, 1)].rearrange("o p n -> p (o n)")).then_inc(up_in, 16)
                    sp.dma_start(head[:, 0:2], part(i, ahead, 0)).then_inc(qk_in, 16)
                    sp.dma_start(head[:, 2:4], part(i, ahead, 2)).then_inc(v_in, 16)

                def load_states(i, ahead):
                    for d in range(2):
                        sp.dma_start(state[d][:, 2 if d == 0 else NCHUNK - 1],
                                     inp["state"][d, bass.ds(i + ahead, 1)].rearrange("o p n -> p (o n)")).then_inc(state_in, 16)

                def body(i, last=False):
                    if not last:
                        wait(sp, a_done, i, 6, 6)
                        load_qkv(i, 1)
                    wait(sp, stepped, i, STEPS, after[1])
                    for d in range(2):
                        sp.dma_start(out["new_state"][d, bass.ds(i, 1)].rearrange("o p n -> p (o n)"),
                                     state[d][:, d]).then_inc(states_out, 16)
                    wait(sp, finished, i, 2, 0)
                    sp.dma_start(head[:, 4:6], part(i, 0, 4)).then_inc(r_in, 16)
                    if not last:
                        wait(sp, o_done, i, OB, OB)
                        load_states(i, 1)
                sp.dma_start(scan_mask[:], inp["c_scan"]).then_inc(mask_in, 16)
                load_qkv(0, 0)
                load_states(0, 0)
                body(0)
                with sp.Fori(1, HEADS - 1) as i:
                    body(i)
                body(HEADS - 1, last=True)
                sp.wait_ge(states_out, 32 * HEADS)

            @block.scalar
            def _(act):
                def gates(i, ahead):
                    for d in range(2):
                        wait(act, z_done, i, 2, 2 * ahead + d + 1)
                        wait(act, gate_sum, i, 2, 2 * ahead + d)
                        if d == 0:
                            wait(act, inverted, i, 1, ahead - 1)
                        act.activation(tri(log_part[:]), ps[:, 0:NC, 0:CW], ACT.Abs,
                                       bias=bgate[:, d, bass.ds(i + ahead, 1)]).then_inc(gate_act, 1)
                        wait(act, gate_act, i, 6, 6 * ahead + 3 * d + 1)
                        act.activation(log_part[:], log_part[:], ACT.Exp, scale=-1.0).then_inc(gate_act, 1)
                        wait(act, gate_act, i, 6, 6 * ahead + 3 * d + 2)
                        act.activation(log_part[:], log_part[:], ACT.Ln, bias=ones[:, 0:1]).then_inc(gate_act, 1)
                        wait(act, scanned, i, 2, 2 * ahead + d + 1)
                        wait(act, a_done, i, 6, 6 * ahead + 3 * d - 3)
                        act.activation(k_t[d][:], decay_sum[d][:], ACT.Exp, scale=-1.0 / GATE_TEMP).then_inc(shrunk, 1)
                        wait(act, stepped, i, STEPS, STEPS * ahead)
                        act.activation(decay[:, d].unsqueeze(2), last_of(decay_sum[d][:], d), ACT.Exp,
                                       scale=1.0 / GATE_TEMP).then_inc(decayed, 1)
                        wait(act, to_go, i, 2, 2 * ahead + d + 1)
                        wait(act, k_end_turned, i, 6, 6 * ahead + 3 * d - 3)
                        act.activation(k_end[d][:], gate[d][:], ACT.Exp, scale=1.0 / GATE_TEMP).then_inc(ended, 1)

                def square(i, back):
                    wait(act, o_out, i, OB, OB * (1 - back))
                    act.activation(squares[:], o_all[:, bass.ds(i * 2 - 2 * back, 2)], ACT.Square).then_inc(squared, 1)

                def root(i, back):
                    wait(act, averaged, i, 1, 1 - back)
                    act.activation(tri(log_part[:]), ps[:, M_BANK0:M_BANK0 + NC, 0:CW], ACT.Ln, bias=eps[:],
                                   scale=1.0 / (2 * P)).then_inc(rooted, 1)
                    wait(act, rooted, i, 1, 1 - back)
                    act.activation(rstd[:], log_part[:], ACT.Exp, scale=-0.5).then_inc(inverted, 1)
                    wait(act, r_in, i, 16, 16 * (1 - back))
                    act.activation(head[:, 4:6], head[:, 4:6], ACT.Silu).then_inc(silu_r, 1)

                def body(i, first=False, last=False):
                    wait(act, o_done, i, OB, 0)
                    for d in range(2):
                        act.activation(q_t[d][:], decay_sum[d][:], ACT.Exp, scale=1.0 / GATE_TEMP).then_inc(grown, 1)
                    flat, t0 = v_tok[:].rearrange("p n m -> p (n m)"), 0
                    for r, n in enumerate(GROUP):
                        wait(act, v_turned, i, OB, r + 1)
                        act.activation(flat[:, t0 * P:(t0 + n) * P], ps[:, V_BANKS[r], 0:n * P], ACT.Copy).then_inc(v_out, 1)
                        t0 += n
                    for d in range(2):
                        for b in range(3):
                            wait(act, k_end_turned, i, 6, 3 * d + b + 1)
                            act.activation(k_end_tok[d][:, 3 * b:3 * b + 3].rearrange("p n m -> p (n m)"),
                                           ps[:, KE_BANKS[d][b], 0:3 * P], ACT.Copy).then_inc(k_end_out, 1)
                        if d == 0 and not first:
                            square(i, 1)
                    if not first:
                        root(i, 1)
                    if not last:
                        gates(i, 1)
                gates(0, 0)
                body(0, first=True)
                with act.Fori(1, HEADS - 1) as i:
                    body(i)
                body(HEADS - 1, last=True)
                square(HEADS - 1, 0)
                root(HEADS - 1, 0)

            @block.vector
            def _(dve):
                dve.wait_ge(mask_in, 16)

                def gates(i, ahead, d):
                    wait(dve, gate_act, i, 6, 6 * ahead + 3 * d + 1)
                    wait(dve, ended, i, 2, 2 * ahead + d - 1)
                    if d == 0:
                        wait(dve, averaged, i, 1, ahead - 1)
                    dve.tensor_scalar(tri(gate[d][:]), ps[:, 0:NC, 0:CW], bgate[:, d, bass.ds(i + ahead, 1)], 0.0,
                                      ALU.add, ALU.min).then_inc(gate_min, 1)
                    wait(dve, gate_act, i, 6, 6 * ahead + 3 * d + 3)
                    wait(dve, gate_min, i, 2, 2 * ahead + d + 1)
                    dve.tensor_tensor(gate[d][:], gate[d][:], log_part[:], ALU.subtract).then_inc(gate_sum, 1)
                    wait(dve, gate_sum, i, 2, 2 * ahead + d + 1)
                    wait(dve, grown, i, 2, 2 * ahead + d - 1)
                    if d == 0:
                        wait(dve, scaled, i, 1, ahead - 1)
                    src, dst = (gate[d][:], decay_sum[d][:]) if d == 0 else (gate[d][:, ::-1], decay_sum[d][:, ::-1])
                    dve.tensor_tensor_scan(dst, scan_mask[:], src, 0.0, ALU.mult, ALU.add).then_inc(scanned, 1)
                    wait(dve, scanned, i, 2, 2 * ahead + d + 1)
                    dve.tensor_tensor(chunk_of(gate[d][:]), last_of(decay_sum[d][:], d).broadcast_to([P, NCHUNK, GCH]),
                                      chunk_of(decay_sum[d][:]), ALU.subtract).then_inc(to_go, 1)

                def finish(i, back):
                    wait(dve, scaled, i, 1, 1 - back)
                    for j in range(2):
                        o_j = o_all[:, bass.ds(i * 2 - 2 * back + j, 1)].rearrange("p o t -> p (o t)")
                        dve.scalar_tensor_tensor(out=o_j, in0=o_j, scalar=vnorm[:, bass.ds(i * 2 - 2 * back + j, 1)],
                                                 in1=head[:, 4 + j], op0=ALU.mult, op1=ALU.mult).then_inc(finished, 1)

                def step(i, n):
                    wait(dve, kv_done, i, KVS, n + 1)
                    for e, (d, src, chunk, dst, before) in enumerate(updates[n]):
                        kv = ps[:, KV_BANKS[n % 4][chunk % 2], 0:2 * P]
                        if src is None:
                            if d == 0:
                                wait(dve, states_out, i, 32, 0)
                            dve.tensor_scalar(state[d][:, dst], kv, 1.0, None, ALU.mult).then_inc(stepped, 1)
                        else:
                            if before:
                                wait(dve, stepped, i, STEPS, before)
                            if n == 2 and e == 0:
                                wait(dve, state_in, i, 32, 32)
                            dve.scalar_tensor_tensor(out=state[d][:, dst], in0=state[d][:, src], scalar=decay[:, d, chunk:chunk + 1],
                                                     in1=kv, op0=ALU.mult, op1=ALU.add).then_inc(stepped, 1)

                def outputs(i, a, b):
                    for n in range(a, b):
                        w = GROUP[n] * P
                        wait(dve, o_done, i, OB, n + 1)
                        flat = o_all[:, bass.ds(i * 2, 2)].rearrange("p m t -> p (m t)")
                        dve.tensor_scalar(flat[:, 512 * n:512 * n + w], ps[:, O_BANK0 + n, 0:w], 1.0, None, ALU.mult).then_inc(o_out, 1)

                def body(i, first=False, last=False):
                    wait(dve, qk_in, i, 16, 16)
                    for d in range(2):
                        wait(dve, grown, i, 2, d + 1)
                        dve.scalar_tensor_tensor(out=q_t[d][:], in0=head[:, 0], scalar=DK_SCALE, in1=q_t[d][:],
                                                 op0=ALU.mult, op1=ALU.mult).then_inc(q_ready, 1)
                    for d in range(2):
                        for b in range(3):
                            wait(dve, a_done, i, 6, 3 * d + b + 1)
                            dve.tensor_tensor(a_t[d][:, 3 * b:3 * b + 3],
                                              ps[:, A_BANKS[d][b], 0:3 * P].rearrange("p (b n) -> p b n", b=3),
                                              mask_gla[:, d:d + 1].broadcast_to([P, 3, P]), ALU.mult).then_inc(a_out, 1)
                    wait(dve, decayed, i, 2, 2)
                    for n in range(KVS):
                        step(i, n)
                    if not first:
                        finish(i, 1)
                    if not last:
                        gates(i, 1, 0)
                    outputs(i, 0, 1)
                    if not last:
                        gates(i, 1, 1)
                    outputs(i, 1, OB)
                for d in range(2):
                    gates(0, 0, d)
                body(0, first=True)
                with dve.Fori(1, HEADS - 1) as i:
                    body(i)
                body(HEADS - 1, last=True)
                dve.wait_ge(silu_r, HEADS)
                dve.wait_ge(inverted, HEADS)
                dve.tensor_tensor(head[:, 4:6], head[:, 4:6], rstd[:].unsqueeze(1).broadcast_to([P, 2, T]),
                                  ALU.mult).then_inc(scaled, 1)
                finish(HEADS - 1, 0)

            @block.gpsimd
            def _(pool):
                def keys(i, ahead):
                    wait(pool, qk_in, i, 16, 16 * ahead + 16)
                    for d in range(2):
                        wait(pool, shrunk, i, 2, 2 * ahead + d + 1)
                        pool.tensor_tensor(k_t[d][:], head[:, 1], k_t[d][:], ALU.mult).then_inc(k_ready, 1)
                        wait(pool, ended, i, 2, 2 * ahead + d + 1)
                        pool.tensor_tensor(k_end[d][:], head[:, 1], k_end[d][:], ALU.mult).then_inc(k_end_ready, 1)

                def rescale(i, back):
                    wait(pool, silu_r, i, 1, 1 - back)
                    wait(pool, inverted, i, 1, 1 - back)
                    pool.tensor_tensor(head[:, 4:6], head[:, 4:6], rstd[:].unsqueeze(1).broadcast_to([P, 2, T]),
                                       ALU.mult).then_inc(scaled, 1)

                def body(i, first=False, last=False):
                    wait(pool, a_out, i, 6, 6)
                    pool.tensor_tensor(a_t[1][:], a_t[0][:], a_t[1][:], ALU.add).then_inc(a_joined, 1)
                    if not first:
                        rescale(i, 1)
                    if not last:
                        keys(i, 1)
                keys(0, 0)
                body(0, first=True)
                with pool.Fori(1, HEADS - 1) as i:
                    body(i)
                body(HEADS - 1, last=True)

            @block.tensor
            def _(pe):
                def gate_inputs(i, ahead, d):
                    rows = slice(32 * d, 32 * d + 16)
                    for c in range(NC):
                        mm = pe.matmul(ps[:, Z_BANKS[c], 0:CW], up[rows, :], gd[rows, cs[c]], start=True, stop=True)
                    mm.then_inc(z_done, 1)

                def scores(i, d):
                    wait(pe, q_ready, i, 2, d + 1)
                    wait(pe, k_ready, i, 2, d + 1)
                    for t in range(NT):
                        if t == 6 and d == 1:
                            wait(pe, a_out, i, 6, 1)
                        tok = slice(t * P, (t + 1) * P)
                        mm = pe.matmul(ps[:, A_BANKS[d][t // 3], (t % 3) * P:(t % 3 + 1) * P], k_t[d][:, tok], q_t[d][:, tok],
                                       start=True, stop=True)
                        if t % 3 == 2:
                            mm.then_inc(a_done, 1)

                def mean(i, back):
                    wait(pe, squared, i, 1, 1 - back)
                    for c in range(NC):
                        for j in range(2):
                            mm = pe.matmul(ps[:, M_BANK0 + c, 0:CW], ones[:], squares[:, j, cs[c]], start=(j == 0), stop=(j == 1))
                    mm.then_inc(averaged, 1)

                def outputs(i, a, b):
                    for n in range(a, b):
                        for m in range(GROUP[n]):
                            j, t = divmod(4 * n + m, NT)
                            dv, bank, c0 = slice(j * P, (j + 1) * P), O_BANK0 + n, m * P
                            pe.matmul(ps[:, bank, c0:c0 + P], v_tok[:, t, dv], a_t[1][:, t], start=True, stop=False,
                                      skip_group_check=True)
                            inter = [(d, c) for d in range(2) for c in (2 * t, 2 * t + 1) if (d, c) not in ((0, 0), (1, 1))]
                            for d, c in inter:
                                c1 = c0 + (c % 2) * GCH
                                mm = pe.matmul(ps[:, bank, c1:c1 + GCH], state[d][:, c, dv], q_t[d][:, c * GCH:(c + 1) * GCH],
                                               start=False, stop=(d, c) == inter[-1], skip_group_check=True)
                        mm.then_inc(o_done, 1)

                def body(i, first=False, last=False):
                    wait(pe, v_in, i, 16, 16)
                    wait(pe, gate_min, i, 2, 2)
                    n = 0
                    for r, tiles in enumerate(GROUP):
                        if r >= 3:
                            wait(pe, v_out, i, OB, r - 2)
                        for m in range(tiles):
                            t, j = divmod(n, 2)
                            n += 1
                            mm = pe.transpose(ps[:, V_BANKS[r], m * P:(m + 1) * P], head[:, 2 + j, t * P:(t + 1) * P], ident[:])
                        mm.then_inc(v_turned, 1)
                    for d in range(2):
                        wait(pe, k_end_ready, i, 2, d + 1)
                        if d == 0:
                            wait(pe, o_out, i, OB, 0)
                        for t in range(NT):
                            if d == 1 and t == 6:
                                wait(pe, v_out, i, OB, 3)
                            mm = pe.transpose(ps[:, KE_BANKS[d][t // 3], (t % 3) * P:(t % 3 + 1) * P],
                                              k_end[d][:, t * P:(t + 1) * P], ident[:])
                            if t % 3 == 2:
                                mm.then_inc(k_end_turned, 1)
                    wait(pe, v_out, i, OB, OB)
                    wait(pe, k_end_out, i, 6, 1)
                    scores(i, 0)
                    wait(pe, k_end_out, i, 6, 4)
                    if not first:
                        mean(i, 1)
                    wait(pe, k_end_out, i, 6, 6)
                    scores(i, 1)
                    for n in range(KVS):
                        if n == 0:
                            wait(pe, rooted, i, 1, 0)
                        elif n < 4:
                            wait(pe, a_out, i, 6, (0, 3, 4, 6)[n])
                        else:
                            wait(pe, stepped, i, STEPS, after[n - 4])
                        d, q = n % 2, pair_order[n % 2][n // 2]
                        for e in range(2):
                            rows = slice(e * GCH, (e + 1) * GCH)
                            mm = pe.matmul(ps[:, KV_BANKS[n % 4][e], 0:2 * P], k_end_tok[d][rows, q, :], v_tok[rows, q, :],
                                           start=True, stop=True)
                        mm.then_inc(kv_done, 1)
                    if not last:
                        wait(pe, up_in, i, 16, 32)
                        wait(pe, stepped, i, STEPS, after[KVS - 3])
                        gate_inputs(i, 1, 0)
                    wait(pe, stepped, i, STEPS, STEPS)
                    wait(pe, a_joined, i, 1, 1)
                    outputs(i, 0, 1)
                    if not last:
                        wait(pe, gate_min, i, 2, 3)
                        gate_inputs(i, 1, 1)
                    outputs(i, 1, OB)
                pe.wait_ge(up_in, 16)
                gate_inputs(0, 0, 0)
                pe.wait_ge(gate_min, 1)
                gate_inputs(0, 0, 1)
                body(0, first=True)
                with pe.Fori(1, HEADS - 1) as i:
                    body(i)
                body(HEADS - 1, last=True)
                mean(HEADS - 1, 0)


    QK0 = X0
    WQ = X0 + 4 * EVEN_TILES * T
    qkvu = at("qkvu", [P, EVEN_TILES, T], F32, QK0)

    o_all = at("o_all", [P, KT, T], F32, X0)
    gd = at("gd", [DH, T], F32, GD0)

    modulation()
    projection(inp["w_in_even"], EVEN_TILES, WQ, result=qkvu, pooling=True,
               prepare=partial(Norm, n=0, layer=0, shift=SHIFT1), mods=(2 * KT, 4, (1,)))
    attention(qkvu, WQ)
    projection(inp["w_out_even"], KT, W0, residual=(inp["x"], 0, GATE1),
               prepare=partial(EvenOutput), mods=(6 * KT, 4, (2,)))
    ffn(0, norm=dict(n=1, layer=0, shift=SHIFT2))
    recycle()
    projection(inp["w_in_odd"], ODD_TILES, W0, spill=gla_dram, extra=(inp["w_gd"], DH, gd),
               prepare=partial(Norm, n=2, layer=1, shift=SHIFT1, spill=True), mods=(8 * KT, 2, (3,)))
    gla(gd, o_all)
    projection(inp["w_out_odd"], KT, W0, residual=(xs_dram, 1, GATE1),
               prepare=partial(Split), mods=(11 * KT, 2))
    ffn(1, norm=dict(n=3, layer=1, shift=SHIFT2))
    final_norm(4, out["y"])

    ctx.close()


def layout(a):
    import numpy as np

    def cols(v):
        v = np.asarray(v)
        return np.moveaxis(v.reshape(*v.shape[:-1], v.shape[-1] // P, P), -1, 0)

    def tiles(w):
        kk, n = w.shape
        return w.reshape(kk // P, P, n // P, P).transpose(2, 1, 0, 3).reshape(n // P, P, kk)

    f = lambda v: np.ascontiguousarray(v, dtype=np.float32)
    x_t = np.concatenate([a["x_prompt"][0], a["x_sample"][0]], axis=0)
    r = {"x": x_t.T.reshape(KT, P, T).transpose(1, 0, 2)}
    r["cond"] = np.moveaxis(cols(np.stack([a["c_ctx"], a["c"][0]])), 1, 2)
    r["w_mod"] = tiles(a["w_mod"][0])[:MOD_FIRST]
    r["w_mod_t"] = np.concatenate([a["w_mod"][l].T.reshape(6 * KT, P, D) for l in range(2)])
    r["cond_row"] = np.broadcast_to(np.stack([a["c_ctx"], a["c"][0]]), (P, 2, D))
    r["b_mod"] = cols(a["b_mod"])
    r["gnorm"] = cols(np.stack([a["norm1_g"][0], a["norm2_g"][0], a["norm1_g"][1], a["norm2_g"][1], a["final_g"]]))
    r["lam"] = np.broadcast_to(a["lam_params"], (P, 4, DH))
    r["subln"] = cols(a["subln_g"][0])
    r["pscale"] = cols(a["pool_scale"][0])
    r["bgate"] = cols(a["b_gate"][0])
    r["gla_norm"] = cols(a["gla_norm_g"][0])
    r["w_in_even"] = np.roll(tiles(a["w_in_even"][0]), HEADS, axis=0)
    r["w_out_even"] = tiles(a["w_out_even"][0])
    w = a["w_in_odd"][0]
    order = []
    for h in range(HEADS):
        order += [h, 4 + h, 8 + 2 * h, 9 + 2 * h, 16 + 2 * h, 17 + 2 * h]
    r["w_in_odd"] = tiles(w[:, :ODD_TILES * P])[order]
    gd = np.zeros((D, DH), np.float32)
    gd[:, 0:16], gd[:, 32:48] = w[:, ODD_TILES * P:ODD_TILES * P + 16], w[:, ODD_TILES * P + 16:]
    r["w_gd"] = gd.reshape(KT, P, DH).transpose(1, 0, 2).reshape(P, KT * DH)
    up = np.zeros((HEADS, 48, P), np.float32)
    for d in range(2):
        up[:, 32 * d:32 * d + 16] = a["w_gate_up"][0, d].reshape(16, HEADS, P).transpose(1, 0, 2)
    r["w_up"] = up
    r["w_out_odd"] = tiles(a["w_out_odd"][0])
    r["w_pool"] = a["w_pool"][0].transpose(1, 0, 2)
    fin, fout = [], []
    for l in range(2):
        t = tiles(a["w_ffn_in"][l])
        n = HIDDEN // P
        fin.append(np.stack([t[:n], t[n:]], axis=2).reshape(n, P, 2 * D))
        fout.append(a["w_ffn_out"][l].reshape(FFN_PAIRS, 2, P, D).transpose(0, 2, 1, 3).reshape(FFN_PAIRS, P, 2 * D))
    r["w_ffn_in"], r["w_ffn_out"] = np.stack(fin), np.stack(fout)
    r["cache_k"] = a["cache_attn_k"][0, 0].reshape(CTX, HEADS, P).transpose(2, 1, 0)
    r["cache_v"] = a["cache_attn_v"][0, 0]
    r["state"] = a["state_gla"][0, 0]

    r["c_ident"] = np.eye(P)
    q = np.arange(P)
    rot = np.zeros((P, P))
    lower = q % 32 < 16
    rot[q[lower], q[lower] + 16] = -1.0
    rot[q[~lower], q[~lower] - 16] = 1.0
    r["c_rot"] = rot.T
    j, i = np.meshgrid(q, q, indexing="ij")
    same = j // GCH == i // GCH
    r["c_mask"] = np.stack([same & (j <= i), same & (j >= i)], axis=1)
    inv = (1.0 / (10000.0 ** (np.arange(0, 32, 2, dtype=np.float32) / np.float32(32)))).astype(np.float32)
    t = np.arange(LAT)
    place = np.where((q[:, None] // 32) % 2 == 0, t // 64, t % 64).astype(np.float32)
    ang = place * inv[q % 16][:, None]
    r["c_cos"], r["c_sin"] = np.cos(ang), np.sin(ang)
    e = np.ones((P, len(WINDOWS), 2, PAD), np.float32)
    for n, w in enumerate(WINDOWS):
        k = np.arange(PAD)
        e[:, n, 0] = w / np.minimum(w, k + w // 2)
        e[:, n, 1] = w / np.minimum(w, PAD - k + w // 2)
    r["c_edge"] = e
    scan = np.ones((P, T), np.float32)
    scan[:, ::GCH] = 0.0
    r["c_scan"] = scan
    return {n: f(v) for n, v in r.items()}


_OUTS = {"y": (P, KT, T), "new_k": (HEADS, P, CTX), "new_v": (HEADS, P, CTX), "new_state": (2, HEADS, P, 2 * P)}


def kernel(**inputs):
    import concourse.bacc as _bacc
    import numpy as _np
    from concourse.bass_utils import run_bass_kernel_spmd as _run

    nc = _bacc.Bacc("TRN2", target_bir_lowering=False, num_devices=1)
    arrays, inp, out = {}, {}, {}
    for name, v in layout({n: _np.asarray(v) for n, v in inputs.items()}).items():
        arrays[f"in_{name}_dram"] = v
        inp[name] = nc.dram_tensor(f"in_{name}_dram", v.shape, F32, kind="ExternalInput").ap()
    for name, shape in _OUTS.items():
        out[name] = nc.dram_tensor(f"out_{name}_dram", shape, F32, kind="ExternalOutput").ap()
    build(nc, inp, out)
    got = _run(nc, [arrays], core_ids=[0]).results[0]
    y = got["out_y_dram"].transpose(2, 1, 0).reshape(T, D)
    new_k = got["out_new_k_dram"].transpose(2, 0, 1).reshape(1, 1, CTX, HEADS, 2, DH)
    new_v = got["out_new_v_dram"].transpose(2, 0, 1).reshape(1, 1, CTX, HEADS, P)
    state = got["out_new_state_dram"].reshape(1, 1, 2, HEADS, P, 2 * P)
    return (y[None, :CTX], y[None, CTX:], new_k, new_v, state)
```
